# Optimizing a Trainium2 kernel written in Bass

```python
import jax, jax.numpy as jnp
from jax import lax
import numpy as np

D_MODEL = 1024
BATCH = 1
SEQ = 1024
DEPTH = 1
DEC_BATCH = 8
DEC_SEQ = 4
PAST_LEN = 1024
PAGE_SIZE = 128

N_HEADS = 16
HEAD_DIM = D_MODEL // N_HEADS
ATT_WIDTH = N_HEADS * HEAD_DIM
CONV_CH = D_MODEL
CONV_W = 31
D_FF = ((8 * D_MODEL // 3 + 127) // 128) * 128
Q_BLOCK = 128
LN_EPS = 1e-5
ALPHA = (2.0 * DEPTH) ** 0.25
BETA_INIT = (8.0 * DEPTH) ** -0.25
SB_BIAS_INIT = -8.0
IN_COLS = 3 * ATT_WIDTH + 2 * CONV_CH + 2 * D_MODEL
SPLIT_POINTS = (ATT_WIDTH, 2 * ATT_WIDTH, 3 * ATT_WIDTH, 3 * ATT_WIDTH + 2 * CONV_CH)

kernel_name = 'stickbreak_conformer_conv_macaron_deepnorm_step'

def layer_norm(x, g, b):
    xf = x.astype(jnp.float32)
    mu = jnp.mean(xf, axis=-1, keepdims=True)
    var = jnp.mean(jnp.square(xf - mu), axis=-1, keepdims=True)
    y = (xf - mu) * lax.rsqrt(var + LN_EPS) * g.astype(jnp.float32) + b.astype(jnp.float32)
    return y.astype(x.dtype)

def swiglu_half(x, w_up, w_down):
    gate, up = jnp.split(jnp.einsum('btd,df->btf', x, w_up), 2, axis=-1)
    return jnp.einsum('btf,fd->btd', jax.nn.silu(gate) * up, w_down)

def stick_breaking_block(q, k, v, q_pos, k_pos, b_sb):
    z = jnp.einsum('bqhd,bkhd->bhqk', q, k).astype(jnp.float32) * (HEAD_DIM ** -0.5)
    z = z + b_sb.astype(jnp.float32)[None, :, None, None]
    causal = k_pos[None, :] < q_pos[:, None]
    log_keep = jnp.where(causal, jax.nn.log_sigmoid(-z), 0.0)
    after = lax.cumsum(log_keep, axis=3, reverse=True) - log_keep
    a = jnp.where(causal, jnp.exp(jax.nn.log_sigmoid(z) + after), 0.0)
    return jnp.einsum('bhqk,bkhd->bqhd', a.astype(v.dtype), v)

def stick_breaking(q, k, v, q_pos, k_pos, b_sb):
    B, T, H, Dh = q.shape
    bq = Q_BLOCK if T % Q_BLOCK == 0 else T
    nb = T // bq
    qb = q.reshape(B, nb, bq, H, Dh).transpose(1, 0, 2, 3, 4)
    pb = q_pos.reshape(nb, bq)
    ob = lax.map(lambda qp: stick_breaking_block(qp[0], k, v, qp[1], k_pos, b_sb), (qb, pb))
    return ob.transpose(1, 0, 2, 3, 4).reshape(B, T, H, Dh)

def conv_module(conv_in, buf, w_dw, b_dw, ln_g, ln_b, w_proj_b):
    a, g = jnp.split(conv_in, 2, axis=-1)
    glu = a * jax.nn.sigmoid(g)
    ext = jnp.concatenate([buf.astype(glu.dtype), glu], axis=1)
    y = lax.conv_general_dilated(ext, w_dw[:, None, :].astype(ext.dtype), window_strides=(1,),
                                 padding='VALID', dimension_numbers=('NWC', 'WIO', 'NWC'),
                                 feature_group_count=CONV_CH) + b_dw
    y = jax.nn.silu(layer_norm(y, ln_g, ln_b))
    return jnp.einsum('btc,cd->btd', y, w_proj_b), ext[:, ext.shape[1] - (CONV_W - 1):]

def decoder_layer(x, k_past, v_past, conv_buf, p):
    B, T, _ = x.shape
    past = k_past.shape[1]
    x = layer_norm(ALPHA * x + 0.5 * swiglu_half(x, p['w_ff1_up'], p['w_ff1_down']), p['ln1_g'], p['ln1_b'])
    h = jnp.einsum('btd,de->bte', x, p['w_in'])
    q, k, v, conv_in, gates = jnp.split(h, SPLIT_POINTS, axis=-1)
    q = q.reshape(B, T, N_HEADS, HEAD_DIM)
    k = k.reshape(B, T, N_HEADS, HEAD_DIM)
    v = v.reshape(B, T, N_HEADS, HEAD_DIM)
    k_all = jnp.concatenate([k_past.astype(k.dtype), k], axis=1)
    v_all = jnp.concatenate([v_past.astype(v.dtype), v], axis=1)
    k_pos = jnp.arange(past + T, dtype=jnp.int32)
    q_pos = past + jnp.arange(T, dtype=jnp.int32)
    o_a = stick_breaking(q, k_all, v_all, q_pos, k_pos, p['b_sb']).reshape(B, T, ATT_WIDTH)
    y_a = jnp.einsum('bte,ed->btd', o_a, p['w_proj_a'])
    y_b, new_buf = conv_module(conv_in, conv_buf, p['w_dw'], p['b_dw'], p['ln_conv_g'], p['ln_conv_b'], p['w_proj_b'])
    g_a, g_b = jnp.split(jax.nn.sigmoid(gates + p['b_gate']), 2, axis=-1)
    mix = jnp.einsum('btd,de->bte', g_a * y_a + g_b * y_b, p['w_out'])
    x = layer_norm(ALPHA * x + mix, p['ln2_g'], p['ln2_b'])
    x = layer_norm(ALPHA * x + 0.5 * swiglu_half(x, p['w_ff2_up'], p['w_ff2_down']), p['ln3_g'], p['ln3_b'])
    return x, k, v, new_buf

def setup_inputs(seed: int = 0) -> dict:
    key = jax.random.key(seed)
    ks = jax.random.split(key, 32)
    n_pages = PAST_LEN // PAGE_SIZE
    n_used = DEC_BATCH * n_pages
    n_pool = (n_used * 5) // 4

    def nrm(k, shape, scale):
        return jax.random.normal(k, shape, jnp.float32) * scale

    w_in = nrm(ks[6], (DEPTH, D_MODEL, IN_COLS), D_MODEL ** -0.5)
    w_in = w_in.at[:, :, 2 * ATT_WIDTH:3 * ATT_WIDTH].multiply(BETA_INIT)
    page_table = jax.random.permutation(ks[5], n_pool)[:n_used].reshape(DEC_BATCH, n_pages).astype(jnp.int32)
    return {
        'x_prompt': nrm(ks[0], (BATCH, SEQ, D_MODEL), 1.0),
        'x_sample': nrm(ks[1], (DEC_BATCH, DEC_SEQ, D_MODEL), 1.0),
        'cache_k': nrm(ks[2], (DEPTH, n_pool, PAGE_SIZE, N_HEADS, HEAD_DIM), 1.0),
        'cache_v': nrm(ks[3], (DEPTH, n_pool, PAGE_SIZE, N_HEADS, HEAD_DIM), 1.0),
        'state_conv': nrm(ks[4], (DEPTH, DEC_BATCH, CONV_W - 1, CONV_CH), 0.5),
        'page_table': page_table,
        'w_ff1_up': nrm(ks[7], (DEPTH, D_MODEL, 2 * D_FF), D_MODEL ** -0.5),
        'w_ff1_down': nrm(ks[8], (DEPTH, D_FF, D_MODEL), BETA_INIT * D_FF ** -0.5),
        'ln1_g': 1.0 + nrm(ks[9], (DEPTH, D_MODEL), 0.05),
        'ln1_b': nrm(ks[10], (DEPTH, D_MODEL), 0.02),
        'w_in': w_in,
        'b_sb': SB_BIAS_INIT + nrm(ks[25], (DEPTH, N_HEADS), 0.5),
        'b_gate': nrm(ks[11], (DEPTH, 2 * D_MODEL), 0.1),
        'w_dw': nrm(ks[12], (DEPTH, CONV_W, CONV_CH), CONV_W ** -0.5),
        'b_dw': nrm(ks[13], (DEPTH, CONV_CH), 0.02),
        'ln_conv_g': 1.0 + nrm(ks[14], (DEPTH, CONV_CH), 0.05),
        'ln_conv_b': nrm(ks[15], (DEPTH, CONV_CH), 0.02),
        'w_proj_a': nrm(ks[16], (DEPTH, ATT_WIDTH, D_MODEL), BETA_INIT * ATT_WIDTH ** -0.5),
        'w_proj_b': nrm(ks[17], (DEPTH, CONV_CH, D_MODEL), BETA_INIT * CONV_CH ** -0.5),
        'w_out': nrm(ks[18], (DEPTH, D_MODEL, D_MODEL), BETA_INIT * D_MODEL ** -0.5),
        'ln2_g': 1.0 + nrm(ks[19], (DEPTH, D_MODEL), 0.05),
        'ln2_b': nrm(ks[20], (DEPTH, D_MODEL), 0.02),
        'w_ff2_up': nrm(ks[21], (DEPTH, D_MODEL, 2 * D_FF), D_MODEL ** -0.5),
        'w_ff2_down': nrm(ks[22], (DEPTH, D_FF, D_MODEL), BETA_INIT * D_FF ** -0.5),
        'ln3_g': 1.0 + nrm(ks[23], (DEPTH, D_MODEL), 0.05),
        'ln3_b': nrm(ks[24], (DEPTH, D_MODEL), 0.02),
    }

def reference(x_prompt, x_sample, cache_k, cache_v, state_conv, page_table,
              w_ff1_up, w_ff1_down, ln1_g, ln1_b, w_in, b_sb, b_gate, w_dw, b_dw,
              ln_conv_g, ln_conv_b, w_proj_a, w_proj_b, w_out, ln2_g, ln2_b,
              w_ff2_up, w_ff2_down, ln3_g, ln3_b):
    dec_b, n_pages = page_table.shape
    xp, xs = x_prompt, x_sample
    kp_l, vp_l, cp_l, ks_l, vs_l, cs_l = [], [], [], [], [], []
    for l in range(DEPTH):
        p = dict(w_ff1_up=w_ff1_up[l], w_ff1_down=w_ff1_down[l], ln1_g=ln1_g[l], ln1_b=ln1_b[l],
                 w_in=w_in[l], b_sb=b_sb[l], b_gate=b_gate[l], w_dw=w_dw[l], b_dw=b_dw[l],
                 ln_conv_g=ln_conv_g[l], ln_conv_b=ln_conv_b[l], w_proj_a=w_proj_a[l],
                 w_proj_b=w_proj_b[l], w_out=w_out[l], ln2_g=ln2_g[l], ln2_b=ln2_b[l],
                 w_ff2_up=w_ff2_up[l], w_ff2_down=w_ff2_down[l], ln3_g=ln3_g[l], ln3_b=ln3_b[l])
        b = xp.shape[0]
        empty = jnp.zeros((b, 0, N_HEADS, HEAD_DIM), xp.dtype)
        zero_buf = jnp.zeros((b, CONV_W - 1, CONV_CH), xp.dtype)
        xp, kp, vp, cp = decoder_layer(xp, empty, empty, zero_buf, p)
        k_past = cache_k[l][page_table].reshape(dec_b, n_pages * PAGE_SIZE, N_HEADS, HEAD_DIM)
        v_past = cache_v[l][page_table].reshape(dec_b, n_pages * PAGE_SIZE, N_HEADS, HEAD_DIM)
        xs, kn, vn, cn = decoder_layer(xs, k_past, v_past, state_conv[l], p)
        kp_l.append(kp); vp_l.append(vp); cp_l.append(cp)
        ks_l.append(kn); vs_l.append(vn); cs_l.append(cn)
    return (xp, xs, jnp.stack(kp_l), jnp.stack(vp_l), jnp.stack(cp_l),
            jnp.stack(ks_l), jnp.stack(vs_l), jnp.stack(cs_l))


_drawn_inputs = setup_inputs


def setup_inputs(seed=0):
    import zlib

    import numpy as np

    out = dict(_drawn_inputs(seed))
    spreads = {}
    factors = {'cache_k': 64.0,
     'cache_v': 64.0,
     'b_sb': 64.0,
     'b_gate': 8.0,
     'b_dw': 8.0,
     'ln_conv_g': 8.0,
     'ln_conv_b': 33.64,
     'w_proj_a': 64.0,
     'ln2_b': 2.922,
     'ln3_b': 2.85}
    for name, (base, spread) in spreads.items():
        noise = np.random.default_rng([zlib.crc32(name.encode()), seed]).standard_normal(out[name].shape)
        drawn = base * np.exp(spread * noise) if base else spread * noise
        out[name] = __import__('jax').numpy.asarray(drawn.astype(out[name].dtype))
    for name, factor in factors.items():
        out[name] = (out[name] * factor).astype(out[name].dtype)
    return out
```

```python
from contextlib import ExitStack

import numpy as np

import concourse.bass as bass
import concourse.mybir as mybir
from concourse.alu_op_type import AluOpType as ALU

ACT = mybir.ActivationFunctionType
F32 = mybir.dt.float32
F32R = mybir.dt.float32r
BF16 = mybir.dt.bfloat16
I32 = mybir.dt.int32

P = 128
D = 1024
KB = D // P
SEQ = 1024
DB, DQ = 8, 4
NS = DB * DQ
T = SEQ + NS
CH = T // 3
H, HD = 16, 64
F = 2816
FT = F // P
FG = FT // 2
CW = 31
HIST = CW - 1
PAGES = 8
POOL = 80
PAST = PAGES * P
ALPHA = 2.0 ** 0.25
SCALE = HD ** -0.5
EPS = 1e-5
ZCAP = 30.0
KEYS = PAST + NS
NSTEP = 24

W_FF1, W_CONV, W_ATT, W_OUT, W_FF2 = 0, 66, 98, 122, 146
W_END = 212

STEPS = [(c, kb, h) for c in range(2) for kb in range(4 * c + 3, -1, -1) for h in range(2)]


LAG_SUM, LAG_OUT = 3, 5

SEMS = [
    "a_done", "a_hi", "a_lo", "acc_done", "acc_init", "aux_in0", "aux_in1", "bias_set",
    "const_in", "conv_in0", "conv_in1", "conv_saved", "csig_done", "down_out", "e_done",
    "eps_set", "glu_done", "hist_in", "hist_kept", "hist_turned", "k_hi", "k_lo", "k_nat",
    "k_raw", "k_saved", "k_turned", "l_done", "ln_aff", "ln_cent", "ln_log", "ln_mean",
    "ln_rstd", "ln_scaled", "ln_sq", "ln_sqread", "mask_set", "mix_out", "mix_tmp", "new_hi",
    "new_lo", "o_kept", "one_set", "op_hi", "op_lo", "pad_set", "page_in0", "page_in1",
    "page_in2", "page_in3", "page_in4", "page_in5", "page_in6", "page_in7", "pk_hi", "pk_lo",
    "pk_turned", "prod_done", "prod_hi", "prod_lo", "pv_hi", "pv_lo", "pv_used", "q_hi", "q_lo",
    "qb_hi", "qb_lo", "run_done", "s_a", "s_capped", "s_chain", "s_exp", "s_ln", "s_log",
    "s_ready", "s_row", "s_zero", "sa_hi", "sa_lo", "sa_turned", "sconst_in", "side_prod",
    "side_sum", "siga_done", "siga_saved", "sigb_done", "sigb_saved", "silu_done", "so_kept",
    "so_mask", "so_out", "so_turned", "sp_ready", "state_saved", "sz_kept", "sz_out",
    "tail_kept", "tail_saved", "tail_turned", "tap_done", "tok_in0", "tok_in1", "tok_turned",
    "v_hi", "v_lo", "v_nat", "v_raw", "v_saved", "v_turned", "v_used", "w_high", "w_landed0",
    "w_landed1", "w_split", "w_used", "x1_saved", "y_kept", "y_saved0", "y_saved1", "y_turned",
    "z_capped", "z_ready",
]


def tri(ap):
    return ap.rearrange("p (c n) -> p c n", c=3)


def chain(step):
    c, kb, _ = step
    off = P * max(kb - 4 * c, 0)
    return off, (None if kb == 4 * c + 3 else P * max(kb + 1 - 4 * c, 0))


def run_ops(step):
    off, before = chain(step)
    if step[1] == 0:
        return []
    if before is None:
        return [(off, 512, False)]
    return ([(off, before, False)] if before > off else []) + [(before, 512, True)]


RUN_OPS = [len(run_ops(s)) for s in STEPS]
RUN_TOTAL = sum(RUN_OPS)
SIDE = 6
MAIN = CW - SIDE
TAPS = 4 + 3 * MAIN + SIDE + 1
OP_FF1, OP_CONV, OP_A, OP_B, OP_OUT, OP_FF2 = 9, 17, 25, 33, 41, 49


def build(nc, A, O):
    with ExitStack() as top:
        def sb(name, shape, dt=F32, ctx=top):
            return ctx.enter_context(nc.sbuf_tensor(name, shape, dt))

        def dram(name, shape):
            return nc.dram_tensor(name, shape, F32, kind="Internal").ap()

        sig_a_d = dram("sig_a_scratch", [KB, P, T])
        sig_b_d = dram("sig_b_scratch", [KB, P, T])
        x1_d = dram("x1_scratch", [KB, P, T])
        conv_d = dram("conv_scratch", [KB, P, T])

        ps = top.enter_context(nc.psum_tensor("ps", [P, 8, 512], F32))

        def pset(s):
            return ps[:, 3 * s:3 * s + 3, 0:CH]

        xh = sb("xh", [P, KB, T], F32R)
        xl = sb("xl", [P, KB, T], F32R)
        acc = sb("acc", [P, KB, T])
        wraw = sb("wraw", [P, 2, D])
        tmp = sb("tmp", [P, 4, T])
        ident = sb("ident", [P, P])
        identb = sb("identb", [P, P], BF16)
        negtri = sb("negtri", [P, P])
        negones = sb("negones", [P, P])
        avg = sb("avg", [P, P])
        dmask = sb("dmask", [P, P], BF16)
        lnp = sb("lnp", [P, 8, KB])
        bgate = sb("bgate", [P, 2 * KB])
        bdw = sb("bdw", [P, KB])
        wdw = sb("wdw", [P, KB, CW])
        bias_p = sb("bias_p", [P, H])
        bias_s = sb("bias_s", [P, 1])
        epsc = sb("epsc", [P, 1])
        one = sb("one", [P, 1])
        pt_sb = sb("pt_sb", [1, DB * PAGES], I32)

        with ExitStack() as ff1:
            wh1, wl1 = (sb(f"{n}1", [P, 4, D], F32R, ff1) for n in ("wh", "wl"))
            gh1, gl1 = (sb(f"{n}1", [P, 4, T], F32R, ff1) for n in ("gh", "gl"))
        with ExitStack() as start:
            sb("hole_w1", [P, 8 * D], F32, start)
            tok = sb("tok", [P, 2, D], F32, start)
        with ExitStack() as cv:
            whc, wlc = (sb(f"{n}c", [P, 4, D], F32R, cv) for n in ("wh", "wl"))
            glu = sb("glu", [P, SEQ + P], F32, cv)
            ext = sb("ext", [P, DB, HIST + DQ], F32, cv)
            cbuf = sb("cbuf", [P, T], F32, cv)
            side = sb("side", [P, SEQ], F32, cv)
            prod1 = sb("prod1", [P, SEQ], F32, cv)
            wm = sb("wm", [P, CW + 1], F32, cv)
            hist = sb("hist", [P, KB, DB * HIST], F32, cv)
            hist_raw = sb("hist_raw", [DB * HIST // 2, 2, D], F32, cv)
            tail = sb("tail", [HIST + NS, D], F32, cv)
        with ExitStack() as at:
            wha, wla = (sb(f"{n}a", [P, 3, D], F32R, at) for n in ("wh", "wl"))
            qs = sb("qs", [P, KB, NS], F32, at)
            ks = sb("ks", [P, KB, NS], F32, at)
            qh, ql, kh, kl = (sb(n, [P, T], F32R, at) for n in ("qh", "ql", "kh", "kl"))
            nat = sb("nat", [P, 2, KB, P], F32, at)
            nat_s = sb("nat_s", [NS, 2, P], F32, at)
            vh, vl = (sb(n, [P, KB, P], F32R, at) for n in ("vh", "vl"))
            ah, al = (sb(n, [P, 3, 512], F32R, at) for n in ("ah", "al"))
            run = sb("run", [P, 2, 512], F32, at)
            bias_m = sb("bias_m", [P, 2], F32, at)
        with ExitStack() as sa:
            pages = sb("pages", [P, 6, D], F32, sa)
            sb("hole_qs", [P, KB, NS], F32, sa)
            sb("hole_ks", [P, KB, NS], F32, sa)
            qbh, qbl = (sb(n, [P, KB, P], F32R, sa) for n in ("qbh", "qbl"))
            ksh, ksl = (sb(n, [P, KB, NS], F32R, sa) for n in ("ksh", "ksl"))
            ath, atl = (sb(n, [P, KB + 1, P], F32R, sa) for n in ("ath", "atl"))
            vnh, vnl = (sb(n, [NS, D], F32R, sa) for n in ("vnh", "vnl"))
            vn_raw = sb("vn_raw", [NS, D], F32, sa)
            om = sb("om", [P, D], F32, sa)
            mbd = sb("mbd", [P, D], F32, sa)
            sel = sb("sel", [P, 2 * DQ], F32, sa)
            smask = sb("smask", [P, DB // 2, NS], F32, sa)
        with ExitStack() as ou:
            who, wlo = (sb(f"{n}o", [P, 4, D], F32R, ou) for n in ("wh", "wl"))
            gh2, gl2 = (sb(f"{n}2", [P, 4, T], F32R, ou) for n in ("gh", "gl"))
        WH = {W_FF1: (wh1, wl1), W_CONV: (whc, wlc), W_ATT: (wha, wla), W_OUT: (who, wlo), W_FF2: (who, wlo)}
        GH = ((gh1, gl1), (gh2, gl2))

        up_w = [A[f"w_ff{f}_up"].rearrange("a (kb p) c -> p (a kb) c", p=P) for f in (1, 2)]
        down_w = [A[f"w_ff{f}_down"].rearrange("a f c -> (a f) c") for f in (1, 2)]
        in_w = A["w_in"].rearrange("a (kb p) c -> p (a kb) c", p=P)
        out_w = [A[n].rearrange("a (kb p) c -> p (a kb) c", p=P) for n in ("w_proj_a", "w_proj_b", "w_out")]
        page_rows = [A[n].rearrange("a n p h d -> (a n) p (h d)") for n in ("cache_k", "cache_v")]
        new_p = [O[n].rearrange("a b (kb p) h d -> p (a b kb) (h d)", p=P) for n in ("new_k_p", "new_v_p")]
        new_s = [O[n].rearrange("a b q h d -> (a b q) (h d)") for n in ("new_k_s", "new_v_s")]
        state_rows = A["state_conv"].rearrange("a b i c -> (a b i) c")

        CONSTS = [(ident[:, :], "c_ident"), (negtri[:, :], "c_negtri"),
                  (negones[:, :], "c_negones"), (avg[:, :], "c_avg"), (tmp[:, 0, 0:P], "c_dmask"),
                  (lnp[:, :, :], "norms"), (bgate[:, :], "gate_bias"), (bdw[:, :], "conv_bias"),
                  (wdw[:, :, :], "taps"), (bias_p[:, :], "b_heads"), (bias_s[:, :], "b_rows"),
                  (pt_sb[:, :], "page_table")]

        S = {n: top.enter_context(nc.semaphore(n)) for n in SEMS}

        def load_tile(sp, i, n, src):
            if n >= 2:
                sp.wait_ge(S["w_split"], i + (n - 1))
            dst = wraw[:, n % 2, :]
            if len(src.shape) == 3:
                dst = dst.rearrange("p (kb c) -> p kb c", kb=KB)
            sp.dma_start(dst, src).then_inc(S[f"w_landed{n % 2}"], 16)

        def split_tile(pool, wh, wl, i, n, pos, used):
            pool.wait_ge(S[f"w_landed{n % 2}"], i * 8 + (n // 2 + 1) * 16)
            if used is not None:
                pool.wait_ge(S["w_used"], used)
            raw = wraw[:, n % 2, :]
            pool.tensor_tensor(wh[:, pos, :], raw, one[:, 0:1].to_broadcast([P, D]), ALU.mult).then_inc(S["w_high"], 1)
            pool.wait_ge(S["w_high"], i + (n + 1))
            pool.tensor_tensor(wl[:, pos, :], raw, wh[:, pos, :].bitcast(F32),
                               ALU.subtract).then_inc(S["w_split"], 1)

        def split_phase(pool, base, count, ring, norm_ops=None):
            wh, wl = WH[base]
            body = ring if ring % 2 == 0 else 2 * ring
            if base:
                pool.wait_ge(S["w_used"], base)
            for k in range(body):
                split_tile(pool, wh, wl, 0, base + k, k % ring, base + k - ring + 1 if k >= ring else None)
            if norm_ops is not None:
                split_lo(pool, norm_ops, range(1, KB, 2))
            whole = (count - body) // body * body
            with pool.Fori(0, whole - body + 1, body) as i:
                for k in range(body):
                    split_tile(pool, wh, wl, i, base + body + k, k % ring, i + (base + body + k - ring + 1))
            for k in range(body + whole, count):
                split_tile(pool, wh, wl, 0, base + k, k % ring, base + k - ring + 1)

        def linear(pe, base, pos, s, sem, value=1):
            wh, wl = WH[base]
            for c in range(3):
                for kb in range(KB):
                    for n, (w, x) in enumerate(((wh, xh), (wh, xl), (wl, xh))):
                        mm = pe.matmul(ps[:, 3 * s + c, 0:CH], w[:, pos, kb * P:(kb + 1) * P],
                                       x[:, kb, c * CH:(c + 1) * CH],
                                       start=(kb == 0 and n == 0), stop=(kb == KB - 1 and n == 2))
            mm.then_inc(sem, value)

        def ln_pe(pe, L, between=None):
            for c in range(3):
                for kb in range(KB):
                    mm = pe.matmul(ps[:, c, 0:CH], avg[:, :], acc[:, kb, c * CH:(c + 1) * CH],
                                   start=(kb == 0), stop=(kb == KB - 1))
            mm.then_inc(S["ln_mean"], 1)
            if between:
                between()
            for kb in range(KB):
                pe.wait_ge(S["ln_sq"], KB * L + kb + 1)
                for c in range(3):
                    mm = pe.matmul(ps[:, 3 + c, 0:CH], avg[:, :], tmp[:, kb % 2, c * CH:(c + 1) * CH],
                                   start=(kb == 0), stop=(kb == KB - 1))
                mm.then_inc(S["ln_sqread"], 1)

        def ln_dve(dve, L, ops):
            dve.wait_ge(S["ln_mean"], L + 1)
            for kb in range(KB):
                dve.tensor_tensor(tri(acc[:, kb, :]), tri(acc[:, kb, :]), pset(0), ALU.subtract) \
                    .then_inc(S["ln_cent"], 1)
            dve.wait_ge(S["ln_rstd"], L + 1)
            dve.wait_ge(S["ln_cent"], KB * (L + 1))
            for kb in range(KB):
                dve.scalar_tensor_tensor(out=acc[:, kb, :], in0=acc[:, kb, :], scalar=lnp[:, 2 * L, kb:kb + 1],
                                         in1=tmp[:, 3, :], op0=ALU.mult, op1=ALU.mult).then_inc(S["ln_scaled"], 1)
            if ops is not None:
                split_lo(dve, ops, range(0, KB, 2))

        def ln_act(act, L, func, ops):
            nc.scalar.preload_act_table_set("natural_log_exp_and_others")
            for kb in range(KB):
                act.wait_ge(S["ln_cent"], KB * L + kb + 1)
                if kb >= 2:
                    act.wait_ge(S["ln_sqread"], KB * L + kb - 1)
                act.activation(tmp[:, kb % 2, :], acc[:, kb, :], ACT.Square).then_inc(S["ln_sq"], 1)
            act.wait_ge(S["ln_sqread"], KB * (L + 1))
            act.activation(tri(tmp[:, 2, :]), pset(1), ACT.Ln, bias=epsc[:, 0:1]).then_inc(S["ln_log"], 1)
            act.wait_ge(S["ln_log"], L + 1)
            act.activation(tmp[:, 3, :], tmp[:, 2, :], ACT.Exp, scale=-0.5).then_inc(S["ln_rstd"], 1)
            for kb in range(KB + 1):
                if kb < KB:
                    act.wait_ge(S["ln_scaled"], KB * L + kb + 1)
                    act.activation(acc[:, kb, :], acc[:, kb, :], func, bias=lnp[:, 2 * L + 1, kb:kb + 1]).then_inc(S["ln_aff"], 1)
                if kb and ops is not None:
                    act.wait_ge(S["ln_aff"], KB * L + kb)
                    act.copy(xh[:, kb - 1, :], acc[:, kb - 1, :]).then_inc(S["op_hi"], 1)

        def split_lo(dve, ops, blocks=range(KB)):
            for kb in blocks:
                dve.wait_ge(S["op_hi"], ops + kb + 1)
                dve.tensor_tensor(xl[:, kb, :], acc[:, kb, :], xh[:, kb, :].bitcast(F32),
                                  ALU.subtract).then_inc(S["op_lo"], 1)

        def ff_sp(sp, f):
            base = (W_FF1, W_FF2)[f]
            for k in range(4):
                col = (k // 2) * P + (k % 2) * F
                load_tile(sp, 0, base + k, up_w[f][:, :, col:col + P])
            with sp.Fori(0, FG - 1) as g:
                for k in range(4):
                    load_tile(sp, g * 6, base + 4 + k,
                              up_w[f][:, :, bass.ds(g * (2 * P) + (2 * P + (k // 2) * P + (k % 2) * F), P)])
                for k in range(2):
                    load_tile(sp, g * 6, base + 8 + k, down_w[f][bass.ds(g * (2 * P) + k * P, P), :])
            for k in range(2):
                load_tile(sp, 0, base + 64 + k, down_w[f][(FT - 2 + k) * P:(FT - 1 + k) * P, :])

        def ff_pe(pe, f):
            base = (W_FF1, W_FF2)[f]
            wh, wl = WH[base]
            gh, gl = GH[f]
            t0, y0 = FT * f, KB + (KB * FG + KB) * f
            pe.wait_ge(S["op_lo"], (OP_FF1, OP_FF2)[f])

            def up(g, gc, n, nc_, r):
                for t in range(2):
                    pe.wait_ge(S["w_split"], n + (nc_ + 2 * t + 1))
                    pe.wait_ge(S["silu_done"], g * 2 + (2 * gc + t0 + t))
                    if t == 0 and gc > 0:
                        pe.wait_ge(S["acc_done"], g * 8 + (8 * gc + y0 - 9))
                    linear(pe, base, (r + 2 * t) % 4, 0, S["w_used"])
                    pe.wait_ge(S["w_split"], n + (nc_ + 2 * t + 2))
                    pe.wait_ge(S["prod_done"], g * 2 + (2 * gc + t0 + t))
                    if t == 0 and gc > 0:
                        pe.wait_ge(S["acc_done"], g * 8 + (8 * gc + y0 - 8))
                    linear(pe, base, (r + 2 * t + 1) % 4, 1, S["w_used"])

            def down(g, gc, n, nc_, r, par, last=False):
                pe.wait_ge(S["w_split"], n + (nc_ + 2))
                pe.wait_ge(S["prod_lo"], g * 2 + (2 * gc + t0 + 2))
                for d in range(KB):
                    if d < 2:
                        pe.wait_ge(S[("silu_done", "prod_done")[d]],
                                   g * 2 + (2 * gc + t0 + (2 if last else 4)))
                        if last:
                            pe.wait_ge(S["acc_done"], g * 8 + (8 * gc + y0 + d - 1))
                    else:
                        pe.wait_ge(S["acc_done"], g * 8 + (8 * gc + y0 + d - 1))
                    for c in range(3):
                        for k in range(2):
                            for i, (w, x) in enumerate(((wh, gh), (wh, gl), (wl, gh))):
                                mm = pe.matmul(ps[:, 3 * (d % 2) + c, 0:CH], w[:, (r + k) % 4, d * P:(d + 1) * P],
                                               x[:, 2 * par + k, c * CH:(c + 1) * CH],
                                               start=(k == 0 and i == 0), stop=(k == 1 and i == 2))
                    mm.then_inc(S["down_out"], 1) if d < KB - 1 else mm.then_inc(S["w_used"], 2)

            up(0, 0, 0, base, 0)
            with pe.Fori(0, FG - 2, 2) as g:
                for u in range(2):
                    up(g, u + 1, g * 6, base + 4 + 6 * u, 2 * u)
                    down(g, u, g * 6, base + 8 + 6 * u, 2 * u, u)
            down(0, FG - 1, 0, base + 64, 0, 0, last=True)

        def ff_act(act, f):
            base = (W_FF1, W_FF2)[f]
            gh = GH[f][0]
            t0 = FT * f

            def hidden(g, gc, n, nc_, par):
                for t in range(2):
                    act.wait_ge(S["w_used"], n + (nc_ + 2 * t + 1))
                    if gc > 0:
                        act.wait_ge(S["prod_done"], g * 2 + (2 * gc + t0 + t - 1))
                    act.activation(tri(tmp[:, t, :]), pset(0), ACT.Silu).then_inc(S["silu_done"], 1)
                    act.wait_ge(S["prod_done"], g * 2 + (2 * gc + t0 + t + 1))
                    if gc > 0:
                        act.wait_ge(S["w_used"], n + nc_)
                    act.copy(gh[:, 2 * par + t, :], tmp[:, 2 + t, :]).then_inc(S["prod_hi"], 1)

            hidden(0, 0, 0, base, 0)
            with act.Fori(0, FG - 2, 2) as g:
                for u in range(2):
                    hidden(g, u + 1, g * 6, base + 4 + 6 * u, 1 - u)

        def ff_dve(dve, f):
            base = (W_FF1, W_FF2)[f]
            gh, gl = GH[f]
            t0, y0, d0 = FT * f, KB + (KB * FG + KB) * f, (KB - 1) * FG * f

            def hidden(g, gc, n, nc_, par):
                for t in range(2):
                    dve.wait_ge(S["w_used"], n + (nc_ + 2 * t + 2))
                    dve.wait_ge(S["silu_done"], g * 2 + (2 * gc + t0 + t + 1))
                    if gc > 0:
                        dve.wait_ge(S["prod_hi"], g * 2 + (2 * gc + t0 + t - 1))
                    dve.scalar_tensor_tensor(out=tri(tmp[:, 2 + t, :]), in0=tri(tmp[:, t, :]), scalar=0.5,
                                             in1=pset(1), op0=ALU.mult, op1=ALU.mult) \
                        .then_inc(S["prod_done"], 1)
                    dve.wait_ge(S["prod_hi"], g * 2 + (2 * gc + t0 + t + 1))
                    dve.tensor_tensor(gl[:, 2 * par + t, :], tmp[:, 2 + t, :],
                                      gh[:, 2 * par + t, :].bitcast(F32), ALU.subtract) \
                        .then_inc(S["prod_lo"], 1)

            def add(g, gc, n):
                for d in range(KB):
                    if d < KB - 1:
                        dve.wait_ge(S["down_out"], g * 7 + (7 * gc + d0 + d + 1))
                    else:
                        dve.wait_ge(S["w_used"], n)
                    dve.wait_ge(S["acc_done"], g * 8 + (8 * gc + y0 + d - 7))
                    dve.tensor_tensor(tri(acc[:, d, :]), tri(acc[:, d, :]), pset(d % 2), ALU.add) \
                        .then_inc(S["acc_done"], 1)

            hidden(0, 0, 0, base, 0)
            with dve.Fori(0, FG - 2, 2) as g:
                for u in range(2):
                    hidden(g, u + 1, g * 6, base + 4 + 6 * u, 1 - u)
                    add(g, u, g * 6 + (base + 10 + 6 * u))
            add(0, FG - 1, base + 66)

        def cv_sp(sp):
            with sp.Fori(0, KB) as m:
                for k, col in enumerate((3 * D, 4 * D, 5 * D, 6 * D)):
                    load_tile(sp, m * 4, W_CONV + k, in_w[:, :, bass.ds(m * P + col, P)])

        def side_prod(j):
            return (tmp[:, 3, 0:SEQ], prod1[:, :])[j % 2]

        def cv_pool(pool):
            for k in range(4):
                split_tile(pool, whc, wlc, 0, W_CONV + k, k, None)
            split_lo(pool, OP_FF1, range(1, KB, 2))
            with pool.Fori(0, KB - 1) as m:
                for k in range(4):
                    split_tile(pool, whc, wlc, m * 4, W_CONV + 4 + k, k, m * 4 + (W_CONV + k + 1))
                    side_sums(pool, m, 0, ((), (1, 2, 3), (4, 5), ())[k])
            side_sums(pool, 0, KB - 1, range(1, SIDE))

        def side_sums(pool, m, dm, taps):
            for j in taps:
                pool.wait_ge(S["side_prod"], m * SIDE + (dm * SIDE + j + 1))
                if j == 1:
                    pool.wait_ge(S["tap_done"], m * TAPS + dm * TAPS)
                else:
                    pool.wait_ge(S["side_sum"], m * (SIDE - 1) + (dm * (SIDE - 1) + j - 1))
                pool.tensor_tensor(side[:, :], side_prod(0) if j == 1 else side[:, :], side_prod(j), ALU.add) \
                    .then_inc(S["side_sum"], 1)

        def side_products(act, m, taps):
            for j in taps:
                if j >= 2:
                    act.wait_ge(S["side_sum"], m * (SIDE - 1) + max(j - 2, 1))
                else:
                    act.wait_ge(S["side_sum"], m * (SIDE - 1))
                act.activation(side_prod(j), glu[:, MAIN + j:MAIN + j + SEQ], ACT.Identity,
                               scale=wm[:, MAIN + j:MAIN + j + 1]).then_inc(S["side_prod"], 1)

        def hist_pe(pe):
            pe.wait_ge(S["hist_in"], 16)
            n = DB * HIST // 2
            for m in range(KB):
                if m >= 2:
                    pe.wait_ge(S["hist_kept"], m - 1)
                for j in range(2):
                    mm = pe.transpose(ps[:, 6 + m % 2, j * n:(j + 1) * n], hist_raw[:, j, m * P:(m + 1) * P],
                                      ident[0:n, 0:n])
                mm.then_inc(S["hist_turned"], 1)

        def cv_pe(pe):
            pe.wait_ge(S["op_lo"], OP_CONV)
            pe.wait_ge(S["hist_kept"], KB)
            with pe.Fori(0, KB) as m:
                for k, (sem, add) in enumerate((("siga_done", 0), ("sigb_done", 0), ("glu_done", 1), ("csig_done", 1))):
                    pe.wait_ge(S["w_split"], m * 4 + (W_CONV + k + 1))
                    pe.wait_ge(S[sem], m + add)
                    linear(pe, W_CONV, k, k % 2, S["w_used"])
                pe.wait_ge(S["glu_done"], m + 1)
                pe.wait_ge(S["tail_kept"], m)
                pe.transpose(ps[:, 6, 0:P], glu[:, SEQ:SEQ + P], ident[:, :]).then_inc(S["tail_turned"], 1)

        def cv_act(act):
            with act.Fori(0, KB) as m:
                act.wait_ge(S["w_used"], m * 4 + (W_CONV + 2))
                act.wait_ge(S["glu_done"], m)
                act.activation(tri(tmp[:, 0, :]), pset(1), ACT.Sigmoid).then_inc(S["csig_done"], 1)
                act.wait_ge(S["glu_done"], m + 1)
                side_products(act, m, range(0, 4))
                for k, (sem, dst) in enumerate((("siga", sig_a_d), ("sigb", sig_b_d))):
                    act.wait_ge(S["w_used"], m * 4 + (W_CONV + 3 + k))
                    act.wait_ge(S[sem + "_saved"], m * 16)
                    act.activation(tri(tmp[:, 1 + k, :]), pset(k), ACT.Sigmoid,
                                   bias=bgate[:, bass.ds(m + k * KB, 1)]).then_inc(S[sem + "_done"], 1)
                    act.wait_ge(S[sem + "_done"], m + 1)
                    act.dma_start(dst[bass.ds(m, 1), :, :].rearrange("a p t -> (a p) t"), tmp[:, 1 + k, :]) \
                        .then_inc(S[sem + "_saved"], 16)
                    if k == 0:
                        side_products(act, m, range(4, SIDE))
                act.wait_ge(S["tail_turned"], m + 1)
                act.copy(tail[:, bass.ds(m * P, P)], ps[0:HIST + NS, 6, 0:P]).then_inc(S["tail_kept"], 1)
            act.wait_ge(S["tail_kept"], KB)
            act.dma_start(O["new_conv_p"].rearrange("a b i c -> (a b i) c"), tail[0:HIST, :]) \
                .then_inc(S["tail_saved"], 16)
            for b in range(DB):
                act.dma_start(O["new_conv_s"][0, b, HIST - DQ:HIST, :], tail[HIST + DQ * b:HIST + DQ * (b + 1), :]) \
                    .then_inc(S["tail_saved"], 16)

        def cv_dve(dve):
            dve.wait_ge(S["w_used"], W_CONV)
            dve.memset(glu[:, 0:HIST], 0.0).then_inc(S["pad_set"], 1)
            dve.memset(glu[:, HIST + T:], 0.0).then_inc(S["pad_set"], 1)
            for m in range(KB):
                dve.wait_ge(S["hist_turned"], m + 1)
                dve.tensor_copy(hist[:, m, :], ps[:, 6 + m % 2, 0:DB * HIST]).then_inc(S["hist_kept"], 1)

        def tap_place(j, q):
            return 4 + (3 * j + q + 1 if j < MAIN else 3 * MAIN + j - MAIN + 1)

        def cv_dve_main(dve):
            dve.wait_ge(S["x1_saved"], 16 * KB)
            dve.wait_ge(S["hist_kept"], KB)
            dve.wait_ge(S["pad_set"], 2)
            with dve.Fori(0, KB) as m:
                dve.wait_ge(S["tap_done"], m * TAPS)
                dve.tensor_copy(wm[:, 0:CW], wdw[:, bass.ds(m, 1), :].rearrange("p a w -> p (a w)")) \
                    .then_inc(S["tap_done"], 1)
                dve.tensor_copy(wm[:, CW:CW + 1], bdw[:, bass.ds(m, 1)]).then_inc(S["tap_done"], 1)
                dve.tensor_copy(ext[:, :, 0:HIST], hist[:, bass.ds(m, 1), :].rearrange("p a (b i) -> p (a b) i", b=DB)) \
                    .then_inc(S["tap_done"], 1)
                dve.wait_ge(S["w_used"], m * 4 + (W_CONV + 1))
                dve.wait_ge(S["csig_done"], m + 1)
                dve.wait_ge(S["tail_turned"], m)
                dve.wait_ge(S["side_prod"], m * SIDE)
                dve.tensor_tensor(tri(glu[:, HIST:HIST + T]), tri(tmp[:, 0, :]), pset(0), ALU.mult) \
                    .then_inc(S["glu_done"], 1)
                dve.wait_ge(S["glu_done"], m + 1)
                dve.tensor_copy(ext[:, :, HIST:HIST + DQ],
                                glu[:, HIST + SEQ:HIST + T].rearrange("p (b q) -> p b q", b=DB)) \
                    .then_inc(S["tap_done"], 1)
                half = SEQ // 2
                for j in range(CW):
                    for q in range(3) if j < MAIN else (2,):
                        dve.wait_ge(S["tap_done"], m * TAPS + (tap_place(j - 1, q) if j else 4))
                        if q < 2:
                            src = glu[:, q * half + j:q * half + j + half]
                            old = cbuf[:, q * half:(q + 1) * half]
                        else:
                            src = ext[:, :, j:j + DQ]
                            old = cbuf[:, SEQ:T].rearrange("p (b q) -> p b q", b=DB)
                            new = acc[:, bass.ds(m, 1), SEQ:T].rearrange("p a (b q) -> p (a b) q", b=DB)
                        dst = new if q == 2 and j == CW - 1 else old
                        if j == 0:
                            dve.tensor_scalar(dst, src, wm[:, 0:1], wm[:, CW:CW + 1], ALU.mult, ALU.add) \
                                .then_inc(S["tap_done"], 1)
                        else:
                            dve.scalar_tensor_tensor(out=dst, in0=src, scalar=wm[:, j:j + 1], in1=old,
                                                     op0=ALU.mult, op1=ALU.add).then_inc(S["tap_done"], 1)
                dve.wait_ge(S["tap_done"], m * TAPS + tap_place(MAIN - 1, 1))
                dve.wait_ge(S["side_sum"], m * (SIDE - 1) + (SIDE - 1))
                dve.tensor_tensor(acc[:, bass.ds(m, 1), 0:SEQ].rearrange("p a t -> p (a t)"), cbuf[:, 0:SEQ],
                                  side[:, :], ALU.add).then_inc(S["tap_done"], 1)

        def at_sp(sp):
            with sp.Fori(0, KB - 1, 2) as m:
                for u in range(2):
                    for k in range(3):
                        load_tile(sp, m * 3, W_ATT + 3 * u + k, in_w[:, :, bass.ds(m * P + (u * P + k * D), P)])

        k_t, v_t = tmp[:, 0, :], tmp[:, 1, :]

        def zbank(i):
            return i % 6

        def at_linear(pe, m, t, s, c):
            for kb in range(KB):
                for n, (w, x) in enumerate(((wha, xh), (wha, xl), (wla, xh))):
                    mm = pe.matmul(ps[:, 3 * s + c, 0:CH], w[:, t % 3, kb * P:(kb + 1) * P],
                                   x[:, kb, c * CH:(c + 1) * CH],
                                   start=(kb == 0 and n == 0), stop=(kb == KB - 1 and n == 2))
            if c == 2:
                mm.then_inc(S["w_used"], 1)

        def at_pe(pe):
            pe.wait_ge(S["ln_cent"], 2 * KB)
            pe.wait_ge(S["ln_log"], 2)
            pe.wait_ge(S["ln_cent"], 2 * KB)
            pe.wait_ge(S["ln_log"], 2)
            pe.wait_ge(S["w_split"], W_ATT + 1)
            for c in range(3):
                at_linear(pe, 0, 0, 0, c)
            with pe.Fori(0, KB - 1) as m:
                at_pair_pe(pe, m, 0, True)
            at_pair_pe(pe, 0, KB - 1, False)

        def at_pair_pe(pe, m, dm, more):
            def count(each, plus):
                return m * each + (dm * each + plus)

            pe.wait_ge(S["a_done"], count(NSTEP, 0))
            pe.wait_ge(S["w_split"], count(3, W_ATT + 2))
            for c in range(3):
                at_linear(pe, m, 1, 1, c)
            pe.wait_ge(S["w_split"], count(3, W_ATT + 3))
            pe.wait_ge(S["q_hi"], count(1, 1))
            pe.wait_ge(S["q_lo"], count(1, 1))
            for c in range(3):
                at_linear(pe, m, 2, 0, c)
            pe.wait_ge(S["k_raw"], count(1, 1))
            pe.wait_ge(S["k_lo"], count(1, 1))
            for kb in range(KB):
                pe.transpose(ps[:, 3 + kb // 4, (kb % 4) * P:(kb % 4 + 1) * P], k_t[:, kb * P:(kb + 1) * P], ident[:, :])
            pe.transpose(ps[0:NS, 5, 0:P], k_t[:, SEQ:T], ident[:, :]).then_inc(S["k_turned"], 1)
            for i in range(NSTEP + LAG_OUT):
                if i < NSTEP:
                    c, kb, h = STEPS[i]
                    off, _ = chain(STEPS[i])
                    out = ps[:, zbank(i), off:512]
                    if i == 0:
                        pe.wait_ge(S["v_raw"], count(1, 1))
                    if i == 2:
                        pe.wait_ge(S["o_kept"], count(4, 0))
                        pe.wait_ge(S["k_nat"], count(2, 2))
                        for t in range(KB):
                            pe.transpose(ps[:, 6 + t // 4, (t % 4) * P:(t % 4 + 1) * P],
                                         v_t[:, t * P:(t + 1) * P], ident[:, :])
                        pe.transpose(ps[0:NS, 5, 0:P], v_t[:, SEQ:T], ident[:, :]).then_inc(S["v_turned"], 1)
                    if i == 5:
                        pe.wait_ge(S["v_nat"], count(2, 2))
                    if i >= 6:
                        pe.wait_ge(S["a_done"], count(NSTEP, i - 5))
                    rows = slice(HD * h, HD * (h + 1))
                    for n, (a, b) in enumerate(((kh, qh), (kh, ql), (kl, qh))):
                        mm = pe.matmul(out, a[rows, kb * P:(kb + 1) * P], b[rows, 512 * c + off:512 * (c + 1)],
                                       start=(n == 0), stop=False, skip_group_check=True)
                    if kb >= 4 * c:
                        mm = pe.matmul(ps[:, zbank(i), off:off + P], identb[:, :], dmask[:, :],
                                       start=False, stop=False, skip_group_check=True)
                    mm.then_inc(S["z_ready"], 1)
                j = i - LAG_SUM
                if 0 <= j < NSTEP:
                    off, before = chain(STEPS[j])
                    h = STEPS[j][2]
                    pe.wait_ge(S["sp_ready"], count(NSTEP, j + 1))
                    if before is not None:
                        pe.wait_ge(S["run_done"], count(RUN_TOTAL, sum(RUN_OPS[:j - 1])))
                        pe.matmul(ps[:, zbank(j), before:512], negones[:, :], run[:, h, before:512],
                                  start=False, stop=False, skip_group_check=True)
                    pe.matmul(ps[:, zbank(j), off:512], negtri[:, :], sp_buf(j)[:, off:512],
                              start=False, stop=True, skip_group_check=True).then_inc(S["s_ready"], 1)
                if more and NSTEP <= i < NSTEP + 3:
                    c = i - NSTEP
                    pe.wait_ge(S["a_done"], count(NSTEP, NSTEP - 5 + c))
                    if c == 0:
                        pe.wait_ge(S["w_split"], count(3, W_ATT + 4))
                    at_linear(pe, m, 3, 0, c)
                j = i - LAG_OUT
                if 0 <= j < NSTEP:
                    c, kb, h = STEPS[j]
                    off, before = chain(STEPS[j])
                    if j == 0:
                        pe.wait_ge(S["v_lo"], count(1, 1))
                    if before is None:
                        pe.wait_ge(S["o_kept"], count(4, 2 * c))
                    pe.wait_ge(S["a_lo"], count(NSTEP, j + 1))
                    for n, (a, b) in enumerate(((vh, ah), (vh, al), (vl, ah))):
                        mm = pe.matmul(ps[:, 6 + h, off:512], a[:, kb, :], b[:, j % 3, off:512],
                                       start=(before is None and n == 0), stop=(kb == 0 and n == 2),
                                       skip_group_check=True)
                    mm.then_inc(S["v_used"], 1)

        def e_buf(i):
            return tmp[:, :, :].rearrange("p a t -> p (a t)")[:, (i % 5) * 512:(i % 5 + 1) * 512]

        def sp_buf(i):
            return tmp[:, :, :].rearrange("p a t -> p (a t)")[:, (5 + i % 3) * 512:(6 + i % 3) * 512]

        def token_major(act, m, n):
            turned, kept, saved = (("k_turned", "k_nat", "k_saved"), ("v_turned", "v_nat", "v_saved"))[n]
            bank = 3 + 3 * n
            act.wait_ge(S[turned], m + 1)
            act.wait_ge(S[saved], m * 32)
            if n:
                act.wait_ge(S["v_lo"], m)
            act.copy(nat[:, n, :, :], ps[:, bank:bank + 2, :].rearrange("p a (b c) -> p (a b) c", b=4)) \
                .then_inc(S[kept], 1)
            act.copy(nat_s[:, n, :], ps[0:NS, 5, 0:P]).then_inc(S[kept], 1)
            act.wait_ge(S[kept], m * 2 + 2)
            act.dma_start(new_p[n][:, :, bass.ds(m * P, P)], nat[:, n, :, :]).then_inc(S[saved], 16)
            act.dma_start(new_s[n][:, bass.ds(m * P, P)], nat_s[:, n, :]).then_inc(S[saved], 16)

        def at_act(act):
            act.wait_ge(S["tail_saved"], 16 * (DB + 1))
            act.wait_ge(S["conv_saved"], 16 * KB)
            nc.scalar.preload_act_table_set("natural_log_exp_and_others")
            with act.Fori(0, KB) as m:
                act.wait_ge(S["w_used"], m * 3 + (W_ATT + 1))
                act.activation(tri(qh[:, :]), pset(0), ACT.Copy, scale=SCALE).then_inc(S["q_hi"], 1)
                act.wait_ge(S["w_used"], m * 3 + (W_ATT + 2))
                act.copy(tri(kh[:, :]), pset(1)).then_inc(S["k_hi"], 1)
                act.wait_ge(S["a_lo"], m * NSTEP)
                act.copy(tri(k_t), pset(1)).then_inc(S["k_raw"], 1)
                act.wait_ge(S["w_used"], m * 3 + (W_ATT + 3))
                act.copy(tri(v_t), pset(0)).then_inc(S["v_raw"], 1)
                token_major(act, m, 0)
                for i in range(NSTEP + LAG_OUT):
                    if i == 2:
                        token_major(act, m, 1)
                        act.copy(vh[:, :, :], nat[:, 1, :, :]).then_inc(S["v_hi"], 1)
                    if i < NSTEP:
                        off, _ = chain(STEPS[i])
                        e = e_buf(i)[:, off:512]
                        act.wait_ge(S["z_capped"], m * NSTEP + (i + 1))
                        act.activation(e, e, ACT.Exp).then_inc(S["e_done"], 1)
                        act.wait_ge(S["e_done"], m * NSTEP + (i + 1))
                        act.activation(e, e, ACT.Ln, bias=1.0).then_inc(S["l_done"], 1)
                    if i in (8 + LAG_OUT, NSTEP + LAG_OUT - 1):
                        c = 0 if i < NSTEP else 1
                        act.wait_ge(S["v_used"], m * NSTEP + (8 if c == 0 else NSTEP))
                        for h in range(2):
                            rows = slice(HD * h, HD * (h + 1))
                            act.copy(acc[rows, bass.ds(m, 1), 512 * c:512 * (c + 1)].rearrange("p a t -> p (a t)"),
                                     ps[rows, 6 + h, :]).then_inc(S["o_kept"], 1)
                    j = i - LAG_SUM
                    if 0 <= j < NSTEP:
                        off, _ = chain(STEPS[j])
                        h = STEPS[j][2]
                        act.wait_ge(S["s_ready"], m * NSTEP + (j + 1))
                        act.activation(e_buf(j)[:, off:512], ps[:, zbank(j), off:512], ACT.Exp,
                                       bias=bias_m[:, h:h + 1]).then_inc(S["a_done"], 1)
                        act.wait_ge(S["a_done"], m * NSTEP + (j + 1))
                        if j >= 3:
                            act.wait_ge(S["v_used"], m * NSTEP + (j - 2))
                        act.copy(ah[:, j % 3, off:512], e_buf(j)[:, off:512]).then_inc(S["a_hi"], 1)

        def at_dve(dve):
            with dve.Fori(0, KB) as m:
                dve.wait_ge(S["a_done"], m * NSTEP)
                dve.wait_ge(S["tail_saved"], 16 * (DB + 1))
                dve.tensor_copy(bias_m[:, :], bias_p[:, bass.ds(m * 2, 2)]).then_inc(S["bias_set"], 1)
                dve.wait_ge(S["q_hi"], m + 1)
                dve.tensor_scalar(qs[:, bass.ds(m, 1), :].rearrange("p a t -> p (a t)"), ps[:, 2, CH - NS:CH],
                                  SCALE, None, ALU.mult).then_inc(S["s_row"], 1)
                dve.scalar_tensor_tensor(out=tri(ql[:, :]), in0=pset(0), scalar=SCALE,
                                         in1=tri(qh[:, :].bitcast(F32)), op0=ALU.mult, op1=ALU.subtract) \
                    .then_inc(S["q_lo"], 1)
                dve.wait_ge(S["k_raw"], m + 1)
                dve.tensor_copy(ks[:, bass.ds(m, 1), :].rearrange("p a t -> p (a t)"), ps[:, 5, CH - NS:CH]) \
                    .then_inc(S["s_row"], 1)
                dve.tensor_tensor(tri(kl[:, :]), pset(1), tri(kh[:, :].bitcast(F32)), ALU.subtract) \
                    .then_inc(S["k_lo"], 1)
                dve.wait_ge(S["bias_set"], m + 1)
                for i in range(NSTEP + LAG_OUT):
                    if i == 4:
                        dve.wait_ge(S["v_hi"], m + 1)
                        dve.tensor_tensor(vl[:, :, :], nat[:, 1, :, :], vh[:, :, :].bitcast(F32), ALU.subtract) \
                            .then_inc(S["v_lo"], 1)
                    if i < NSTEP:
                        off, _ = chain(STEPS[i])
                        h = STEPS[i][2]
                        dve.wait_ge(S["z_ready"], m * NSTEP + (i + 1))
                        if i >= 5:
                            dve.wait_ge(S["a_hi"], m * NSTEP + (i - 4))
                            dve.wait_ge(S["a_lo"], m * NSTEP + (i - 4))
                        dve.tensor_scalar(e_buf(i)[:, off:512], ps[:, zbank(i), off:512], bias_m[:, h:h + 1],
                                          ZCAP, ALU.add, ALU.min).then_inc(S["z_capped"], 1)
                    j = i - LAG_SUM - 1
                    if 0 <= j < NSTEP and run_ops(STEPS[j]):
                        h = STEPS[j][2]
                        dve.wait_ge(S["s_ready"], m * NSTEP + (j + 1))
                        dve.wait_ge(S["run_done"], m * RUN_TOTAL + sum(RUN_OPS[:j]))
                        for lo, hi, adds in run_ops(STEPS[j]):
                            s = sp_buf(j)[:, lo:hi]
                            r = run[:, h, lo:hi]
                            ins = dve.tensor_tensor(r, r, s, ALU.add) if adds else dve.tensor_copy(r, s)
                            ins.then_inc(S["run_done"], 1)
                    j = i - 1
                    if 0 <= j < NSTEP:
                        off, _ = chain(STEPS[j])
                        h = STEPS[j][2]
                        dve.wait_ge(S["l_done"], m * NSTEP + (j + 1))
                        if j >= 3:
                            dve.wait_ge(S["s_ready"], m * NSTEP + (j - 2))
                            dve.wait_ge(S["run_done"], m * RUN_TOTAL + sum(RUN_OPS[:j - 2]))
                        dve.scalar_tensor_tensor(out=sp_buf(j)[:, off:512], in0=ps[:, zbank(j), off:512],
                                                 scalar=bias_m[:, h:h + 1], in1=e_buf(j)[:, off:512],
                                                 op0=ALU.add, op1=ALU.max).then_inc(S["sp_ready"], 1)
                    j = i - LAG_SUM - 1
                    if 0 <= j < NSTEP:
                        off, _ = chain(STEPS[j])
                        dve.wait_ge(S["a_hi"], m * NSTEP + (j + 1))
                        if j >= 3:
                            dve.wait_ge(S["v_used"], m * NSTEP + (j - 2))
                        dve.tensor_tensor(al[:, j % 3, off:512], e_buf(j)[:, off:512],
                                          ah[:, j % 3, off:512].bitcast(F32), ALU.subtract) \
                            .then_inc(S["a_lo"], 1)

        NP = 2 * PAGES
        GCOLS = KB * 2 * P

        def page_slot(k):
            return wraw[:, k % 8, :] if k % 8 < 2 else pages[:, k % 8 - 2, :]

        def flat(t):
            return t[:, :, :].rearrange("p a t -> p (a t)")

        def kt_group(t, g):
            return flat(t)[:, (g % 2) * GCOLS:(g % 2 + 1) * GCOLS]

        def kt_block(t, k):
            return kt_group(t, k // 2).rearrange("p (e n) -> p e n", e=KB)[:, :, (k % 2) * P:(k % 2 + 1) * P]

        def kt_psum(k):
            return ps[:, 2 * (k % 2):2 * (k % 2) + 2, :].rearrange("p a (b c) -> p (a b) c", b=4)

        def v_slot(t, k):
            return flat(t)[:, 2 * GCOLS + (k % 4) * D:2 * GCOLS + (k % 4 + 1) * D]

        def out_banks(b):
            return 6 - 2 * b

        def page_count(k):
            return (k // 8 + 1) * 16

        def load_page(sp, i, d, kv, k):
            page = sp.value_load(pt_sb[0:1, bass.ds(i * NP + (d * NP + k), 1)], min_val=0, max_val=POOL - 1)
            return page_rows[kv][bass.ds(page, 1), :, :].rearrange("a p c -> (a p) c")

        def k_pages_sp(sp, i, d, lo, hi):
            for k in range(lo, hi):
                src = load_page(sp, i, d, 0, k)
                if k >= 8:
                    sp.wait_ge(S["pk_turned"], i * NP + (d * NP + k - 7))
                elif d:
                    sp.wait_ge(S["pv_lo"], i * NP + (k + 9))
                sp.dma_start(page_slot(k), src).then_inc(S[f"page_in{k % 8}"], 16)

        def v_pages_sp(sp, i, d):
            for k in range(NP):
                src = load_page(sp, i, d, 1, k)
                if k >= 8:
                    sp.wait_ge(S["pv_lo"], i * NP + (d * NP + NP + k - 7))
                elif d:
                    sp.wait_ge(S["pv_lo"], i * NP + (d * NP + k + 9))
                else:
                    sp.wait_ge(S["pk_turned"], i * NP + (NP + k + 9))
                sp.dma_start(page_slot(k), src).then_inc(S[f"page_in{k % 8}"], 16)

        def sa_sp(sp):
            sp.wait_ge(S["w_used"], W_OUT)
            k_pages_sp(sp, 0, 0, 0, 8)
            sp.wait_ge(S["v_used"], NSTEP * KB)
            sp.wait_ge(S["a_lo"], NSTEP * KB)
            sp.wait_ge(S["o_kept"], 4 * KB)
            sp.wait_ge(S["v_saved"], 32 * KB)
            sp.wait_ge(S["k_saved"], 32 * KB)
            sp.dma_start(vn_raw[:, :], new_s[1]).then_inc(S["sconst_in"], 16)
            sp.dma_start(mbd[:, :], A["c_mbd"]).then_inc(S["sconst_in"], 16)
            sp.dma_start(sel[:, :], A["c_sel"]).then_inc(S["sconst_in"], 16)
            sp.dma_start(smask[:, :, :], A["c_smask"]).then_inc(S["sconst_in"], 16)
            k_pages_sp(sp, 0, 0, 8, NP)
            sp.wait_ge(S["pk_turned"], NP)
            with sp.Fori(0, DB // 2 - 1) as i:
                k_pages_sp(sp, i, 1, 0, NP)
                v_pages_sp(sp, i, 0)
            v_pages_sp(sp, 0, DB // 2 - 1)

        def k_phase_pe(pe, i, d):
            for g in range(PAGES + 1):
                if g < PAGES:
                    for u in range(2):
                        k = 2 * g + u
                        pe.wait_ge(S[f"page_in{k % 8}"], i * 64 + (d * 32 + page_count(k)))
                        pe.wait_ge(S["pk_lo"], i * NP + (d * NP + max(k - 1, 0)))
                        if g == 0 and d:
                            pe.wait_ge(S["sa_lo"], i * 2 + 2)
                            pe.wait_ge(S["so_kept"], i)
                        for e in range(KB):
                            mm = pe.transpose(ps[:, 2 * u + e // 4, (e % 4) * P:(e % 4 + 1) * P],
                                              page_slot(k)[:, e * P:(e + 1) * P], ident[:, :])
                        mm.then_inc(S["pk_turned"], 1)
                if g:
                    q = g - 1
                    pe.wait_ge(S["pk_lo"], i * NP + (d * NP + 2 * g))
                    pe.wait_ge(S["sz_kept"], i * 9 + (d * 9 + max(q - 1, 0)))
                    if q == 0:
                        pe.wait_ge(S["qb_lo"], i * NP + (d * NP + NP))
                    for e in range(KB):
                        for n, (a, b) in enumerate(((qbh, xh), (qbh, xl), (qbl, xh))):
                            mm = pe.matmul(ps[:, 4 + q % 2, 0:2 * P], a[:, e, :],
                                           kt_group(b, q)[:, e * 2 * P:(e + 1) * 2 * P],
                                           start=(e == 0 and n == 0), stop=(e == KB - 1 and n == 2))
                    mm.then_inc(S["sz_out"], 1)
            pe.wait_ge(S["sz_kept"], i * 9 + (d * 9 + 7))
            for e in range(KB):
                for n, (a, b) in enumerate(((qbh, ksh), (qbh, ksl), (qbl, ksh))):
                    pe.matmul(ps[:, 4, 0:NS], a[:, e, :], b[:, e, :], start=(e == 0 and n == 0), stop=False)
            mask = smask[:, bass.ds(i + d, 1), :].rearrange("p a n -> p (a n)") if d else smask[:, 0, :]
            pe.matmul(ps[:, 4, 0:NS], ident[:, :], mask, start=False, stop=True).then_inc(S["sz_out"], 1)

        def turn_weights_pe(pe, i, d):
            pe.wait_ge(S["s_a"], i + (d + 1))
            for kb in range(PAGES):
                pe.transpose(ps[:, kb // 4, (kb % 4) * P:(kb % 4 + 1) * P], tmp[:, 1, kb * P:(kb + 1) * P], ident[:, :])
            pe.transpose(ps[0:NS, 2, 0:P], tmp[:, 1, PAST:KEYS], ident[:, :]).then_inc(S["sa_turned"], 1)

        def v_phase_pe(pe, i, d):
            pe.wait_ge(S["sa_lo"], i * 2 + (d * 2 + 2))
            for b in range(2):
                bank = out_banks(b)
                if b == 0:
                    pe.wait_ge(S["so_mask"], i * 2 + d * 2)
                else:
                    pe.wait_ge(S["sz_kept"], i * 9 + (9 * min(d + 2, DB // 2)))
                for pg in range(PAGES + 1):
                    new = pg == PAGES
                    k = PAGES * b + pg
                    if not new:
                        pe.wait_ge(S["pv_lo"], i * NP + (d * NP + NP + k + 1))
                    r = slice(0, NS) if new else slice(0, P)
                    for n2 in range(2):
                        c = slice(n2 * 512, (n2 + 1) * 512)
                        vv = (vnh[:, c], vnl[:, c]) if new else (v_slot(xh, k)[:, c], v_slot(xl, k)[:, c])
                        for n, (a, x) in enumerate(((ath, vv[0]), (ath, vv[1]), (atl, vv[0]))):
                            mm = pe.matmul(ps[:, bank + n2, :], a[r, pg, :], x,
                                           start=(pg == 0 and n == 0), stop=(new and n == 2))
                    mm.then_inc(S["so_out" if new else "pv_used"], 1)

        def turn_out_pe(pe, i, d):
            pe.wait_ge(S["so_mask"], i * 2 + (d * 2 + 2))
            pe.wait_ge(S["so_kept"], i + d)
            for e in range(KB):
                mm = pe.matmul(ps[:, 3, e * 2 * DQ:(e + 1) * 2 * DQ], om[:, e * P:(e + 1) * P], sel[:, :],
                               start=True, stop=True)
            mm.then_inc(S["so_turned"], 1)

        def sa_pe(pe):
            pe.wait_ge(S["sconst_in"], 64)
            pe.wait_ge(S["new_lo"], 1)
            pe.wait_ge(S["pv_lo"], NP)
            pe.wait_ge(S["a_done"], NSTEP * KB)
            pe.wait_ge(S["o_kept"], 4 * KB)
            k_phase_pe(pe, 0, 0)
            turn_weights_pe(pe, 0, 0)
            with pe.Fori(0, DB // 2 - 1) as i:
                k_phase_pe(pe, i, 1)
                v_phase_pe(pe, i, 0)
                turn_weights_pe(pe, i, 1)
                turn_out_pe(pe, i, 0)
            v_phase_pe(pe, 0, DB // 2 - 1)
            turn_out_pe(pe, 0, DB // 2 - 1)

        def k_phase_act(act, i, d):
            for k in range(NP):
                act.wait_ge(S["pk_turned"], i * NP + (d * NP + k + 1))
                act.wait_ge(S["sz_out"], i * 9 + (d * 9 + max(k // 2 - 1, 0)))
                act.copy(kt_block(xh, k), kt_psum(k)).then_inc(S["pk_hi"], 1)

        def exp_act(act, i, d):
            act.wait_ge(S["s_capped"], i + (d + 1))
            act.activation(tmp[:, 1, :], tmp[:, 1, :], ACT.Exp).then_inc(S["s_exp"], 1)
            act.wait_ge(S["s_exp"], i + (d + 1))
            act.activation(tmp[:, 1, :], tmp[:, 1, :], ACT.Ln, bias=1.0).then_inc(S["s_ln"], 1)

        def weights_act(act, i, d):
            act.wait_ge(S["s_log"], i + (d + 1))
            act.activation(tmp[:, 1, :], tmp[:, 0, :], ACT.Exp).then_inc(S["s_a"], 1)

        def turned_act(act, i, d):
            act.wait_ge(S["sa_turned"], i + (d + 1))
            act.wait_ge(S["so_out"], i * 2 + d * 2)
            act.copy(ath[:, 0:PAGES, :], ps[:, 0:2, :].rearrange("p a (b c) -> p (a b) c", b=4)).then_inc(S["sa_hi"], 1)
            act.copy(ath[0:NS, PAGES, :], ps[0:NS, 2, 0:P]).then_inc(S["sa_hi"], 1)

        def v_phase_act(act, i, d, first_page):
            for k in range(NP):
                if d == 0 and k == 2:
                    exp_act(act, i, 1)
                if d == 0 and k == 8:
                    weights_act(act, i, 1)
                act.wait_ge(S["pv_used"], i * NP + (d * NP + max(k - 3, 0)))
                act.wait_ge(S[f"page_in{k % 8}"], i * 64 + (first_page + page_count(k)))
                act.copy(v_slot(xh, k), page_slot(k)).then_inc(S["pv_hi"], 1)

        def keep_out_act(act, i, d):
            act.wait_ge(S["so_turned"], i + (d + 1))
            src = ps[:, 3, 0:NS * 2].rearrange("p (e n) -> p e n", e=KB)
            act.copy(acc[:, :, bass.ds(i * (2 * DQ) + (d * 2 * DQ + SEQ), 2 * DQ)], src).then_inc(S["so_kept"], 1)

        def sa_act(act):
            act.wait_ge(S["sconst_in"], 64)
            act.wait_ge(S["s_zero"], 2)
            for dst, src in ((ksh, ks), (vnh, vn_raw)):
                act.copy(dst[:], src[:]).then_inc(S["new_hi"], 1)
            k_phase_act(act, 0, 0)
            exp_act(act, 0, 0)
            weights_act(act, 0, 0)
            turned_act(act, 0, 0)
            with act.Fori(0, DB // 2 - 1) as i:
                k_phase_act(act, i, 1)
                v_phase_act(act, i, 0, 64)
                turned_act(act, i, 1)
                keep_out_act(act, i, 0)
            v_phase_act(act, 0, DB // 2 - 1, 7 * 32)
            keep_out_act(act, 0, DB // 2 - 1)

        def qb_block(t, e, h):
            rows = slice(HD * h, HD * (h + 1))
            return t[rows, e, :].rearrange("p (b c) -> p b c", b=2)[:, :, DQ * (2 * e + h):DQ * (2 * e + h + 1)]

        def qs_block(i, e, rows):
            return qs[rows, e, i * (2 * DQ):(i + 1) * (2 * DQ)].rearrange("p (b q) -> p b q", b=2)

        def sa_pool(pool):
            pool.wait_ge(S["s_zero"], 2)
            pool.wait_ge(S["s_row"], 2 * KB)
            for i in range(DB // 2):
                pool.wait_ge(S["sz_out"], i * 9)
                for e in range(KB):
                    for h in range(2):
                        rows = slice(HD * h, HD * (h + 1))
                        ones = one[rows, 0:1].to_broadcast([HD, 2 * DQ]).rearrange("p (b q) -> p b q", b=2)
                        pool.tensor_tensor(qb_block(qbh, e, h), qs_block(i, e, rows), ones, ALU.mult) \
                            .then_inc(S["qb_hi"], 1)
                for e in range(KB):
                    for h in range(2):
                        rows = slice(HD * h, HD * (h + 1))
                        pool.wait_ge(S["qb_hi"], i * NP + (2 * e + h + 1))
                        pool.tensor_tensor(qb_block(qbl, e, h), qs_block(i, e, rows), qb_block(qbh, e, h).bitcast(F32),
                                           ALU.subtract).then_inc(S["qb_lo"], 1)

        def k_phase_dve(dve, i, d):
            for g in range(PAGES + 1):
                if g < PAGES:
                    for k in (2 * g, 2 * g + 1):
                        dve.wait_ge(S["pk_hi"], i * NP + (d * NP + k + 1))
                        dve.tensor_tensor(kt_block(xl, k), kt_psum(k), kt_block(xh, k).bitcast(F32),
                                          ALU.subtract).then_inc(S["pk_lo"], 1)
                if g:
                    q = g - 1
                    rows = slice(64 * (q // 4), 64 * (q // 4) + 64)
                    dve.wait_ge(S["sz_out"], i * 9 + (d * 9 + g))
                    if q == 0:
                        dve.wait_ge(S["s_a"], i + d)
                    dve.tensor_scalar(tmp[rows, 0, (q % 4) * 2 * P:(q % 4 + 1) * 2 * P], ps[rows, 4 + q % 2, 0:2 * P],
                                      bias_s[rows, 0:1], None, ALU.add).then_inc(S["sz_kept"], 1)
            dve.wait_ge(S["sz_out"], i * 9 + (d * 9 + 9))
            dve.tensor_scalar(tmp[:, 0, PAST:KEYS], ps[:, 4, 0:NS], bias_s[:, 0:1], None, ALU.add) \
                .then_inc(S["sz_kept"], 1)

        def softmax_dve(dve, i, d, step):
            if step == 0:
                dve.wait_ge(S["sz_kept"], i * 9 + (d * 9 + 9))
                dve.wait_ge(S["sa_turned"], i + d)
                dve.tensor_scalar(tmp[:, 1, :], tmp[:, 0, :], ZCAP, None, ALU.min).then_inc(S["s_capped"], 1)
            elif step == 1:
                dve.wait_ge(S["s_ln"], i + (d + 1))
                dve.tensor_tensor(tmp[:, 1, :], tmp[:, 0, :], tmp[:, 1, :], ALU.max).then_inc(S["s_chain"], 1)
            elif step == 2:
                dve.wait_ge(S["s_chain"], i * 2 + (d * 2 + 1))
                dve.tensor_tensor_scan(out=tmp[:, 2, ::-1], data0=tmp[:, 1, ::-1], data1=tmp[:, 1, ::-1],
                                       initial=0.0, op0=ALU.add, op1=ALU.bypass).then_inc(S["s_chain"], 1)
            else:
                dve.wait_ge(S["s_chain"], i * 2 + (d * 2 + 2))
                dve.tensor_tensor(tmp[:, 0, :], tmp[:, 0, :], tmp[:, 2, :], ALU.subtract).then_inc(S["s_log"], 1)

        def turned_dve(dve, i, d):
            dve.wait_ge(S["sa_hi"], i * 2 + (d * 2 + 2))
            dve.tensor_tensor(atl[:, 0:PAGES, :], ps[:, 0:2, :].rearrange("p a (b c) -> p (a b) c", b=4),
                              ath[:, 0:PAGES, :].bitcast(F32), ALU.subtract).then_inc(S["sa_lo"], 1)
            dve.tensor_tensor(atl[0:NS, PAGES, :], ps[0:NS, 2, 0:P], ath[0:NS, PAGES, :].bitcast(F32),
                              ALU.subtract).then_inc(S["sa_lo"], 1)

        def mask_out_dve(dve, i, d, b):
            rows = slice(64 * b, 64 * b + 64)
            dve.wait_ge(S["so_out"], i * 2 + (d * 2 + b + 1))
            dve.wait_ge(S["so_turned"], i + d)
            dve.tensor_tensor(om[rows, :], ps[rows, out_banks(b):out_banks(b) + 2, :].rearrange("p a c -> p (a c)"),
                              mbd[rows, :], ALU.mult).then_inc(S["so_mask"], 1)

        def v_phase_dve(dve, i, d):
            for k in range(NP):
                if d == 0 and k in (0, 4, 5, 6):
                    softmax_dve(dve, i, 1, (0, 4, 5, 6).index(k))
                if k == 12:
                    mask_out_dve(dve, i, d, 0)
                dve.wait_ge(S["pv_hi"], i * NP + (d * NP + k + 1))
                dve.tensor_tensor(v_slot(xl, k), page_slot(k), v_slot(xh, k).bitcast(F32), ALU.subtract) \
                    .then_inc(S["pv_lo"], 1)
            mask_out_dve(dve, i, d, 1)

        def sa_dve(dve):
            dve.wait_ge(S["v_used"], NSTEP * KB)
            dve.wait_ge(S["w_used"], W_OUT)
            dve.wait_ge(S["a_hi"], NSTEP * KB)
            dve.wait_ge(S["v_saved"], 32 * KB)
            dve.memset(qbh[:, :, :].bitcast(F32), 0.0).then_inc(S["s_zero"], 1)
            dve.memset(qbl[:, :, :].bitcast(F32), 0.0).then_inc(S["s_zero"], 1)
            dve.wait_ge(S["s_zero"], 2)
            dve.wait_ge(S["sconst_in"], 64)
            dve.wait_ge(S["s_row"], 2 * KB)
            dve.wait_ge(S["new_hi"], 2)
            dve.tensor_tensor(ksl[:], ks[:], ksh[:].bitcast(F32), ALU.subtract).then_inc(S["new_lo"], 1)
            dve.tensor_tensor(vnl[:], vn_raw[:], vnh[:].bitcast(F32), ALU.subtract).then_inc(S["pv_lo"], NP)
            k_phase_dve(dve, 0, 0)
            for step in range(4):
                softmax_dve(dve, 0, 0, step)
            turned_dve(dve, 0, 0)
            with dve.Fori(0, DB // 2 - 1) as i:
                k_phase_dve(dve, i, 1)
                v_phase_dve(dve, i, 0)
                turned_dve(dve, i, 1)
            v_phase_dve(dve, 0, DB // 2 - 1)

        def ou_sp(sp):
            sp.wait_ge(S["so_kept"], DB // 2)
            for n in range(3):
                with sp.Fori(0, KB - 1, 2) as m:
                    for u in range(2):
                        load_tile(sp, m, W_OUT + n * KB + u, out_w[n][:, :, bass.ds(m * P + u * P, P)])

        def ou_pe(pe):
            for n in range(3):
                pe.wait_ge(S["op_lo"], (OP_A, OP_B, OP_OUT)[n])
                with pe.Fori(0, KB - 3, 4) as m:
                    for u in range(4):
                        pe.wait_ge(S["w_split"], m + (W_OUT + n * KB + u + 1))
                        if n or u >= 2:
                            pe.wait_ge(S["mix_out"], m + (n * KB + u - 1))
                        elif u < 2:
                            pe.wait_ge(S["mix_out"], m)
                        linear(pe, W_OUT, u, u % 2, S["w_used"])

        def aux_load(act, src, m, n, u):
            act.wait_ge(S["mix_out"], m + (n + u - 1))
            act.dma_start(tmp[:, u, :], src[bass.ds(m + u, 1), :, :].rearrange("a p t -> (a p) t")) \
                .then_inc(S[f"aux_in{u}"], 16)

        def ou_act(act):
            act.wait_ge(S["so_kept"], DB // 2)
            for kb in range(KB):
                act.copy(xh[:, kb, :], acc[:, kb, :]).then_inc(S["op_hi"], 1)
            act.wait_ge(S["siga_saved"], 16 * KB)
            act.wait_ge(S["sigb_saved"], 16 * KB)
            act.wait_ge(S["sa_turned"], DB // 2)
            act.dma_start(tmp[:, 0, :], sig_a_d[0, :, :]).then_inc(S["aux_in0"], 16)
            act.dma_start(tmp[:, 1, :], sig_a_d[1, :, :]).then_inc(S["aux_in1"], 16)
            with act.Fori(0, KB - 3, 2) as m:
                for u in range(2):
                    act.wait_ge(S["mix_out"], m + (u + 1))
                    act.dma_start(tmp[:, u, :], sig_a_d[bass.ds(m + (u + 2), 1), :, :].rearrange("a p t -> (a p) t")) \
                        .then_inc(S[f"aux_in{u}"], 16)
            act.wait_ge(S["conv_saved"], 16 * KB)
            for kb in range(KB):
                if kb >= 2:
                    act.wait_ge(S["op_lo"], OP_A + kb - 1)
                act.dma_start(tmp[:, 2 + kb % 2, :], conv_d[kb, :, :]).then_inc(S[f"conv_in{kb % 2}"], 16)
                if kb == 0:
                    act.wait_ge(S["w_used"], W_OUT + KB)
                if kb:
                    act.wait_ge(S[f"conv_in{(kb - 1) % 2}"], 16 * ((kb - 1) // 2 + 1))
                    act.copy(xh[:, kb - 1, :], tmp[:, 2 + (kb - 1) % 2, :]).then_inc(S["op_hi"], 1)
            act.wait_ge(S["conv_in1"], 16 * (KB // 2))
            act.copy(xh[:, KB - 1, :], tmp[:, 3, :]).then_inc(S["op_hi"], 1)
            with act.Fori(0, KB - 1, 2) as m:
                for u in range(2):
                    aux_load(act, sig_b_d, m, KB, u)
            act.wait_ge(S["x1_saved"], 16 * KB)
            for u in range(2):
                act.wait_ge(S["mix_out"], 2 * KB + u - 1)
                act.dma_start(tmp[:, u, :], x1_d[u, :, :]).then_inc(S[f"aux_in{u}"], 16)
            act.wait_ge(S["w_used"], W_OUT + 2 * KB)
            for kb in range(KB):
                act.wait_ge(S["mix_out"], KB + kb + 1)
                act.copy(xh[:, kb, :], acc[:, kb, :]).then_inc(S["op_hi"], 1)
            with act.Fori(0, KB - 3, 2) as m:
                for u in range(2):
                    aux_load(act, x1_d, m + 2, 2 * KB, u)

        def ou_dve(dve):
            dve.wait_ge(S["so_kept"], DB // 2)
            split_lo(dve, OP_A - KB)
            for n in range(3):
                if n == 1:
                    for kb in range(KB):
                        dve.wait_ge(S["op_hi"], OP_B - KB + kb + 1)
                        dve.tensor_tensor(xl[:, kb, :], tmp[:, 2 + kb % 2, :], xh[:, kb, :].bitcast(F32),
                                          ALU.subtract).then_inc(S["op_lo"], 1)
                if n == 2:
                    split_lo(dve, OP_OUT - KB)
                with dve.Fori(0, KB - 1, 2) as m:
                    for u in range(2):
                        out = acc[:, bass.ds(m + u, 1), :].rearrange("p a (c n) -> p (a c) n", c=3)
                        aux = tri(tmp[:, u, :])
                        dve.wait_ge(S["w_used"], m + (W_OUT + n * KB + u + 1))
                        dve.wait_ge(S[f"aux_in{u}"], m * 8 + (n * KB // 2 + 1) * 16)
                        if n == 0:
                            dve.tensor_tensor(out, aux, pset(u), ALU.mult).then_inc(S["mix_out"], 1)
                        elif n == 1:
                            dve.tensor_tensor(aux, aux, pset(u), ALU.mult).then_inc(S["mix_tmp"], 1)
                            dve.wait_ge(S["mix_tmp"], m + (u + 1))
                            dve.wait_ge(S["mix_out"], m + (KB + u))
                            dve.tensor_tensor(out, out, aux, ALU.add).then_inc(S["mix_out"], 1)
                        else:
                            dve.scalar_tensor_tensor(out=out, in0=aux, scalar=ALPHA, in1=pset(u), op0=ALU.mult,
                                                     op1=ALU.add).then_inc(S["mix_out"], 1)

        NTOK = SEQ // P + 1

        def tok_rows(k):
            return P if k < NTOK - 1 else NS

        def tok_psum(k, n):
            return ps[:, 2 * (k % 2):2 * (k % 2) + 2, :].rearrange("p a (b c) -> p (a b) c", b=4)[:, :, 0:n]

        block = top.enter_context(nc.Block())

        @block.sync
        def _(sp):
            for dst, name in CONSTS:
                sp.dma_start(dst, A[name]).then_inc(S["const_in"], 16)
            for k in range(NTOK):
                if k >= 2:
                    sp.wait_ge(S["tok_turned"], k - 1)
                src = A["x_prompt"][0, k * P:(k + 1) * P, :] if k < NTOK - 1 else \
                    A["x_sample"].rearrange("b q d -> (b q) d")
                sp.dma_start(tok[0:tok_rows(k), k % 2, :], src).then_inc(S[f"tok_in{k % 2}"], 16)
            sp.dma_start(O["new_conv_s"][0, :, 0:HIST - DQ, :], A["state_conv"][0, :, DQ:HIST, :]) \
                .then_inc(S["state_saved"], 16)
            ff_sp(sp, 0)
            cv_sp(sp)
            at_sp(sp)
            sa_sp(sp)
            ou_sp(sp)
            ff_sp(sp, 1)
            for k in range(NTOK):
                sp.wait_ge(S["y_kept"], k + 1)
                dst = O["y_p"][0, k * P:(k + 1) * P, :] if k < NTOK - 1 else O["y_s"].rearrange("b q d -> (b q) d")
                sp.dma_start(dst, tmp[0:tok_rows(k), k % 2, 0:D]).then_inc(S[f"y_saved{k % 2}"], 16)
            sp.wait_ge(S["y_saved0"], 16 * ((NTOK + 1) // 2))
            sp.wait_ge(S["y_saved1"], 16 * (NTOK // 2))
            sp.wait_ge(S["k_saved"], 32 * KB)
            sp.wait_ge(S["v_saved"], 32 * KB)
            sp.wait_ge(S["tail_saved"], 16 * (DB + 1))
            sp.wait_ge(S["state_saved"], 16)

        @block.gpsimd
        def _(pool):
            pool.memset(one[:, :], 1.0).then_inc(S["one_set"], 1)
            pool.wait_ge(S["one_set"], 1)
            split_phase(pool, W_FF1, W_CONV - W_FF1, 4)
            pool.wait_ge(S["w_used"], W_CONV)
            cv_pool(pool)
            split_phase(pool, W_ATT, W_OUT - W_ATT, 3)
            sa_pool(pool)
            pool.wait_ge(S["so_kept"], DB // 2)
            split_phase(pool, W_OUT, W_FF2 - W_OUT, 4)
            split_phase(pool, W_FF2, W_END - W_FF2, 4, OP_OUT)

        @block.tensor
        def _(pe):
            pe.wait_ge(S["const_in"], 16 * len(CONSTS))
            for k in range(NTOK):
                n = tok_rows(k)
                pe.wait_ge(S[f"tok_in{k % 2}"], 16 * (k // 2 + 1))
                if k >= 2:
                    pe.wait_ge(S["op_lo"], k - 1)
                    pe.wait_ge(S["acc_done"], k - 1)
                for e in range(KB):
                    mm = pe.transpose(ps[:, 2 * (k % 2) + e // 4, (e % 4) * P:(e % 4) * P + n],
                                      tok[0:n, k % 2, e * P:(e + 1) * P], ident[0:n, 0:n])
                mm.then_inc(S["tok_turned"], 1)
            pe.wait_ge(S["acc_init"], 1)
            pe.wait_ge(S["mask_set"], 2)
            ff_pe(pe, 0)
            pe.wait_ge(S["acc_done"], KB + KB * FG)
            ln_pe(pe, 0)
            hist_pe(pe)
            cv_pe(pe)
            pe.wait_ge(S["tap_done"], TAPS * KB)
            pe.wait_ge(S["siga_done"], KB)
            pe.wait_ge(S["sigb_done"], KB)
            ln_pe(pe, 1)
            at_pe(pe)
            sa_pe(pe)
            ou_pe(pe)
            pe.wait_ge(S["mix_out"], 3 * KB)
            ln_pe(pe, 2)
            ff_pe(pe, 1)
            pe.wait_ge(S["acc_done"], 2 * (KB + KB * FG))
            ln_pe(pe, 3)
            for k in range(NTOK):
                n = tok_rows(k)
                pe.wait_ge(S["ln_aff"], 4 * KB)
                if k >= 2:
                    pe.wait_ge(S["y_kept"], k - 1)
                for e in range(KB):
                    mm = pe.transpose(ps[0:n, 2 * (k % 2) + e // 4, (e % 4) * P:(e % 4 + 1) * P],
                                      acc[:, e, k * P:k * P + n], ident[:, :])
                mm.then_inc(S["y_turned"], 1)

        @block.scalar
        def _(act):
            act.wait_ge(S["const_in"], 16 * len(CONSTS))
            for k in range(NTOK):
                n = tok_rows(k)
                act.wait_ge(S["tok_turned"], k + 1)
                act.copy(xh[:, :, k * P:k * P + n], tok_psum(k, n)).then_inc(S["op_hi"], 1)
                act.mul(acc[:, :, k * P:k * P + n], tok_psum(k, n), ALPHA) \
                    .then_inc(S["acc_done" if k < KB else "acc_init"], 1)
            act.wait_ge(S["mask_set"], 2)
            ff_act(act, 0)
            act.wait_ge(S["eps_set"], 1)
            ln_act(act, 0, ACT.Identity, OP_FF1)
            act.dma_start(hist_raw[:, :, :], state_rows.rearrange("(j p) c -> p j c", j=2)) \
                .then_inc(S["hist_in"], 16)
            for kb in range(KB):
                act.wait_ge(S["ln_aff"], kb + 1)
                act.dma_start(x1_d[kb, :, :], acc[:, kb, :]).then_inc(S["x1_saved"], 16)
            cv_act(act)
            act.wait_ge(S["siga_saved"], 16 * KB)
            act.wait_ge(S["sigb_saved"], 16 * KB)
            ln_act(act, 1, ACT.Silu, None)
            for kb in range(KB):
                act.wait_ge(S["ln_aff"], KB + kb + 1)
                act.dma_start(conv_d[kb, :, :], acc[:, kb, :]).then_inc(S["conv_saved"], 16)
            at_act(act)
            sa_act(act)
            ou_act(act)
            ln_act(act, 2, ACT.Identity, OP_OUT)
            for kb in range(KB):
                act.wait_ge(S["op_lo"], OP_OUT + KB)
                act.mul(acc[:, kb, :], acc[:, kb, :], ALPHA).then_inc(S["acc_done"], 1)
            ff_act(act, 1)
            ln_act(act, 3, ACT.Identity, None)

        @block.vector
        def _(dve):
            dve.memset(epsc[:, :], EPS).then_inc(S["eps_set"], 1)
            dve.wait_ge(S["const_in"], 16 * len(CONSTS))
            dve.tensor_copy(identb[:, :], ident[:, :]).then_inc(S["mask_set"], 1)
            dve.tensor_copy(dmask[:, :], tmp[:, 0, 0:P]).then_inc(S["mask_set"], 1)
            for k in range(NTOK):
                n = tok_rows(k)
                dve.wait_ge(S["op_hi"], k + 1)
                dve.wait_ge(S["acc_done" if k < KB else "acc_init"], k + 1 if k < KB else 1)
                dve.tensor_tensor(xl[:, :, k * P:k * P + n], tok_psum(k, n), xh[:, :, k * P:k * P + n].bitcast(F32),
                                  ALU.subtract).then_inc(S["op_lo"], 1)
            dve.wait_ge(S["acc_init"], 1)
            ff_dve(dve, 0)
            dve.wait_ge(S["acc_done"], KB + KB * FG)
            ln_dve(dve, 0, OP_FF1)
            cv_dve(dve)
            cv_dve_main(dve)
            dve.wait_ge(S["tap_done"], TAPS * KB)
            ln_dve(dve, 1, None)
            at_dve(dve)
            sa_dve(dve)
            ou_dve(dve)
            dve.wait_ge(S["mix_out"], 3 * KB)
            ln_dve(dve, 2, OP_OUT)
            ff_dve(dve, 1)
            dve.wait_ge(S["acc_done"], 2 * (KB + KB * FG))
            ln_dve(dve, 3, None)
            for k in range(NTOK):
                n = tok_rows(k)
                dve.wait_ge(S["y_turned"], k + 1)
                if k >= 2:
                    dve.wait_ge(S[f"y_saved{k % 2}"], 16 * (k // 2))
                dve.tensor_copy(tmp[0:n, k % 2, 0:D].rearrange("p (a c) -> p a c", a=2),
                                ps[0:n, 2 * (k % 2):2 * (k % 2) + 2, :]).then_inc(S["y_kept"], 1)


def shape_constants():
    i = np.arange(P)
    col = np.arange(D)
    head = (i // DQ) % H
    new = np.arange(NS)
    low = -(2.0 ** 60)
    smask = np.full((P, DB // 2, NS), low, np.float32)
    for pair in range(DB // 2):
        own = (new[None, :] // DQ == 2 * pair + i[:, None] // 64) & (new[None, :] % DQ < i[:, None] % DQ)
        smask[:, pair, :][own] = 0.0
    return {
        "c_ident": np.eye(P, dtype=np.float32),
        "c_negtri": -(i[:, None] >= i[None, :]).astype(np.float32),
        "c_negones": -np.ones((P, P), np.float32),
        "c_avg": np.full((P, P), 1.0 / D, np.float32),
        "c_dmask": np.where(i[:, None] < i[None, :], 0.0, low).astype(np.float32),
        "c_mbd": (col[None, :] // HD == head[:, None]).astype(np.float32),
        "c_sel": ((i[:, None] // 64) * DQ + i[:, None] % DQ == np.arange(2 * DQ)[None, :]).astype(np.float32),
        "c_smask": smask,
    }


def by_feature(a):
    return np.ascontiguousarray(np.reshape(a, (-1, P)).T)


OUTS = {
    "y_p": (1, SEQ, D), "y_s": (DB, DQ, D), "new_k_p": (1, 1, SEQ, H, HD), "new_v_p": (1, 1, SEQ, H, HD),
    "new_conv_p": (1, 1, HIST, D), "new_k_s": (1, DB, DQ, H, HD), "new_v_s": (1, DB, DQ, H, HD),
    "new_conv_s": (1, DB, HIST, D),
}


def kernel(**inputs):
    import concourse.bacc as bacc
    from concourse.bass_utils import run_bass_kernel_spmd

    x = {k: np.asarray(v) for k, v in inputs.items()}
    arrays = {k: np.ascontiguousarray(x[k]) for k in (
        "x_prompt", "x_sample", "cache_k", "cache_v", "state_conv", "w_ff1_up", "w_ff1_down", "w_in",
        "w_proj_a", "w_proj_b", "w_out", "w_ff2_up", "w_ff2_down")}
    arrays["page_table"] = np.ascontiguousarray(x["page_table"].reshape(1, -1))
    arrays["norms"] = np.stack([by_feature(x[n]) for n in (
        "ln1_g", "ln1_b", "ln_conv_g", "ln_conv_b", "ln2_g", "ln2_b", "ln3_g", "ln3_b")], axis=1)
    arrays["gate_bias"] = by_feature(x["b_gate"])
    arrays["conv_bias"] = by_feature(x["b_dw"])
    arrays["taps"] = np.ascontiguousarray(x["w_dw"].reshape(CW, KB, P).transpose(2, 1, 0))
    arrays["b_heads"] = np.ascontiguousarray(np.broadcast_to(x["b_sb"].reshape(1, H), (P, H)))
    arrays["b_rows"] = np.ascontiguousarray(np.tile(np.repeat(x["b_sb"].reshape(H), DQ), 2).reshape(P, 1))
    arrays.update(shape_constants())

    nc = bacc.Bacc("TRN2", target_bir_lowering=False, num_devices=1)
    A = {k: nc.dram_tensor("in_" + k, a.shape, mybir.dt.from_np(a.dtype), kind="ExternalInput").ap()
         for k, a in arrays.items()}
    O = {k: nc.dram_tensor("out_" + k, s, F32, kind="ExternalOutput").ap() for k, s in OUTS.items()}
    build(nc, A, O)
    r = run_bass_kernel_spmd(nc, [{"in_" + k: a for k, a in arrays.items()}], core_ids=[0])
    return tuple(r.results[0]["out_" + k] for k in OUTS)
```

```python
from contextlib import ExitStack

import numpy as np

import concourse.bass as bass
import concourse.mybir as mybir
from concourse.alu_op_type import AluOpType as ALU

ACT = mybir.ActivationFunctionType
F32 = mybir.dt.float32
F32R = mybir.dt.float32r
BF16 = mybir.dt.bfloat16
I32 = mybir.dt.int32

P = 128
D = 1024
KB = D // P
SEQ = 1024
DB, DQ = 8, 4
NS = DB * DQ
T = SEQ + NS
CH = T // 3
H, HD = 16, 64
F = 2816
FT = F // P
FG = FT // 2
CW = 31
HIST = CW - 1
PAGES = 8
POOL = 80
PAST = PAGES * P
ALPHA = 2.0 ** 0.25
SCALE = HD ** -0.5
EPS = 1e-5
ZCAP = 30.0
KEYS = PAST + NS
NSTEP = 24

W_FF1, W_CONV, W_ATT, W_OUT, W_FF2 = 0, 66, 98, 122, 146
W_END = 212
W_OUT_B = W_OUT + KB

STEPS = [(c, kb, h) for c in range(2) for kb in range(4 * c + 3, -1, -1) for h in range(2)]


LAG_SUM, LAG_OUT = 3, 5

SEMS = [
    "a_done", "a_hi", "a_lo", "acc_done", "acc_init", "aux_in0", "aux_in1", "bias_set",
    "const_in", "conv_in0", "conv_in1", "conv_saved", "csig_done", "down_out", "e_done",
    "eps_set", "glu_done", "hist_in", "hist_kept", "hist_turned", "ident_in", "k_hi", "k_lo",
    "k_nat", "k_raw", "k_saved", "k_turned", "l_done", "ln_aff", "ln_cent", "ln_log", "ln_mean",
    "ln_rstd", "ln_scaled", "ln_sq", "ln_sqread", "ln_sum", "mask_set", "mix_out", "mix_tmp",
    "new_hi", "new_lo", "o_kept", "one_set", "op_hi", "op_lo", "op_lo_odd", "pad_set",
    "page_in0", "page_in1", "page_in2", "page_in3", "page_in4", "page_in5", "page_in6",
    "page_in7", "pk_hi", "pk_lo", "pk_turned", "prod_done", "prod_hi", "prod_lo", "pv_hi",
    "pv_lo", "pv_used", "q_hi", "q_lo", "qb_hi", "qb_lo", "run_done", "s_a", "s_capped",
    "s_chain", "s_exp", "s_ln", "s_log", "s_ready", "s_row", "s_zero", "sa_hi", "sa_lo",
    "sa_turned", "sconst_in", "side_prod", "side_sum", "siga_done", "siga_saved", "sigb_done",
    "sigb_saved", "silu_done", "so_kept", "so_mask", "so_out", "so_turned", "sp_ready",
    "state_saved", "sz_kept", "sz_out", "tail_kept", "tail_saved", "tail_turned", "tap_done",
    "tok_in0", "tok_in1", "tok_in2", "tok_in3", "tok_in4", "tok_in5", "tok_in6", "tok_in7",
    "tok_turned", "v_hi", "v_lo", "v_nat", "v_raw", "v_saved", "v_turned", "v_used", "w_high",
    "w_landed0", "w_landed1", "w_split", "w_used", "x1_saved", "y_kept", "y_saved0", "y_saved1",
    "y_saved2", "y_saved3", "y_turned", "z_capped", "z_ready",
]


def tri(ap):
    return ap.rearrange("p (c n) -> p c n", c=3)


def chain(step):
    c, kb, _ = step
    off = P * max(kb - 4 * c, 0)
    return off, (None if kb == 4 * c + 3 else P * max(kb + 1 - 4 * c, 0))


def run_ops(step):
    off, before = chain(step)
    if step[1] == 0:
        return []
    if before is None:
        return [(off, 512, False)]
    return ([(off, before, False)] if before > off else []) + [(before, 512, True)]


RUN_OPS = [len(run_ops(s)) for s in STEPS]
RUN_TOTAL = sum(RUN_OPS)
SIDE = 8
MAIN = CW - SIDE
SUMS = (7, 15, 22, 29)
TAPS = 4 + 3 * MAIN + SIDE + 1
HI_FF1, HI_CONV, HI_A, HI_B, HI_OUT, HI_FF2 = 9, 17, 25, 33, 41, 49
LO_FF1, LO_CONV, LO_A, LO_B, LO_OUT, LO_FF2 = 9, 13, 21, 29, 37, 41
HB = KB // 2


def build(nc, A, O):
    with ExitStack() as top:
        def sb(name, shape, dt=F32, ctx=top):
            return ctx.enter_context(nc.sbuf_tensor(name, shape, dt))

        def dram(name, shape):
            return nc.dram_tensor(name, shape, F32, kind="Internal").ap()

        sig_a_d = dram("sig_a_scratch", [KB, P, T])
        sig_b_d = dram("sig_b_scratch", [KB, P, T])
        x1_d = dram("x1_scratch", [KB, P, T])
        conv_d = dram("conv_scratch", [KB, P, T])

        ps = top.enter_context(nc.psum_tensor("ps", [P, 8, 512], F32))

        def pset(s):
            return ps[:, 3 * s:3 * s + 3, 0:CH]

        xh = sb("xh", [P, KB, T], F32R)
        xl = sb("xl", [P, KB, T], F32R)
        acc = sb("acc", [P, KB, T])
        wraw = sb("wraw", [P, 2, D])
        tmp = sb("tmp", [P, 4, T])
        ident = sb("ident", [P, P])
        identb = sb("identb", [P, P], BF16)
        negtri = sb("negtri", [P, P])
        negones = sb("negones", [P, P])
        avg = sb("avg", [P, P])
        dmask = sb("dmask", [P, P], BF16)
        lnp = sb("lnp", [P, 8, KB])
        bgate = sb("bgate", [P, 2 * KB])
        bdw = sb("bdw", [P, KB])
        wdw = sb("wdw", [P, KB, CW])
        bias_p = sb("bias_p", [P, H])
        bias_s = sb("bias_s", [P, 1])
        epsc = sb("epsc", [P, 1])
        one = sb("one", [P, 1])
        pt_sb = sb("pt_sb", [1, DB * PAGES], I32)

        with ExitStack() as ff1:
            wh1, wl1 = (sb(f"{n}1", [P, 4, D], F32R, ff1) for n in ("wh", "wl"))
            gh1, gl1 = (sb(f"{n}1", [P, 4, T], F32R, ff1) for n in ("gh", "gl"))
        with ExitStack() as start:
            sb("hole_w1", [P, 8 * D], F32, start)
            tok = sb("tok", [P, 8, D], F32, start)
        with ExitStack() as cv:
            whc, wlc = (sb(f"{n}c", [P, 4, D], F32R, cv) for n in ("wh", "wl"))
            glu = sb("glu", [P, SEQ + P], F32, cv)
            ext = sb("ext", [P, DB, HIST + DQ], F32, cv)
            cbuf = sb("cbuf", [P, T], F32, cv)
            csum = sb("csum", [P, T], F32, cv)
            side = sb("side", [P, SEQ], F32, cv)
            prod1 = sb("prod1", [P, SEQ], F32, cv)
            wm = sb("wm", [P, CW + 1], F32, cv)
            tail = sb("tail", [HIST + NS, D], F32, cv)
        with ExitStack() as keep:
            sb("hole_ff1", [P, 8 * (D + T)], F32, keep)
            hist = sb("hist", [P, KB, DB * HIST], F32, keep)
        with ExitStack() as at:
            wha, wla = (sb(f"{n}a", [P, 3, D], F32R, at) for n in ("wh", "wl"))
            qs = sb("qs", [P, KB, NS], F32, at)
            ks = sb("ks", [P, KB, NS], F32, at)
            qh, ql, kh, kl = (sb(n, [P, T], F32R, at) for n in ("qh", "ql", "kh", "kl"))
            nat = sb("nat", [P, 2, KB, P], F32, at)
            nat_s = sb("nat_s", [NS, 2, P], F32, at)
            vh, vl = (sb(n, [P, KB, P], F32R, at) for n in ("vh", "vl"))
            ah, al = (sb(n, [P, 3, 512], F32R, at) for n in ("ah", "al"))
            run = sb("run", [P, 2, 512], F32, at)
            bias_m = sb("bias_m", [P, 2], F32, at)
        with ExitStack() as sa:
            pages = sb("pages", [P, 6, D], F32, sa)
            sb("hole_qs", [P, KB, NS], F32, sa)
            sb("hole_ks", [P, KB, NS], F32, sa)
            qbh, qbl = (sb(n, [P, KB, P], F32R, sa) for n in ("qbh", "qbl"))
            ksh, ksl = (sb(n, [P, KB, NS], F32R, sa) for n in ("ksh", "ksl"))
            ath, atl = (sb(n, [P, KB + 1, P], F32R, sa) for n in ("ath", "atl"))
            vnh, vnl = (sb(n, [NS, D], F32R, sa) for n in ("vnh", "vnl"))
            vn_raw = sb("vn_raw", [NS, D], F32, sa)
            om = sb("om", [P, D], F32, sa)
            mbd = sb("mbd", [P, D], F32, sa)
            sel = sb("sel", [P, 2 * DQ], F32, sa)
            smask = sb("smask", [P, DB // 2, NS], F32, sa)
        with ExitStack() as ou:
            who, wlo = (sb(f"{n}o", [P, 4, D], F32R, ou) for n in ("wh", "wl"))
            gh2, gl2 = (sb(f"{n}2", [P, 4, T], F32R, ou) for n in ("gh", "gl"))
        WH = {W_OUT_B: (who, wlo), W_FF1: (wh1, wl1), W_CONV: (whc, wlc), W_ATT: (wha, wla), W_OUT: (who, wlo), W_FF2: (who, wlo)}
        GH = ((gh1, gl1), (gh2, gl2))

        up_w = [A[f"w_ff{f}_up"].rearrange("a (kb p) c -> p (a kb) c", p=P) for f in (1, 2)]
        down_w = [A[f"w_ff{f}_down"].rearrange("a f c -> (a f) c") for f in (1, 2)]
        in_w = A["w_in"].rearrange("a (kb p) c -> p (a kb) c", p=P)
        out_w = [A[n].rearrange("a (kb p) c -> p (a kb) c", p=P) for n in ("w_proj_a", "w_proj_b", "w_out")]
        page_rows = [A[n].rearrange("a n p h d -> (a n) p (h d)") for n in ("cache_k", "cache_v")]
        new_p = [O[n].rearrange("a b (kb p) h d -> p (a b kb) (h d)", p=P) for n in ("new_k_p", "new_v_p")]
        new_s = [O[n].rearrange("a b q h d -> (a b q) (h d)") for n in ("new_k_s", "new_v_s")]
        state_rows = A["state_conv"].rearrange("a b i c -> (a b i) c")

        CONSTS = [(negtri[:, :], "c_negtri"),
                  (negones[:, :], "c_negones"), (avg[:, :], "c_avg"), (tmp[:, 0, 0:P], "c_dmask"),
                  (lnp[:, :, :], "norms"), (bgate[:, :], "gate_bias"), (bdw[:, :], "conv_bias"),
                  (wdw[:, :, :], "taps"), (bias_p[:, :], "b_heads"), (bias_s[:, :], "b_rows"),
                  (pt_sb[:, :], "page_table")]

        S = {n: top.enter_context(nc.semaphore(n)) for n in SEMS}

        def load_tile(sp, i, n, src):
            if n >= 2:
                sp.wait_ge(S["w_split"], i + (n - 1))
            dst = wraw[:, n % 2, :]
            if len(src.shape) == 3:
                dst = dst.rearrange("p (kb c) -> p kb c", kb=KB)
            sp.dma_start(dst, src).then_inc(S[f"w_landed{n % 2}"], 16)

        def split_tile(pool, wh, wl, i, n, pos, used):
            pool.wait_ge(S[f"w_landed{n % 2}"], i * 8 + (n // 2 + 1) * 16)
            if used is not None:
                pool.wait_ge(S["w_used"], used)
            raw = wraw[:, n % 2, :]
            pool.tensor_tensor(wh[:, pos, :], raw, one[:, 0:1].to_broadcast([P, D]), ALU.mult).then_inc(S["w_high"], 1)
            pool.wait_ge(S["w_high"], i + (n + 1))
            pool.tensor_tensor(wl[:, pos, :], raw, wh[:, pos, :].bitcast(F32),
                               ALU.subtract).then_inc(S["w_split"], 1)

        def split_phase(pool, base, count, ring, norm_ops=None):
            wh, wl = WH[base]
            body = ring if ring % 2 == 0 else 2 * ring
            if base:
                pool.wait_ge(S["w_used"], base)
            for k in range(body):
                if norm_ops is not None and k == 2:
                    split_lo(pool, norm_ops, range(1, KB, 2), "op_lo_odd")
                split_tile(pool, wh, wl, 0, base + k, k % ring, base + k - ring + 1 if k >= ring else None)
            whole = (count - body) // body * body
            with pool.Fori(0, whole - body + 1, body) as i:
                for k in range(body):
                    split_tile(pool, wh, wl, i, base + body + k, k % ring, i + (base + body + k - ring + 1))
            for k in range(body + whole, count):
                split_tile(pool, wh, wl, 0, base + k, k % ring, base + k - ring + 1)

        def linear(pe, base, pos, s, sem, operand=None):
            wh, wl = WH[base]
            for kb in range(KB):
                if operand in ("conv", "ff2"):
                    if kb % 2:
                        pe.wait_ge(S["op_lo_odd"], (HB if operand == "ff2" else 0) + kb // 2 + 1)
                    else:
                        pe.wait_ge(S["op_lo"], (LO_FF2 if operand == "ff2" else LO_CONV) - HB + kb // 2 + 1)
                elif operand:
                    pe.wait_ge(S["op_lo"], {"a": LO_A, "b": LO_B, "out": LO_OUT}[operand] - KB + kb + 1)
                xh_, xl_ = (gh2, gl2) if base == W_OUT_B and kb < HB else (xh, xl)
                for n, (w, x) in enumerate(((wh, xh_), (wh, xl_), (wl, xh_))):
                    for c in range(3):
                        mm = pe.matmul(ps[:, 3 * s + c, 0:CH], w[:, pos, kb * P:(kb + 1) * P],
                                       x[:, kb, c * CH:(c + 1) * CH],
                                       start=(kb == 0 and n == 0), stop=(kb == KB - 1 and n == 2))
            mm.then_inc(sem, 1)

        def block_sum(L):
            return csum[:, :] if L == 1 else tmp[:, 2, :]

        def ln_sum_pool(pool, L, sem, before):
            buf = block_sum(L)
            for kb in range(1, KB):
                pool.wait_ge(S[sem], before + kb + 1)
                if kb > 1:
                    pool.wait_ge(S["ln_sum"], SUMS[L] - KB + kb)
                pool.tensor_tensor(buf, acc[:, 0, :] if kb == 1 else buf, acc[:, kb, :], ALU.add) \
                    .then_inc(S["ln_sum"], 1)

        def ln_pe(pe, L):
            pe.wait_ge(S["ln_sum"], SUMS[L])
            for c in range(3):
                mm = pe.matmul(ps[:, c, 0:CH], avg[:, :], block_sum(L)[:, c * CH:(c + 1) * CH],
                               start=True, stop=True)
            mm.then_inc(S["ln_mean"], 1)
            for kb in range(KB):
                pe.wait_ge(S["ln_sq"], KB * L + kb + 1)
                for c in range(3):
                    mm = pe.matmul(ps[:, 3 + c, 0:CH], avg[:, :], tmp[:, kb % 2, c * CH:(c + 1) * CH],
                                   start=(kb == 0), stop=(kb == KB - 1))
                mm.then_inc(S["ln_sqread"], 1)

        def ln_dve(dve, L, ops):
            dve.wait_ge(S["ln_mean"], L + 1)
            for kb in range(KB):
                dve.tensor_tensor(tri(acc[:, kb, :]), tri(acc[:, kb, :]), pset(0), ALU.subtract) \
                    .then_inc(S["ln_cent"], 1)
            dve.wait_ge(S["ln_rstd"], L + 1)
            dve.wait_ge(S["ln_cent"], KB * (L + 1))
            for kb in range(KB):
                dve.scalar_tensor_tensor(out=acc[:, kb, :], in0=acc[:, kb, :], scalar=lnp[:, 2 * L, kb:kb + 1],
                                         in1=tmp[:, 3, :], op0=ALU.mult, op1=ALU.mult).then_inc(S["ln_scaled"], 1)
            if ops is not None:
                split_lo(dve, ops, range(0, KB, 2), "op_lo")

        def ln_act(act, L, func, ops):
            nc.scalar.preload_act_table_set("natural_log_exp_and_others")
            for kb in range(KB):
                act.wait_ge(S["ln_cent"], KB * L + kb + 1)
                if kb >= 2:
                    act.wait_ge(S["ln_sqread"], KB * L + kb - 1)
                act.activation(tmp[:, kb % 2, :], acc[:, kb, :], ACT.Square).then_inc(S["ln_sq"], 1)
            act.wait_ge(S["ln_sqread"], KB * (L + 1))
            act.activation(tri(tmp[:, 2, :]), pset(1), ACT.Ln, bias=epsc[:, 0:1]).then_inc(S["ln_log"], 1)
            act.wait_ge(S["ln_log"], L + 1)
            act.activation(tmp[:, 3, :], tmp[:, 2, :], ACT.Exp, scale=-0.5).then_inc(S["ln_rstd"], 1)
            for kb in range(KB + 1):
                if kb < KB:
                    act.wait_ge(S["ln_scaled"], KB * L + kb + 1)
                    act.activation(acc[:, kb, :], acc[:, kb, :], func, bias=lnp[:, 2 * L + 1, kb:kb + 1]).then_inc(S["ln_aff"], 1)
                if kb and ops is not None:
                    act.wait_ge(S["ln_aff"], KB * L + kb)
                    act.copy(xh[:, kb - 1, :], acc[:, kb - 1, :]).then_inc(S["op_hi"], 1)

        def split_lo(eng, ops, blocks, sem):
            for kb in blocks:
                eng.wait_ge(S["op_hi"], ops + kb + 1)
                eng.tensor_tensor(xl[:, kb, :], acc[:, kb, :], xh[:, kb, :].bitcast(F32),
                                  ALU.subtract).then_inc(S[sem], 1)

        def ff_sp(sp, f):
            base = (W_FF1, W_FF2)[f]
            for k in range(4):
                col = (k // 2) * P + (k % 2) * F
                load_tile(sp, 0, base + k, up_w[f][:, :, col:col + P])
            with sp.Fori(0, FG - 1) as g:
                for k in range(4):
                    load_tile(sp, g * 6, base + 4 + k,
                              up_w[f][:, :, bass.ds(g * (2 * P) + (2 * P + (k // 2) * P + (k % 2) * F), P)])
                for k in range(2):
                    load_tile(sp, g * 6, base + 8 + k, down_w[f][bass.ds(g * (2 * P) + k * P, P), :])
            for k in range(2):
                load_tile(sp, 0, base + 64 + k, down_w[f][(FT - 2 + k) * P:(FT - 1 + k) * P, :])

        def ff_pe(pe, f):
            base = (W_FF1, W_FF2)[f]
            wh, wl = WH[base]
            gh, gl = GH[f]
            t0, y0 = FT * f, KB + (KB * FG + KB) * f
            if f == 0:
                pe.wait_ge(S["op_lo"], LO_FF1)

            def up(g, gc, n, nc_, r):
                for t in range(2):
                    pe.wait_ge(S["w_split"], n + (nc_ + 2 * t + 1))
                    pe.wait_ge(S["silu_done"], g * 2 + (2 * gc + t0 + t))
                    if t == 0 and gc > 0:
                        pe.wait_ge(S["acc_done"], g * 8 + (8 * gc + y0 - 9))
                    first = f == 1 and gc == 0 and t == 0
                    linear(pe, base, (r + 2 * t) % 4, 0, S["w_used"], "ff2" if first else None)
                    pe.wait_ge(S["w_split"], n + (nc_ + 2 * t + 2))
                    pe.wait_ge(S["prod_done"], g * 2 + (2 * gc + t0 + t))
                    if t == 0 and gc > 0:
                        pe.wait_ge(S["acc_done"], g * 8 + (8 * gc + y0 - 8))
                    linear(pe, base, (r + 2 * t + 1) % 4, 1, S["w_used"])

            def down(g, gc, n, nc_, r, par, last=False):
                pe.wait_ge(S["w_split"], n + (nc_ + 2))
                pe.wait_ge(S["prod_lo"], g * 2 + (2 * gc + t0 + 2))
                for d in range(KB):
                    if d < 2:
                        pe.wait_ge(S[("silu_done", "prod_done")[d]],
                                   g * 2 + (2 * gc + t0 + (2 if last else 4)))
                        if last:
                            pe.wait_ge(S["acc_done"], g * 8 + (8 * gc + y0 + d - 1))
                    else:
                        pe.wait_ge(S["acc_done"], g * 8 + (8 * gc + y0 + d - 1))
                    for c in range(3):
                        for k in range(2):
                            for i, (w, x) in enumerate(((wh, gh), (wh, gl), (wl, gh))):
                                mm = pe.matmul(ps[:, 3 * (d % 2) + c, 0:CH], w[:, (r + k) % 4, d * P:(d + 1) * P],
                                               x[:, 2 * par + k, c * CH:(c + 1) * CH],
                                               start=(k == 0 and i == 0), stop=(k == 1 and i == 2))
                    mm.then_inc(S["down_out"], 1) if d < KB - 1 else mm.then_inc(S["w_used"], 2)

            up(0, 0, 0, base, 0)
            with pe.Fori(0, FG - 2, 2) as g:
                for u in range(2):
                    up(g, u + 1, g * 6, base + 4 + 6 * u, 2 * u)
                    down(g, u, g * 6, base + 8 + 6 * u, 2 * u, u)
            down(0, FG - 1, 0, base + 64, 0, 0, last=True)

        def ff_act(act, f):
            base = (W_FF1, W_FF2)[f]
            gh = GH[f][0]
            t0 = FT * f

            def hidden(g, gc, n, nc_, par):
                for t in range(2):
                    act.wait_ge(S["w_used"], n + (nc_ + 2 * t + 1))
                    if gc > 0:
                        act.wait_ge(S["prod_done"], g * 2 + (2 * gc + t0 + t - 1))
                    act.activation(tri(tmp[:, t, :]), pset(0), ACT.Silu).then_inc(S["silu_done"], 1)
                    act.wait_ge(S["prod_done"], g * 2 + (2 * gc + t0 + t + 1))
                    if gc > 0:
                        act.wait_ge(S["w_used"], n + nc_)
                    act.copy(gh[:, 2 * par + t, :], tmp[:, 2 + t, :]).then_inc(S["prod_hi"], 1)

            hidden(0, 0, 0, base, 0)
            with act.Fori(0, FG - 2, 2) as g:
                for u in range(2):
                    hidden(g, u + 1, g * 6, base + 4 + 6 * u, 1 - u)

        def ff_dve(dve, f):
            base = (W_FF1, W_FF2)[f]
            gh, gl = GH[f]
            t0, y0, d0 = FT * f, KB + (KB * FG + KB) * f, (KB - 1) * FG * f

            def hidden(g, gc, n, nc_, par):
                for t in range(2):
                    dve.wait_ge(S["w_used"], n + (nc_ + 2 * t + 2))
                    dve.wait_ge(S["silu_done"], g * 2 + (2 * gc + t0 + t + 1))
                    if gc > 0:
                        dve.wait_ge(S["prod_hi"], g * 2 + (2 * gc + t0 + t - 1))
                    dve.scalar_tensor_tensor(out=tri(tmp[:, 2 + t, :]), in0=tri(tmp[:, t, :]), scalar=0.5,
                                             in1=pset(1), op0=ALU.mult, op1=ALU.mult) \
                        .then_inc(S["prod_done"], 1)
                    dve.wait_ge(S["prod_hi"], g * 2 + (2 * gc + t0 + t + 1))
                    dve.tensor_tensor(gl[:, 2 * par + t, :], tmp[:, 2 + t, :],
                                      gh[:, 2 * par + t, :].bitcast(F32), ALU.subtract) \
                        .then_inc(S["prod_lo"], 1)

            def add(g, gc, n):
                for d in range(KB):
                    if d < KB - 1:
                        dve.wait_ge(S["down_out"], g * 7 + (7 * gc + d0 + d + 1))
                    else:
                        dve.wait_ge(S["w_used"], n)
                    dve.wait_ge(S["acc_done"], g * 8 + (8 * gc + y0 + d - 7))
                    dve.tensor_tensor(tri(acc[:, d, :]), tri(acc[:, d, :]), pset(d % 2), ALU.add) \
                        .then_inc(S["acc_done"], 1)

            hidden(0, 0, 0, base, 0)
            with dve.Fori(0, FG - 2, 2) as g:
                for u in range(2):
                    hidden(g, u + 1, g * 6, base + 4 + 6 * u, 1 - u)
                    add(g, u, g * 6 + (base + 10 + 6 * u))
            add(0, FG - 1, base + 66)

        def cv_sp(sp):
            with sp.Fori(0, KB) as m:
                for k, col in enumerate((3 * D, 4 * D, 5 * D, 6 * D)):
                    load_tile(sp, m * 4, W_CONV + k, in_w[:, :, bass.ds(m * P + col, P)])

        def side_prod(j):
            return (tmp[:, 3, 0:SEQ], prod1[:, :])[j % 2]

        def cv_pool(pool):
            for k in range(4):
                if k == 2:
                    split_lo(pool, HI_FF1, range(1, KB, 2), "op_lo_odd")
                split_tile(pool, whc, wlc, 0, W_CONV + k, k, None)
            with pool.Fori(0, KB - 1) as m:
                for k in range(4):
                    split_tile(pool, whc, wlc, m * 4, W_CONV + 4 + k, k, m * 4 + (W_CONV + k + 1))
                    side_sums(pool, m, 0, ((), (1, 2, 3), (4, 5, 6, 7), ())[k])
            side_sums(pool, 0, KB - 1, range(1, SIDE))

        def side_sums(pool, m, dm, taps):
            for j in taps:
                pool.wait_ge(S["side_prod"], m * SIDE + (dm * SIDE + j + 1))
                if j == 1:
                    pool.wait_ge(S["tap_done"], m * TAPS + dm * TAPS)
                else:
                    pool.wait_ge(S["side_sum"], m * (SIDE - 1) + (dm * (SIDE - 1) + j - 1))
                pool.tensor_tensor(side[:, :], side_prod(0) if j == 1 else side[:, :], side_prod(j), ALU.add) \
                    .then_inc(S["side_sum"], 1)

        def side_products(act, m, taps):
            for j in taps:
                if j >= 2:
                    act.wait_ge(S["side_sum"], m * (SIDE - 1) + max(j - 2, 1))
                else:
                    act.wait_ge(S["side_sum"], m * (SIDE - 1))
                act.activation(side_prod(j), glu[:, MAIN + j:MAIN + j + SEQ], ACT.Identity,
                               scale=wm[:, MAIN + j:MAIN + j + 1]).then_inc(S["side_prod"], 1)

        def hist_pe(pe):
            pe.wait_ge(S["hist_in"], 16)
            n = DB * HIST // 2
            for m in range(KB):
                if m >= 2:
                    pe.wait_ge(S["hist_kept"], m - 1)
                for j in range(2):
                    mm = pe.transpose(ps[:, 6 + m % 2, j * n:(j + 1) * n], tmp[0:n, 2 + j, m * P:(m + 1) * P],
                                      ident[0:n, 0:n])
                mm.then_inc(S["hist_turned"], 1)

        def cv_pe(pe):
            pe.wait_ge(S["hist_kept"], KB)
            with pe.Fori(0, KB) as m:
                for k, (sem, add) in enumerate((("siga_done", 0), ("sigb_done", 0), ("glu_done", 1), ("csig_done", 1))):
                    pe.wait_ge(S["w_split"], m * 4 + (W_CONV + k + 1))
                    pe.wait_ge(S[sem], m + add)
                    linear(pe, W_CONV, k, k % 2, S["w_used"], "conv" if k == 0 else None)
                pe.wait_ge(S["glu_done"], m + 1)
                pe.wait_ge(S["tail_kept"], m)
                pe.transpose(ps[:, 6, 0:P], glu[:, SEQ:SEQ + P], ident[:, :]).then_inc(S["tail_turned"], 1)

        def cv_act(act):
            with act.Fori(0, KB) as m:
                act.wait_ge(S["w_used"], m * 4 + (W_CONV + 2))
                act.wait_ge(S["glu_done"], m)
                act.activation(tri(tmp[:, 0, :]), pset(1), ACT.Sigmoid).then_inc(S["csig_done"], 1)
                act.wait_ge(S["glu_done"], m + 1)
                side_products(act, m, range(0, 4))
                for k, (sem, dst) in enumerate((("siga", sig_a_d), ("sigb", sig_b_d))):
                    act.wait_ge(S["w_used"], m * 4 + (W_CONV + 3 + k))
                    act.wait_ge(S[sem + "_saved"], m * 16)
                    act.activation(tri(tmp[:, 1 + k, :]), pset(k), ACT.Sigmoid,
                                   bias=bgate[:, bass.ds(m + k * KB, 1)]).then_inc(S[sem + "_done"], 1)
                    act.wait_ge(S[sem + "_done"], m + 1)
                    act.dma_start(dst[bass.ds(m, 1), :, :].rearrange("a p t -> (a p) t"), tmp[:, 1 + k, :]) \
                        .then_inc(S[sem + "_saved"], 16)
                    if k == 0:
                        side_products(act, m, range(4, SIDE))
                act.wait_ge(S["tail_turned"], m + 1)
                act.copy(tail[:, bass.ds(m * P, P)], ps[0:HIST + NS, 6, 0:P]).then_inc(S["tail_kept"], 1)
            act.wait_ge(S["tail_kept"], KB)
            act.dma_start(O["new_conv_p"].rearrange("a b i c -> (a b i) c"), tail[0:HIST, :]) \
                .then_inc(S["tail_saved"], 16)
            for b in range(DB):
                act.dma_start(O["new_conv_s"][0, b, HIST - DQ:HIST, :], tail[HIST + DQ * b:HIST + DQ * (b + 1), :]) \
                    .then_inc(S["tail_saved"], 16)

        def cv_dve(dve):
            dve.wait_ge(S["w_used"], W_CONV)
            dve.memset(glu[:, 0:HIST], 0.0).then_inc(S["pad_set"], 1)
            dve.memset(glu[:, HIST + T:], 0.0).then_inc(S["pad_set"], 1)
            dve.memset(csum[:, :], 0.0).then_inc(S["pad_set"], 1)

        def hist_dve(dve):
            for m in range(KB):
                dve.wait_ge(S["hist_turned"], m + 1)
                dve.tensor_copy(hist[:, m, :], ps[:, 6 + m % 2, 0:DB * HIST]).then_inc(S["hist_kept"], 1)

        def tap_place(j, q):
            return 4 + (3 * j + q + 1 if j < MAIN else 3 * MAIN + j - MAIN + 1)

        def cv_dve_main(dve):
            dve.wait_ge(S["x1_saved"], 16 * KB)
            dve.wait_ge(S["hist_kept"], KB)
            dve.wait_ge(S["pad_set"], 3)
            with dve.Fori(0, KB) as m:
                dve.wait_ge(S["tap_done"], m * TAPS)
                dve.tensor_copy(wm[:, 0:CW], wdw[:, bass.ds(m, 1), :].rearrange("p a w -> p (a w)")) \
                    .then_inc(S["tap_done"], 1)
                dve.tensor_copy(wm[:, CW:CW + 1], bdw[:, bass.ds(m, 1)]).then_inc(S["tap_done"], 1)
                dve.tensor_copy(ext[:, :, 0:HIST], hist[:, bass.ds(m, 1), :].rearrange("p a (b i) -> p (a b) i", b=DB)) \
                    .then_inc(S["tap_done"], 1)
                dve.wait_ge(S["w_used"], m * 4 + (W_CONV + 1))
                dve.wait_ge(S["csig_done"], m + 1)
                dve.wait_ge(S["tail_turned"], m)
                dve.wait_ge(S["side_prod"], m * SIDE)
                dve.tensor_tensor(tri(glu[:, HIST:HIST + T]), tri(tmp[:, 0, :]), pset(0), ALU.mult) \
                    .then_inc(S["glu_done"], 1)
                dve.wait_ge(S["glu_done"], m + 1)
                dve.tensor_copy(ext[:, :, HIST:HIST + DQ],
                                glu[:, HIST + SEQ:HIST + T].rearrange("p (b q) -> p b q", b=DB)) \
                    .then_inc(S["tap_done"], 1)
                half = SEQ // 2
                for j in range(CW):
                    for q in range(3) if j < MAIN else (2,):
                        dve.wait_ge(S["tap_done"], m * TAPS + (tap_place(j - 1, q) if j else 4))
                        if q < 2:
                            src = glu[:, q * half + j:q * half + j + half]
                            old = cbuf[:, q * half:(q + 1) * half]
                        else:
                            src = ext[:, :, j:j + DQ]
                            old = cbuf[:, SEQ:T].rearrange("p (b q) -> p b q", b=DB)
                            new = acc[:, bass.ds(m, 1), SEQ:T].rearrange("p a (b q) -> p (a b) q", b=DB)
                        dst = new if q == 2 and j == CW - 1 else old
                        if j == 0:
                            dve.tensor_scalar(dst, src, wm[:, 0:1], wm[:, CW:CW + 1], ALU.mult, ALU.add) \
                                .then_inc(S["tap_done"], 1)
                        else:
                            dve.scalar_tensor_tensor(out=dst, in0=src, scalar=wm[:, j:j + 1], in1=old,
                                                     op0=ALU.mult, op1=ALU.add).then_inc(S["tap_done"], 1)
                dve.wait_ge(S["tap_done"], m * TAPS + tap_place(MAIN - 1, 1))
                dve.wait_ge(S["side_sum"], m * (SIDE - 1) + (SIDE - 1))
                dve.tensor_tensor(acc[:, bass.ds(m, 1), 0:SEQ].rearrange("p a t -> p (a t)"), cbuf[:, 0:SEQ],
                                  side[:, :], ALU.add).then_inc(S["tap_done"], 1)
                dve.wait_ge(S["tap_done"], m * TAPS + TAPS)
                dve.wait_ge(S["ln_sum"], m + SUMS[0])
                dve.tensor_tensor(csum[:, :], csum[:, :], acc[:, bass.ds(m, 1), :].rearrange("p a t -> p (a t)"),
                                  ALU.add).then_inc(S["ln_sum"], 1)

        def at_sp(sp):
            with sp.Fori(0, KB - 1, 2) as m:
                for u in range(2):
                    for k in range(3):
                        load_tile(sp, m * 3, W_ATT + 3 * u + k, in_w[:, :, bass.ds(m * P + (u * P + k * D), P)])

        k_t, v_t = tmp[:, 0, :], tmp[:, 1, :]

        def zbank(i):
            return i % 6

        def at_linear(pe, m, t, s, c):
            for kb in range(KB):
                for n, (w, x) in enumerate(((wha, xh), (wha, xl), (wla, xh))):
                    mm = pe.matmul(ps[:, 3 * s + c, 0:CH], w[:, t % 3, kb * P:(kb + 1) * P],
                                   x[:, kb, c * CH:(c + 1) * CH],
                                   start=(kb == 0 and n == 0), stop=(kb == KB - 1 and n == 2))
            if c == 2:
                mm.then_inc(S["w_used"], 1)

        def at_pe(pe):
            pe.wait_ge(S["ln_cent"], 2 * KB)
            pe.wait_ge(S["ln_log"], 2)
            pe.wait_ge(S["ln_cent"], 2 * KB)
            pe.wait_ge(S["ln_log"], 2)
            pe.wait_ge(S["w_split"], W_ATT + 1)
            for c in range(3):
                at_linear(pe, 0, 0, 0, c)
            with pe.Fori(0, KB - 1) as m:
                at_pair_pe(pe, m, 0, True)
            at_pair_pe(pe, 0, KB - 1, False)

        def at_pair_pe(pe, m, dm, more):
            def count(each, plus):
                return m * each + (dm * each + plus)

            pe.wait_ge(S["a_done"], count(NSTEP, 0))
            pe.wait_ge(S["w_split"], count(3, W_ATT + 2))
            for c in range(3):
                at_linear(pe, m, 1, 1, c)
            pe.wait_ge(S["w_split"], count(3, W_ATT + 3))
            pe.wait_ge(S["q_hi"], count(1, 1))
            pe.wait_ge(S["q_lo"], count(1, 1))
            for c in range(3):
                at_linear(pe, m, 2, 0, c)
            pe.wait_ge(S["k_raw"], count(1, 1))
            pe.wait_ge(S["k_lo"], count(1, 1))
            for kb in range(KB):
                pe.transpose(ps[:, 3 + kb // 4, (kb % 4) * P:(kb % 4 + 1) * P], k_t[:, kb * P:(kb + 1) * P], ident[:, :])
            pe.transpose(ps[0:NS, 5, 0:P], k_t[:, SEQ:T], ident[:, :]).then_inc(S["k_turned"], 1)
            for i in range(NSTEP + LAG_OUT):
                if i < NSTEP:
                    c, kb, h = STEPS[i]
                    off, _ = chain(STEPS[i])
                    out = ps[:, zbank(i), off:512]
                    if i == 0:
                        pe.wait_ge(S["v_raw"], count(1, 1))
                    if i == 2:
                        pe.wait_ge(S["o_kept"], count(4, 0))
                        pe.wait_ge(S["k_nat"], count(2, 2))
                        for t in range(KB):
                            pe.transpose(ps[:, 6 + t // 4, (t % 4) * P:(t % 4 + 1) * P],
                                         v_t[:, t * P:(t + 1) * P], ident[:, :])
                        pe.transpose(ps[0:NS, 5, 0:P], v_t[:, SEQ:T], ident[:, :]).then_inc(S["v_turned"], 1)
                    if i == 5:
                        pe.wait_ge(S["v_nat"], count(2, 2))
                    if i >= 6:
                        pe.wait_ge(S["a_done"], count(NSTEP, i - 5))
                    rows = slice(HD * h, HD * (h + 1))
                    for n, (a, b) in enumerate(((kh, qh), (kh, ql), (kl, qh))):
                        mm = pe.matmul(out, a[rows, kb * P:(kb + 1) * P], b[rows, 512 * c + off:512 * (c + 1)],
                                       start=(n == 0), stop=False, skip_group_check=True)
                    if kb >= 4 * c:
                        mm = pe.matmul(ps[:, zbank(i), off:off + P], identb[:, :], dmask[:, :],
                                       start=False, stop=False, skip_group_check=True)
                    mm.then_inc(S["z_ready"], 1)
                j = i - LAG_SUM
                if 0 <= j < NSTEP:
                    off, before = chain(STEPS[j])
                    h = STEPS[j][2]
                    pe.wait_ge(S["sp_ready"], count(NSTEP, j + 1))
                    if before is not None:
                        pe.wait_ge(S["run_done"], count(RUN_TOTAL, sum(RUN_OPS[:j - 1])))
                        pe.matmul(ps[:, zbank(j), before:512], negones[:, :], run[:, h, before:512],
                                  start=False, stop=False, skip_group_check=True)
                    pe.matmul(ps[:, zbank(j), off:512], negtri[:, :], sp_buf(j)[:, off:512],
                              start=False, stop=True, skip_group_check=True).then_inc(S["s_ready"], 1)
                if more and NSTEP <= i < NSTEP + 3:
                    c = i - NSTEP
                    pe.wait_ge(S["a_done"], count(NSTEP, NSTEP - 5 + c))
                    if c == 0:
                        pe.wait_ge(S["w_split"], count(3, W_ATT + 4))
                    at_linear(pe, m, 3, 0, c)
                j = i - LAG_OUT
                if 0 <= j < NSTEP:
                    c, kb, h = STEPS[j]
                    off, before = chain(STEPS[j])
                    if j == 0:
                        pe.wait_ge(S["v_lo"], count(1, 1))
                    if before is None:
                        pe.wait_ge(S["o_kept"], count(4, 2 * c))
                    pe.wait_ge(S["a_lo"], count(NSTEP, j + 1))
                    for n, (a, b) in enumerate(((vh, ah), (vh, al), (vl, ah))):
                        mm = pe.matmul(ps[:, 6 + h, off:512], a[:, kb, :], b[:, j % 3, off:512],
                                       start=(before is None and n == 0), stop=(kb == 0 and n == 2),
                                       skip_group_check=True)
                    mm.then_inc(S["v_used"], 1)

        def e_buf(i):
            return tmp[:, :, :].rearrange("p a t -> p (a t)")[:, (i % 5) * 512:(i % 5 + 1) * 512]

        def sp_buf(i):
            return tmp[:, :, :].rearrange("p a t -> p (a t)")[:, (5 + i % 3) * 512:(6 + i % 3) * 512]

        def token_major(act, m, n):
            turned, kept, saved = (("k_turned", "k_nat", "k_saved"), ("v_turned", "v_nat", "v_saved"))[n]
            bank = 3 + 3 * n
            act.wait_ge(S[turned], m + 1)
            act.wait_ge(S[saved], m * 32)
            if n:
                act.wait_ge(S["v_lo"], m)
            act.copy(nat[:, n, :, :], ps[:, bank:bank + 2, :].rearrange("p a (b c) -> p (a b) c", b=4)) \
                .then_inc(S[kept], 1)
            act.copy(nat_s[:, n, :], ps[0:NS, 5, 0:P]).then_inc(S[kept], 1)
            act.wait_ge(S[kept], m * 2 + 2)
            act.dma_start(new_p[n][:, :, bass.ds(m * P, P)], nat[:, n, :, :]).then_inc(S[saved], 16)
            act.dma_start(new_s[n][:, bass.ds(m * P, P)], nat_s[:, n, :]).then_inc(S[saved], 16)

        def at_act(act):
            act.wait_ge(S["tail_saved"], 16 * (DB + 1))
            act.wait_ge(S["conv_saved"], 16 * KB)
            nc.scalar.preload_act_table_set("natural_log_exp_and_others")
            with act.Fori(0, KB) as m:
                act.wait_ge(S["w_used"], m * 3 + (W_ATT + 1))
                act.activation(tri(qh[:, :]), pset(0), ACT.Copy, scale=SCALE).then_inc(S["q_hi"], 1)
                act.wait_ge(S["w_used"], m * 3 + (W_ATT + 2))
                act.copy(tri(kh[:, :]), pset(1)).then_inc(S["k_hi"], 1)
                act.wait_ge(S["a_lo"], m * NSTEP)
                act.copy(tri(k_t), pset(1)).then_inc(S["k_raw"], 1)
                act.wait_ge(S["w_used"], m * 3 + (W_ATT + 3))
                act.copy(tri(v_t), pset(0)).then_inc(S["v_raw"], 1)
                token_major(act, m, 0)
                for i in range(NSTEP + LAG_OUT):
                    if i == 2:
                        token_major(act, m, 1)
                        act.copy(vh[:, :, :], nat[:, 1, :, :]).then_inc(S["v_hi"], 1)
                    if i < NSTEP:
                        off, _ = chain(STEPS[i])
                        e = e_buf(i)[:, off:512]
                        act.wait_ge(S["z_capped"], m * NSTEP + (i + 1))
                        act.activation(e, e, ACT.Exp).then_inc(S["e_done"], 1)
                        act.wait_ge(S["e_done"], m * NSTEP + (i + 1))
                        act.activation(e, e, ACT.Ln, bias=1.0).then_inc(S["l_done"], 1)
                    if i in (8 + LAG_OUT, NSTEP + LAG_OUT - 1):
                        c = 0 if i < NSTEP else 1
                        act.wait_ge(S["v_used"], m * NSTEP + (8 if c == 0 else NSTEP))
                        for h in range(2):
                            rows = slice(HD * h, HD * (h + 1))
                            act.copy(acc[rows, bass.ds(m, 1), 512 * c:512 * (c + 1)].rearrange("p a t -> p (a t)"),
                                     ps[rows, 6 + h, :]).then_inc(S["o_kept"], 1)
                    j = i - LAG_SUM
                    if 0 <= j < NSTEP:
                        off, _ = chain(STEPS[j])
                        h = STEPS[j][2]
                        act.wait_ge(S["s_ready"], m * NSTEP + (j + 1))
                        act.activation(e_buf(j)[:, off:512], ps[:, zbank(j), off:512], ACT.Exp,
                                       bias=bias_m[:, h:h + 1]).then_inc(S["a_done"], 1)
                        act.wait_ge(S["a_done"], m * NSTEP + (j + 1))
                        if j >= 3:
                            act.wait_ge(S["v_used"], m * NSTEP + (j - 2))
                        act.copy(ah[:, j % 3, off:512], e_buf(j)[:, off:512]).then_inc(S["a_hi"], 1)

        def at_dve(dve):
            with dve.Fori(0, KB) as m:
                dve.wait_ge(S["a_done"], m * NSTEP)
                dve.wait_ge(S["tail_saved"], 16 * (DB + 1))
                dve.tensor_copy(bias_m[:, :], bias_p[:, bass.ds(m * 2, 2)]).then_inc(S["bias_set"], 1)
                dve.wait_ge(S["q_hi"], m + 1)
                dve.tensor_scalar(qs[:, bass.ds(m, 1), :].rearrange("p a t -> p (a t)"), ps[:, 2, CH - NS:CH],
                                  SCALE, None, ALU.mult).then_inc(S["s_row"], 1)
                dve.scalar_tensor_tensor(out=tri(ql[:, :]), in0=pset(0), scalar=SCALE,
                                         in1=tri(qh[:, :].bitcast(F32)), op0=ALU.mult, op1=ALU.subtract) \
                    .then_inc(S["q_lo"], 1)
                dve.wait_ge(S["k_raw"], m + 1)
                dve.tensor_copy(ks[:, bass.ds(m, 1), :].rearrange("p a t -> p (a t)"), ps[:, 5, CH - NS:CH]) \
                    .then_inc(S["s_row"], 1)
                dve.tensor_tensor(tri(kl[:, :]), pset(1), tri(kh[:, :].bitcast(F32)), ALU.subtract) \
                    .then_inc(S["k_lo"], 1)
                dve.wait_ge(S["bias_set"], m + 1)
                for i in range(NSTEP + LAG_OUT):
                    if i == 4:
                        dve.wait_ge(S["v_hi"], m + 1)
                        dve.tensor_tensor(vl[:, :, :], nat[:, 1, :, :], vh[:, :, :].bitcast(F32), ALU.subtract) \
                            .then_inc(S["v_lo"], 1)
                    if i < NSTEP:
                        off, _ = chain(STEPS[i])
                        h = STEPS[i][2]
                        dve.wait_ge(S["z_ready"], m * NSTEP + (i + 1))
                        if i >= 5:
                            dve.wait_ge(S["a_hi"], m * NSTEP + (i - 4))
                            dve.wait_ge(S["a_lo"], m * NSTEP + (i - 4))
                        dve.tensor_scalar(e_buf(i)[:, off:512], ps[:, zbank(i), off:512], bias_m[:, h:h + 1],
                                          ZCAP, ALU.add, ALU.min).then_inc(S["z_capped"], 1)
                    j = i - LAG_SUM - 1
                    if 0 <= j < NSTEP and run_ops(STEPS[j]):
                        h = STEPS[j][2]
                        dve.wait_ge(S["s_ready"], m * NSTEP + (j + 1))
                        dve.wait_ge(S["run_done"], m * RUN_TOTAL + sum(RUN_OPS[:j]))
                        for lo, hi, adds in run_ops(STEPS[j]):
                            s = sp_buf(j)[:, lo:hi]
                            r = run[:, h, lo:hi]
                            ins = dve.tensor_tensor(r, r, s, ALU.add) if adds else dve.tensor_copy(r, s)
                            ins.then_inc(S["run_done"], 1)
                    j = i - 1
                    if 0 <= j < NSTEP:
                        off, _ = chain(STEPS[j])
                        h = STEPS[j][2]
                        dve.wait_ge(S["l_done"], m * NSTEP + (j + 1))
                        if j >= 3:
                            dve.wait_ge(S["s_ready"], m * NSTEP + (j - 2))
                            dve.wait_ge(S["run_done"], m * RUN_TOTAL + sum(RUN_OPS[:j - 2]))
                        dve.scalar_tensor_tensor(out=sp_buf(j)[:, off:512], in0=ps[:, zbank(j), off:512],
                                                 scalar=bias_m[:, h:h + 1], in1=e_buf(j)[:, off:512],
                                                 op0=ALU.add, op1=ALU.max).then_inc(S["sp_ready"], 1)
                    j = i - LAG_SUM - 1
                    if 0 <= j < NSTEP:
                        off, _ = chain(STEPS[j])
                        dve.wait_ge(S["a_hi"], m * NSTEP + (j + 1))
                        if j >= 3:
                            dve.wait_ge(S["v_used"], m * NSTEP + (j - 2))
                        dve.tensor_tensor(al[:, j % 3, off:512], e_buf(j)[:, off:512],
                                          ah[:, j % 3, off:512].bitcast(F32), ALU.subtract) \
                            .then_inc(S["a_lo"], 1)

        NP = 2 * PAGES
        GCOLS = KB * 2 * P

        def page_slot(k):
            return wraw[:, k % 8, :] if k % 8 < 2 else pages[:, k % 8 - 2, :]

        def flat(t):
            return t[:, :, :].rearrange("p a t -> p (a t)")

        def kt_group(t, g):
            return flat(t)[:, (g % 2) * GCOLS:(g % 2 + 1) * GCOLS]

        def kt_block(t, k):
            return kt_group(t, k // 2).rearrange("p (e n) -> p e n", e=KB)[:, :, (k % 2) * P:(k % 2 + 1) * P]

        def kt_psum(k):
            return ps[:, 2 * (k % 2):2 * (k % 2) + 2, :].rearrange("p a (b c) -> p (a b) c", b=4)

        def v_slot(t, k):
            return flat(t)[:, 2 * GCOLS + (k % 4) * D:2 * GCOLS + (k % 4 + 1) * D]

        def out_banks(b):
            return 6 - 2 * b

        def page_count(k):
            return (k // 8 + 1) * 16

        def load_page(sp, i, d, kv, k):
            page = sp.value_load(pt_sb[0:1, bass.ds(i * NP + (d * NP + k), 1)], min_val=0, max_val=POOL - 1)
            return page_rows[kv][bass.ds(page, 1), :, :].rearrange("a p c -> (a p) c")

        def k_pages_sp(sp, i, d, lo, hi):
            for k in range(lo, hi):
                src = load_page(sp, i, d, 0, k)
                if k >= 8:
                    sp.wait_ge(S["pk_turned"], i * NP + (d * NP + k - 7))
                elif d:
                    sp.wait_ge(S["pv_lo"], i * NP + (k + 9))
                sp.dma_start(page_slot(k), src).then_inc(S[f"page_in{k % 8}"], 16)

        def v_pages_sp(sp, i, d):
            for k in range(NP):
                src = load_page(sp, i, d, 1, k)
                if k >= 8:
                    sp.wait_ge(S["pv_lo"], i * NP + (d * NP + NP + k - 7))
                elif d:
                    sp.wait_ge(S["pv_lo"], i * NP + (d * NP + k + 9))
                else:
                    sp.wait_ge(S["pk_turned"], i * NP + (NP + k + 9))
                sp.dma_start(page_slot(k), src).then_inc(S[f"page_in{k % 8}"], 16)

        def sa_sp(sp):
            sp.wait_ge(S["w_used"], W_OUT)
            k_pages_sp(sp, 0, 0, 0, 8)
            sp.wait_ge(S["v_used"], NSTEP * KB)
            sp.wait_ge(S["a_lo"], NSTEP * KB)
            sp.wait_ge(S["o_kept"], 4 * KB)
            sp.wait_ge(S["v_saved"], 32 * KB)
            sp.wait_ge(S["k_saved"], 32 * KB)
            sp.dma_start(vn_raw[:, :], new_s[1]).then_inc(S["sconst_in"], 16)
            sp.dma_start(mbd[:, :], A["c_mbd"]).then_inc(S["sconst_in"], 16)
            sp.dma_start(sel[:, :], A["c_sel"]).then_inc(S["sconst_in"], 16)
            sp.dma_start(smask[:, :, :], A["c_smask"]).then_inc(S["sconst_in"], 16)
            k_pages_sp(sp, 0, 0, 8, NP)
            sp.wait_ge(S["pk_turned"], NP)
            with sp.Fori(0, DB // 2 - 1) as i:
                k_pages_sp(sp, i, 1, 0, NP)
                v_pages_sp(sp, i, 0)
            v_pages_sp(sp, 0, DB // 2 - 1)

        def k_phase_pe(pe, i, d):
            for g in range(PAGES + 1):
                if g < PAGES:
                    for u in range(2):
                        k = 2 * g + u
                        pe.wait_ge(S[f"page_in{k % 8}"], i * 64 + (d * 32 + page_count(k)))
                        pe.wait_ge(S["pk_lo"], i * NP + (d * NP + max(k - 1, 0)))
                        if g == 0 and d:
                            pe.wait_ge(S["sa_lo"], i * 2 + 2)
                            pe.wait_ge(S["so_kept"], i)
                        for e in range(KB):
                            mm = pe.transpose(ps[:, 2 * u + e // 4, (e % 4) * P:(e % 4 + 1) * P],
                                              page_slot(k)[:, e * P:(e + 1) * P], ident[:, :])
                        mm.then_inc(S["pk_turned"], 1)
                if g:
                    q = g - 1
                    pe.wait_ge(S["pk_lo"], i * NP + (d * NP + 2 * g))
                    pe.wait_ge(S["sz_kept"], i * 9 + (d * 9 + max(q - 1, 0)))
                    if q == 0:
                        pe.wait_ge(S["qb_lo"], i * NP + (d * NP + NP))
                    for e in range(KB):
                        for n, (a, b) in enumerate(((qbh, xh), (qbh, xl), (qbl, xh))):
                            mm = pe.matmul(ps[:, 4 + q % 2, 0:2 * P], a[:, e, :],
                                           kt_group(b, q)[:, e * 2 * P:(e + 1) * 2 * P],
                                           start=(e == 0 and n == 0), stop=(e == KB - 1 and n == 2))
                    mm.then_inc(S["sz_out"], 1)
            if d == 0:
                pe.wait_ge(S["sconst_in"], 64)
                pe.wait_ge(S["new_lo"], 1)
                pe.wait_ge(S["pv_lo"], NP)
            pe.wait_ge(S["sz_kept"], i * 9 + (d * 9 + 7))
            for e in range(KB):
                for n, (a, b) in enumerate(((qbh, ksh), (qbh, ksl), (qbl, ksh))):
                    pe.matmul(ps[:, 4, 0:NS], a[:, e, :], b[:, e, :], start=(e == 0 and n == 0), stop=False)
            mask = smask[:, bass.ds(i + d, 1), :].rearrange("p a n -> p (a n)") if d else smask[:, 0, :]
            pe.matmul(ps[:, 4, 0:NS], ident[:, :], mask, start=False, stop=True).then_inc(S["sz_out"], 1)

        def turn_weights_pe(pe, i, d):
            pe.wait_ge(S["s_a"], i + (d + 1))
            for kb in range(PAGES):
                pe.transpose(ps[:, kb // 4, (kb % 4) * P:(kb % 4 + 1) * P], tmp[:, 1, kb * P:(kb + 1) * P], ident[:, :])
            pe.transpose(ps[0:NS, 2, 0:P], tmp[:, 1, PAST:KEYS], ident[:, :]).then_inc(S["sa_turned"], 1)

        def v_phase_pe(pe, i, d):
            pe.wait_ge(S["sa_lo"], i * 2 + (d * 2 + 2))
            for b in range(2):
                bank = out_banks(b)
                if b == 0:
                    pe.wait_ge(S["so_mask"], i * 2 + d * 2)
                else:
                    pe.wait_ge(S["sz_kept"], i * 9 + (9 * min(d + 2, DB // 2)))
                for pg in range(PAGES + 1):
                    new = pg == PAGES
                    k = PAGES * b + pg
                    if not new:
                        pe.wait_ge(S["pv_lo"], i * NP + (d * NP + NP + k + 1))
                    r = slice(0, NS) if new else slice(0, P)
                    for n2 in range(2):
                        c = slice(n2 * 512, (n2 + 1) * 512)
                        vv = (vnh[:, c], vnl[:, c]) if new else (v_slot(xh, k)[:, c], v_slot(xl, k)[:, c])
                        for n, (a, x) in enumerate(((ath, vv[0]), (ath, vv[1]), (atl, vv[0]))):
                            mm = pe.matmul(ps[:, bank + n2, :], a[r, pg, :], x,
                                           start=(pg == 0 and n == 0), stop=(new and n == 2))
                    mm.then_inc(S["so_out" if new else "pv_used"], 1)

        def turn_out_pe(pe, i, d):
            pe.wait_ge(S["so_mask"], i * 2 + (d * 2 + 2))
            pe.wait_ge(S["so_kept"], i + d)
            for e in range(KB):
                mm = pe.matmul(ps[:, 3, e * 2 * DQ:(e + 1) * 2 * DQ], om[:, e * P:(e + 1) * P], sel[:, :],
                               start=True, stop=True)
            mm.then_inc(S["so_turned"], 1)

        def sa_pe(pe):
            pe.wait_ge(S["a_done"], NSTEP * KB)
            pe.wait_ge(S["o_kept"], 4 * KB)
            k_phase_pe(pe, 0, 0)
            turn_weights_pe(pe, 0, 0)
            with pe.Fori(0, DB // 2 - 1) as i:
                k_phase_pe(pe, i, 1)
                v_phase_pe(pe, i, 0)
                turn_weights_pe(pe, i, 1)
                turn_out_pe(pe, i, 0)
            v_phase_pe(pe, 0, DB // 2 - 1)
            turn_out_pe(pe, 0, DB // 2 - 1)

        def k_phase_act(act, i, d):
            for k in range(NP):
                if d == 0 and k == 8:
                    act.wait_ge(S["sconst_in"], 64)
                    act.wait_ge(S["s_zero"], 2)
                    for dst, src in ((ksh, ks), (vnh, vn_raw)):
                        act.copy(dst[:], src[:]).then_inc(S["new_hi"], 1)
                act.wait_ge(S["pk_turned"], i * NP + (d * NP + k + 1))
                act.wait_ge(S["sz_out"], i * 9 + (d * 9 + max(k // 2 - 1, 0)))
                act.copy(kt_block(xh, k), kt_psum(k)).then_inc(S["pk_hi"], 1)

        def exp_act(act, i, d):
            act.wait_ge(S["s_capped"], i + (d + 1))
            act.activation(tmp[:, 1, :], tmp[:, 1, :], ACT.Exp).then_inc(S["s_exp"], 1)
            act.wait_ge(S["s_exp"], i + (d + 1))
            act.activation(tmp[:, 1, :], tmp[:, 1, :], ACT.Ln, bias=1.0).then_inc(S["s_ln"], 1)

        def weights_act(act, i, d):
            act.wait_ge(S["s_log"], i + (d + 1))
            act.activation(tmp[:, 1, :], tmp[:, 0, :], ACT.Exp).then_inc(S["s_a"], 1)

        def turned_act(act, i, d):
            act.wait_ge(S["sa_turned"], i + (d + 1))
            act.wait_ge(S["so_out"], i * 2 + d * 2)
            act.copy(ath[:, 0:PAGES, :], ps[:, 0:2, :].rearrange("p a (b c) -> p (a b) c", b=4)).then_inc(S["sa_hi"], 1)
            act.copy(ath[0:NS, PAGES, :], ps[0:NS, 2, 0:P]).then_inc(S["sa_hi"], 1)

        def v_phase_act(act, i, d, first_page):
            for k in range(NP):
                if d == 0 and k == 2:
                    exp_act(act, i, 1)
                if d == 0 and k == 8:
                    weights_act(act, i, 1)
                act.wait_ge(S["pv_used"], i * NP + (d * NP + max(k - 3, 0)))
                act.wait_ge(S[f"page_in{k % 8}"], i * 64 + (first_page + page_count(k)))
                act.copy(v_slot(xh, k), page_slot(k)).then_inc(S["pv_hi"], 1)

        def keep_out_act(act, i, d):
            act.wait_ge(S["so_turned"], i + (d + 1))
            src = ps[:, 3, 0:NS * 2].rearrange("p (e n) -> p e n", e=KB)
            act.copy(acc[:, :, bass.ds(i * (2 * DQ) + (d * 2 * DQ + SEQ), 2 * DQ)], src).then_inc(S["so_kept"], 1)

        def sa_act(act):
            k_phase_act(act, 0, 0)
            exp_act(act, 0, 0)
            weights_act(act, 0, 0)
            turned_act(act, 0, 0)
            with act.Fori(0, DB // 2 - 1) as i:
                k_phase_act(act, i, 1)
                v_phase_act(act, i, 0, 64)
                turned_act(act, i, 1)
                keep_out_act(act, i, 0)
            v_phase_act(act, 0, DB // 2 - 1, 7 * 32)
            keep_out_act(act, 0, DB // 2 - 1)

        def qb_block(t, e, h):
            rows = slice(HD * h, HD * (h + 1))
            return t[rows, e, :].rearrange("p (b c) -> p b c", b=2)[:, :, DQ * (2 * e + h):DQ * (2 * e + h + 1)]

        def qs_block(i, e, rows):
            return qs[rows, e, i * (2 * DQ):(i + 1) * (2 * DQ)].rearrange("p (b q) -> p b q", b=2)

        def sa_pool(pool):
            pool.wait_ge(S["s_zero"], 2)
            pool.wait_ge(S["s_row"], 2 * KB)
            for i in range(DB // 2):
                pool.wait_ge(S["sz_out"], i * 9)
                for e in range(KB):
                    for h in range(2):
                        rows = slice(HD * h, HD * (h + 1))
                        ones = one[rows, 0:1].to_broadcast([HD, 2 * DQ]).rearrange("p (b q) -> p b q", b=2)
                        pool.tensor_tensor(qb_block(qbh, e, h), qs_block(i, e, rows), ones, ALU.mult) \
                            .then_inc(S["qb_hi"], 1)
                for e in range(KB):
                    for h in range(2):
                        rows = slice(HD * h, HD * (h + 1))
                        pool.wait_ge(S["qb_hi"], i * NP + (2 * e + h + 1))
                        pool.tensor_tensor(qb_block(qbl, e, h), qs_block(i, e, rows), qb_block(qbh, e, h).bitcast(F32),
                                           ALU.subtract).then_inc(S["qb_lo"], 1)

        def k_phase_dve(dve, i, d):
            for g in range(PAGES + 1):
                if d == 0 and g == 5:
                    dve.wait_ge(S["sconst_in"], 64)
                    dve.wait_ge(S["new_hi"], 2)
                    dve.tensor_tensor(ksl[:], ks[:], ksh[:].bitcast(F32), ALU.subtract).then_inc(S["new_lo"], 1)
                    dve.tensor_tensor(vnl[:], vn_raw[:], vnh[:].bitcast(F32), ALU.subtract).then_inc(S["pv_lo"], NP)
                if g < PAGES:
                    for k in (2 * g, 2 * g + 1):
                        dve.wait_ge(S["pk_hi"], i * NP + (d * NP + k + 1))
                        dve.tensor_tensor(kt_block(xl, k), kt_psum(k), kt_block(xh, k).bitcast(F32),
                                          ALU.subtract).then_inc(S["pk_lo"], 1)
                if g:
                    q = g - 1
                    rows = slice(64 * (q // 4), 64 * (q // 4) + 64)
                    dve.wait_ge(S["sz_out"], i * 9 + (d * 9 + g))
                    if q == 0:
                        dve.wait_ge(S["s_a"], i + d)
                    dve.tensor_scalar(tmp[rows, 0, (q % 4) * 2 * P:(q % 4 + 1) * 2 * P], ps[rows, 4 + q % 2, 0:2 * P],
                                      bias_s[rows, 0:1], None, ALU.add).then_inc(S["sz_kept"], 1)
            dve.wait_ge(S["sz_out"], i * 9 + (d * 9 + 9))
            dve.tensor_scalar(tmp[:, 0, PAST:KEYS], ps[:, 4, 0:NS], bias_s[:, 0:1], None, ALU.add) \
                .then_inc(S["sz_kept"], 1)

        def softmax_dve(dve, i, d, step):
            if step == 0:
                dve.wait_ge(S["sz_kept"], i * 9 + (d * 9 + 9))
                dve.wait_ge(S["sa_turned"], i + d)
                dve.tensor_scalar(tmp[:, 1, :], tmp[:, 0, :], ZCAP, None, ALU.min).then_inc(S["s_capped"], 1)
            elif step == 1:
                dve.wait_ge(S["s_ln"], i + (d + 1))
                dve.tensor_tensor(tmp[:, 1, :], tmp[:, 0, :], tmp[:, 1, :], ALU.max).then_inc(S["s_chain"], 1)
            elif step == 2:
                dve.wait_ge(S["s_chain"], i * 2 + (d * 2 + 1))
                dve.tensor_tensor_scan(out=tmp[:, 2, ::-1], data0=tmp[:, 1, ::-1], data1=tmp[:, 1, ::-1],
                                       initial=0.0, op0=ALU.add, op1=ALU.bypass).then_inc(S["s_chain"], 1)
            else:
                dve.wait_ge(S["s_chain"], i * 2 + (d * 2 + 2))
                dve.tensor_tensor(tmp[:, 0, :], tmp[:, 0, :], tmp[:, 2, :], ALU.subtract).then_inc(S["s_log"], 1)

        def turned_dve(dve, i, d):
            dve.wait_ge(S["sa_hi"], i * 2 + (d * 2 + 2))
            dve.tensor_tensor(atl[:, 0:PAGES, :], ps[:, 0:2, :].rearrange("p a (b c) -> p (a b) c", b=4),
                              ath[:, 0:PAGES, :].bitcast(F32), ALU.subtract).then_inc(S["sa_lo"], 1)
            dve.tensor_tensor(atl[0:NS, PAGES, :], ps[0:NS, 2, 0:P], ath[0:NS, PAGES, :].bitcast(F32),
                              ALU.subtract).then_inc(S["sa_lo"], 1)

        def mask_out_dve(dve, i, d, b):
            rows = slice(64 * b, 64 * b + 64)
            dve.wait_ge(S["so_out"], i * 2 + (d * 2 + b + 1))
            dve.wait_ge(S["so_turned"], i + d)
            dve.tensor_tensor(om[rows, :], ps[rows, out_banks(b):out_banks(b) + 2, :].rearrange("p a c -> p (a c)"),
                              mbd[rows, :], ALU.mult).then_inc(S["so_mask"], 1)

        def v_phase_dve(dve, i, d):
            for k in range(NP):
                if d == 0 and k in (0, 4, 5, 6):
                    softmax_dve(dve, i, 1, (0, 4, 5, 6).index(k))
                if k == 12:
                    mask_out_dve(dve, i, d, 0)
                dve.wait_ge(S["pv_hi"], i * NP + (d * NP + k + 1))
                dve.tensor_tensor(v_slot(xl, k), page_slot(k), v_slot(xh, k).bitcast(F32), ALU.subtract) \
                    .then_inc(S["pv_lo"], 1)
            mask_out_dve(dve, i, d, 1)

        def sa_dve(dve):
            dve.wait_ge(S["v_used"], NSTEP * KB)
            dve.wait_ge(S["w_used"], W_OUT)
            dve.wait_ge(S["a_hi"], NSTEP * KB)
            dve.wait_ge(S["v_saved"], 32 * KB)
            dve.memset(qbh[:, :, :].bitcast(F32), 0.0).then_inc(S["s_zero"], 1)
            dve.memset(qbl[:, :, :].bitcast(F32), 0.0).then_inc(S["s_zero"], 1)
            k_phase_dve(dve, 0, 0)
            for step in range(4):
                softmax_dve(dve, 0, 0, step)
            turned_dve(dve, 0, 0)
            with dve.Fori(0, DB // 2 - 1) as i:
                k_phase_dve(dve, i, 1)
                v_phase_dve(dve, i, 0)
                turned_dve(dve, i, 1)
            v_phase_dve(dve, 0, DB // 2 - 1)

        def ou_sp(sp):
            sp.wait_ge(S["pv_lo"], NP * (DB // 2 + 1))
            for n in range(3):
                with sp.Fori(0, KB - 1, 2) as m:
                    for u in range(2):
                        load_tile(sp, m, W_OUT + n * KB + u, out_w[n][:, :, bass.ds(m * P + u * P, P)])

        def ou_pe(pe):
            for n in range(3):
                with pe.Fori(0, KB - 3, 4) as m:
                    for u in range(4):
                        pe.wait_ge(S["w_split"], m + (W_OUT + n * KB + u + 1))
                        if n or u >= 2:
                            pe.wait_ge(S["mix_out"], m + (n * KB + u - 1))
                        else:
                            pe.wait_ge(S["mix_out"], m)
                        linear(pe, W_OUT_B if n == 1 else W_OUT, u, u % 2, S["w_used"],
                               ("a", "b", "out")[n] if u == 0 else None)

        def aux_load(act, src, m, n, u):
            act.wait_ge(S["mix_out"], m + (n + u - 1))
            act.dma_start(tmp[:, u % 2, :], src[bass.ds(m + u, 1), :, :].rearrange("a p t -> (a p) t")) \
                .then_inc(S[f"aux_in{u % 2}"], 16)

        def conv_load(act, kb):
            if kb >= 2:
                act.wait_ge(S["op_lo"], LO_A + kb - 1)
            act.dma_start(tmp[:, 2 + kb % 2, :], conv_d[kb, :, :]).then_inc(S[f"conv_in{kb % 2}"], 16)

        def conv_high(act, kb):
            act.wait_ge(S[f"conv_in{kb % 2}"], 16 * (kb // 2 + 1))
            dst = gh2 if kb < HB else xh
            act.copy(dst[:, kb, :], tmp[:, 2 + kb % 2, :]).then_inc(S["op_hi"], 1)

        def conv_low(dve, kb):
            hi, lo = (gh2, gl2) if kb < HB else (xh, xl)
            dve.wait_ge(S["op_hi"], HI_A + kb + 1)
            dve.tensor_tensor(lo[:, kb, :], tmp[:, 2 + kb % 2, :], hi[:, kb, :].bitcast(F32),
                              ALU.subtract).then_inc(S["op_lo"], 1)

        def ou_act(act):
            act.wait_ge(S["siga_saved"], 16 * KB)
            act.wait_ge(S["sigb_saved"], 16 * KB)
            act.wait_ge(S["conv_saved"], 16 * KB)
            act.wait_ge(S["sa_turned"], DB // 2)
            act.dma_start(tmp[:, 0, :], sig_a_d[0, :, :]).then_inc(S["aux_in0"], 16)
            act.dma_start(tmp[:, 1, :], sig_a_d[1, :, :]).then_inc(S["aux_in1"], 16)
            conv_load(act, 0)
            conv_load(act, 1)
            act.wait_ge(S["so_kept"], DB // 2)
            for kb in range(KB):
                act.copy(xh[:, kb, :], acc[:, kb, :]).then_inc(S["op_hi"], 1)
            for kb in range(HB):
                conv_high(act, kb)
                conv_load(act, kb + 2)
            with act.Fori(0, KB - 3, 2) as m:
                for u in range(2):
                    aux_load(act, sig_a_d, m, 0, u + 2)
            act.wait_ge(S["w_used"], W_OUT + KB)
            for kb in range(HB, KB):
                conv_high(act, kb)
                if kb + 2 < KB:
                    conv_load(act, kb + 2)
            for kb in range(KB):
                aux_load(act, sig_b_d, 0, KB, kb)
                if 2 <= kb < HB + 2:
                    act.wait_ge(S["mix_out"], KB + kb - 1)
                    act.copy(xh[:, kb - 2, :], acc[:, kb - 2, :]).then_inc(S["op_hi"], 1)
            act.wait_ge(S["x1_saved"], 16 * KB)
            for u in range(2):
                aux_load(act, x1_d, 0, 2 * KB, u)
            act.wait_ge(S["w_used"], W_OUT + 2 * KB)
            for kb in range(HB, KB):
                act.wait_ge(S["mix_out"], KB + kb + 1)
                act.copy(xh[:, kb, :], acc[:, kb, :]).then_inc(S["op_hi"], 1)
            with act.Fori(0, KB - 3, 2) as m:
                for u in range(2):
                    aux_load(act, x1_d, m, 2 * KB, u + 2)

        def mix(dve, m, n, u):
            out = acc[:, bass.ds(m + u, 1), :].rearrange("p a (c n) -> p (a c) n", c=3)
            aux = tri(tmp[:, u % 2, :])
            dve.wait_ge(S["w_used"], m + (W_OUT + n * KB + u + 1))
            dve.wait_ge(S[f"aux_in{u % 2}"], m * 8 + (n * KB // 2 + u // 2 + 1) * 16)
            if n == 0:
                dve.tensor_tensor(out, aux, pset(u % 2), ALU.mult).then_inc(S["mix_out"], 1)
            elif n == 1:
                dve.tensor_tensor(aux, aux, pset(u % 2), ALU.mult).then_inc(S["mix_tmp"], 1)
                dve.wait_ge(S["mix_tmp"], m + (u + 1))
                dve.wait_ge(S["mix_out"], m + (KB + u))
                dve.tensor_tensor(out, out, aux, ALU.add).then_inc(S["mix_out"], 1)
            else:
                dve.scalar_tensor_tensor(out=out, in0=aux, scalar=ALPHA, in1=pset(u % 2), op0=ALU.mult,
                                         op1=ALU.add).then_inc(S["mix_out"], 1)

        def ou_dve(dve):
            dve.wait_ge(S["so_kept"], DB // 2)
            split_lo(dve, HI_A - KB, range(KB), "op_lo")
            for kb in range(HB):
                conv_low(dve, kb)
            with dve.Fori(0, KB - 1, 2) as m:
                for u in range(2):
                    mix(dve, m, 0, u)
            for kb in range(HB, KB):
                conv_low(dve, kb)
            for kb in range(KB):
                mix(dve, 0, 1, kb)
                if kb < HB:
                    split_lo(dve, HI_OUT - KB, (kb,), "op_lo")
            split_lo(dve, HI_OUT - KB, range(HB, KB), "op_lo")
            with dve.Fori(0, KB - 1, 2) as m:
                for u in range(2):
                    mix(dve, m, 2, u)

        NTOK = SEQ // P + 1

        def tok_rows(k):
            return P if k < NTOK - 1 else NS

        def tok_psum(k, n):
            return ps[:, 2 * (k % 3):2 * (k % 3) + 2, :].rearrange("p a (b c) -> p (a b) c", b=4)[:, :, 0:n]

        block = top.enter_context(nc.Block())

        @block.sync
        def _(sp):
            sp.dma_start(ident[:, :], A["c_ident"]).then_inc(S["ident_in"], 16)
            for k in range(NTOK):
                if k == 4:
                    sp.dma_start(tmp[0:DB * HIST // 2, 2:4, 0:D], state_rows.rearrange("(j p) c -> p j c", j=2)) \
                        .then_inc(S["hist_in"], 16)
                if k >= 8:
                    sp.wait_ge(S["tok_turned"], k - 7)
                src = A["x_prompt"][0, k * P:(k + 1) * P, :] if k < NTOK - 1 else \
                    A["x_sample"].rearrange("b q d -> (b q) d")
                sp.dma_start(tok[0:tok_rows(k), k % 8, :], src).then_inc(S[f"tok_in{k % 8}"], 16)
            sp.dma_start(O["new_conv_s"][0, :, 0:HIST - DQ, :], A["state_conv"][0, :, DQ:HIST, :]) \
                .then_inc(S["state_saved"], 16)
            ff_sp(sp, 0)
            cv_sp(sp)
            at_sp(sp)
            sa_sp(sp)
            ou_sp(sp)
            ff_sp(sp, 1)
            for k in range(NTOK):
                sp.wait_ge(S["y_kept"], k + 1)
                dst = O["y_p"][0, k * P:(k + 1) * P, :] if k < NTOK - 1 else O["y_s"].rearrange("b q d -> (b q) d")
                sp.dma_start(dst, tmp[0:tok_rows(k), k % 4, 0:D]).then_inc(S[f"y_saved{k % 4}"], 16)
            for k in range(4):
                sp.wait_ge(S[f"y_saved{k}"], 16 * ((NTOK - k + 3) // 4))
            sp.wait_ge(S["k_saved"], 32 * KB)
            sp.wait_ge(S["v_saved"], 32 * KB)
            sp.wait_ge(S["tail_saved"], 16 * (DB + 1))
            sp.wait_ge(S["state_saved"], 16)

        @block.gpsimd
        def _(pool):
            pool.memset(one[:, :], 1.0).then_inc(S["one_set"], 1)
            pool.wait_ge(S["one_set"], 1)
            split_phase(pool, W_FF1, W_CONV - W_FF1, 4)
            ln_sum_pool(pool, 0, "acc_done", KB * FG)
            pool.wait_ge(S["w_used"], W_CONV)
            cv_pool(pool)
            split_phase(pool, W_ATT, W_OUT - W_ATT, 3)
            sa_pool(pool)
            pool.wait_ge(S["pv_lo"], NP * (DB // 2 + 1))
            split_phase(pool, W_OUT, W_FF2 - W_OUT, 4)
            ln_sum_pool(pool, 2, "mix_out", 2 * KB)
            split_phase(pool, W_FF2, W_END - W_FF2, 4, HI_OUT)
            ln_sum_pool(pool, 3, "acc_done", KB + 2 * KB * FG)

        @block.tensor
        def _(pe):
            pe.wait_ge(S["ident_in"], 16)
            for k in range(NTOK):
                n = tok_rows(k)
                pe.wait_ge(S[f"tok_in{k % 8}"], 16 * (k // 8 + 1))
                if k >= 3:
                    pe.wait_ge(S["op_lo"], k - 2)
                    pe.wait_ge(S["acc_done"], k - 2)
                for e in range(KB):
                    mm = pe.transpose(ps[:, 2 * (k % 3) + e // 4, (e % 4) * P:(e % 4) * P + n],
                                      tok[0:n, k % 8, e * P:(e + 1) * P], ident[0:n, 0:n])
                mm.then_inc(S["tok_turned"], 1)
            pe.wait_ge(S["acc_init"], 1)
            hist_pe(pe)
            pe.wait_ge(S["const_in"], 16 * len(CONSTS))
            pe.wait_ge(S["mask_set"], 2)
            ff_pe(pe, 0)
            pe.wait_ge(S["acc_done"], KB + KB * FG)
            ln_pe(pe, 0)
            cv_pe(pe)
            pe.wait_ge(S["tap_done"], TAPS * KB)
            pe.wait_ge(S["siga_done"], KB)
            pe.wait_ge(S["sigb_done"], KB)
            ln_pe(pe, 1)
            at_pe(pe)
            sa_pe(pe)
            ou_pe(pe)
            pe.wait_ge(S["mix_out"], 3 * KB)
            ln_pe(pe, 2)
            ff_pe(pe, 1)
            pe.wait_ge(S["acc_done"], 2 * (KB + KB * FG))
            ln_pe(pe, 3)
            for k in range(NTOK):
                n = tok_rows(k)
                pe.wait_ge(S["ln_aff"], 4 * KB)
                if k >= 3:
                    pe.wait_ge(S["y_kept"], k - 2)
                for e in range(KB):
                    mm = pe.transpose(ps[0:n, 2 * (k % 3) + e // 4, (e % 4) * P:(e % 4 + 1) * P],
                                      acc[:, e, k * P:k * P + n], ident[:, :])
                mm.then_inc(S["y_turned"], 1)

        @block.scalar
        def _(act):
            for dst, name in CONSTS:
                act.dma_start(dst, A[name]).then_inc(S["const_in"], 16)
            for k in range(NTOK):
                n = tok_rows(k)
                act.wait_ge(S["tok_turned"], k + 1)
                act.copy(xh[:, :, k * P:k * P + n], tok_psum(k, n)).then_inc(S["op_hi"], 1)
                act.mul(acc[:, :, k * P:k * P + n], tok_psum(k, n), ALPHA) \
                    .then_inc(S["acc_done" if k < KB else "acc_init"], 1)
            act.wait_ge(S["const_in"], 16 * len(CONSTS))
            act.wait_ge(S["mask_set"], 2)
            ff_act(act, 0)
            act.wait_ge(S["eps_set"], 1)
            ln_act(act, 0, ACT.Identity, HI_FF1)
            for kb in range(KB):
                act.wait_ge(S["ln_aff"], kb + 1)
                act.dma_start(x1_d[kb, :, :], acc[:, kb, :]).then_inc(S["x1_saved"], 16)
            cv_act(act)
            act.wait_ge(S["siga_saved"], 16 * KB)
            act.wait_ge(S["sigb_saved"], 16 * KB)
            ln_act(act, 1, ACT.Silu, None)
            for kb in range(KB):
                act.wait_ge(S["ln_aff"], KB + kb + 1)
                act.dma_start(conv_d[kb, :, :], acc[:, kb, :]).then_inc(S["conv_saved"], 16)
            at_act(act)
            sa_act(act)
            ou_act(act)
            ln_act(act, 2, ACT.Identity, HI_OUT)
            for kb in range(KB):
                act.wait_ge(S["op_lo_odd"] if kb % 2 else S["op_lo"], (HB if kb % 2 else LO_OUT) + kb // 2 + 1)
                act.mul(acc[:, kb, :], acc[:, kb, :], ALPHA).then_inc(S["acc_done"], 1)
            ff_act(act, 1)
            ln_act(act, 3, ACT.Identity, None)

        @block.vector
        def _(dve):
            dve.memset(epsc[:, :], EPS).then_inc(S["eps_set"], 1)
            for k in range(NTOK):
                n = tok_rows(k)
                dve.wait_ge(S["op_hi"], k + 1)
                dve.wait_ge(S["acc_done" if k < KB else "acc_init"], k + 1 if k < KB else 1)
                dve.tensor_tensor(xl[:, :, k * P:k * P + n], tok_psum(k, n), xh[:, :, k * P:k * P + n].bitcast(F32),
                                  ALU.subtract).then_inc(S["op_lo"], 1)
            hist_dve(dve)
            dve.wait_ge(S["const_in"], 16 * len(CONSTS))
            dve.wait_ge(S["ident_in"], 16)
            dve.tensor_copy(identb[:, :], ident[:, :]).then_inc(S["mask_set"], 1)
            dve.tensor_copy(dmask[:, :], tmp[:, 0, 0:P]).then_inc(S["mask_set"], 1)
            dve.wait_ge(S["acc_init"], 1)
            ff_dve(dve, 0)
            dve.wait_ge(S["acc_done"], KB + KB * FG)
            ln_dve(dve, 0, HI_FF1)
            cv_dve(dve)
            cv_dve_main(dve)
            dve.wait_ge(S["tap_done"], TAPS * KB)
            ln_dve(dve, 1, None)
            at_dve(dve)
            sa_dve(dve)
            ou_dve(dve)
            dve.wait_ge(S["mix_out"], 3 * KB)
            ln_dve(dve, 2, HI_OUT)
            ff_dve(dve, 1)
            dve.wait_ge(S["acc_done"], 2 * (KB + KB * FG))
            ln_dve(dve, 3, None)
            for k in range(NTOK):
                n = tok_rows(k)
                dve.wait_ge(S["y_turned"], k + 1)
                if k >= 4:
                    dve.wait_ge(S[f"y_saved{k % 4}"], 16 * (k // 4))
                dve.tensor_copy(tmp[0:n, k % 4, 0:D].rearrange("p (a c) -> p a c", a=2),
                                ps[0:n, 2 * (k % 3):2 * (k % 3) + 2, :]).then_inc(S["y_kept"], 1)


def shape_constants():
    i = np.arange(P)
    col = np.arange(D)
    head = (i // DQ) % H
    new = np.arange(NS)
    low = -(2.0 ** 60)
    smask = np.full((P, DB // 2, NS), low, np.float32)
    for pair in range(DB // 2):
        own = (new[None, :] // DQ == 2 * pair + i[:, None] // 64) & (new[None, :] % DQ < i[:, None] % DQ)
        smask[:, pair, :][own] = 0.0
    return {
        "c_ident": np.eye(P, dtype=np.float32),
        "c_negtri": -(i[:, None] >= i[None, :]).astype(np.float32),
        "c_negones": -np.ones((P, P), np.float32),
        "c_avg": np.full((P, P), 1.0 / D, np.float32),
        "c_dmask": np.where(i[:, None] < i[None, :], 0.0, low).astype(np.float32),
        "c_mbd": (col[None, :] // HD == head[:, None]).astype(np.float32),
        "c_sel": ((i[:, None] // 64) * DQ + i[:, None] % DQ == np.arange(2 * DQ)[None, :]).astype(np.float32),
        "c_smask": smask,
    }


def by_feature(a):
    return np.ascontiguousarray(np.reshape(a, (-1, P)).T)


OUTS = {
    "y_p": (1, SEQ, D), "y_s": (DB, DQ, D), "new_k_p": (1, 1, SEQ, H, HD), "new_v_p": (1, 1, SEQ, H, HD),
    "new_conv_p": (1, 1, HIST, D), "new_k_s": (1, DB, DQ, H, HD), "new_v_s": (1, DB, DQ, H, HD),
    "new_conv_s": (1, DB, HIST, D),
}


def kernel(**inputs):
    import concourse.bacc as bacc
    from concourse.bass_utils import run_bass_kernel_spmd

    x = {k: np.asarray(v) for k, v in inputs.items()}
    arrays = {k: np.ascontiguousarray(x[k]) for k in (
        "x_prompt", "x_sample", "cache_k", "cache_v", "state_conv", "w_ff1_up", "w_ff1_down", "w_in",
        "w_proj_a", "w_proj_b", "w_out", "w_ff2_up", "w_ff2_down")}
    arrays["page_table"] = np.ascontiguousarray(x["page_table"].reshape(1, -1))
    arrays["norms"] = np.stack([by_feature(x[n]) for n in (
        "ln1_g", "ln1_b", "ln_conv_g", "ln_conv_b", "ln2_g", "ln2_b", "ln3_g", "ln3_b")], axis=1)
    arrays["gate_bias"] = by_feature(x["b_gate"])
    arrays["conv_bias"] = by_feature(x["b_dw"])
    arrays["taps"] = np.ascontiguousarray(x["w_dw"].reshape(CW, KB, P).transpose(2, 1, 0))
    arrays["b_heads"] = np.ascontiguousarray(np.broadcast_to(x["b_sb"].reshape(1, H), (P, H)))
    arrays["b_rows"] = np.ascontiguousarray(np.tile(np.repeat(x["b_sb"].reshape(H), DQ), 2).reshape(P, 1))
    arrays.update(shape_constants())

    nc = bacc.Bacc("TRN2", target_bir_lowering=False, num_devices=1)
    A = {k: nc.dram_tensor("in_" + k, a.shape, mybir.dt.from_np(a.dtype), kind="ExternalInput").ap()
         for k, a in arrays.items()}
    O = {k: nc.dram_tensor("out_" + k, s, F32, kind="ExternalOutput").ap() for k, s in OUTS.items()}
    build(nc, A, O)
    r = run_bass_kernel_spmd(nc, [{"in_" + k: a for k, a in arrays.items()}], core_ids=[0])
    return tuple(r.results[0]["out_" + k] for k in OUTS)
```

```python
from contextlib import ExitStack

import numpy as np

import concourse.bass as bass
import concourse.mybir as mybir
from concourse.alu_op_type import AluOpType as ALU

ACT = mybir.ActivationFunctionType
F32 = mybir.dt.float32
F32R = mybir.dt.float32r
BF16 = mybir.dt.bfloat16
I32 = mybir.dt.int32

P = 128
D = 1024
KB = D // P
SEQ = 1024
DB, DQ = 8, 4
NS = DB * DQ
T = SEQ + NS
CH = T // 3
H, HD = 16, 64
F = 2816
FT = F // P
FG = FT // 2
CW = 31
HIST = CW - 1
PAGES = 8
POOL = 80
PAST = PAGES * P
ALPHA = 2.0 ** 0.25
SCALE = HD ** -0.5
EPS = 1e-5
ZCAP = 30.0
KEYS = PAST + NS
NSTEP = 24

W_FF1, W_CONV, W_ATT, W_OUT, W_FF2 = 0, 66, 98, 122, 146
W_END = 212
W_OUT_B = W_OUT + KB

STEPS = [(c, kb, h) for c in range(2) for kb in range(4 * c + 3, -1, -1) for h in range(2)]


LAG_SUM, LAG_OUT = 3, 5

SEMS = [
    "a_done", "a_hi", "a_lo", "acc_done", "acc_init", "aux_in0", "aux_in1", "bias_set",
    "const_in", "conv_in0", "conv_in1", "conv_saved", "csig_done", "down_out", "e_done",
    "eps_set", "glu_done", "hist_in", "hist_kept", "hist_turned", "ident_in", "k_hi", "k_lo",
    "k_nat", "k_raw", "k_saved", "k_turned", "l_done", "ln_aff", "ln_cent", "ln_log", "ln_mean",
    "ln_rstd", "ln_scaled", "ln_sq", "ln_sqread", "ln_sum", "mask_set", "mix_out", "mix_tmp",
    "new_hi", "new_lo", "o_kept", "one_set", "op_hi", "op_lo", "op_lo_odd", "pad_set",
    "page_in0", "page_in1", "page_in2", "page_in3", "page_in4", "page_in5", "page_in6",
    "page_in7", "pk_hi", "pk_lo", "pk_turned", "prod_done", "prod_hi", "prod_lo", "pv_hi",
    "pv_lo", "pv_used", "q_hi", "q_lo", "qb_hi", "qb_lo", "run_done", "run_high", "run_split",
    "s_a", "s_capped", "s_chain", "s_exp", "s_ln", "s_log", "s_ready", "s_row", "s_zero",
    "sa_hi", "sa_lo", "sa_turned", "sconst_in", "side_prod", "side_sum", "siga_done",
    "siga_saved", "sigb_done", "sigb_saved", "silu_done", "so_kept", "so_mask", "so_out",
    "so_turned", "sp_ready", "state_saved", "sz_kept", "sz_out", "tail_kept", "tail_saved",
    "tail_turned", "tap_done", "tok_in0", "tok_in1", "tok_in2", "tok_in3", "tok_in4", "tok_in5",
    "tok_in6", "tok_in7", "tok_turned", "v_hi", "v_lo", "v_nat", "v_raw", "v_saved", "v_turned",
    "v_used", "w_high", "w_landed0", "w_landed1", "w_split", "w_used", "x1_saved", "y_kept",
    "y_saved0", "y_saved1", "y_saved2", "y_saved3", "y_turned", "z_capped", "z_ready",
]

FROM_ONE = [
    "a_done", "a_lo", "acc_done", "acc_init", "csig_done", "glu_done", "k_saved", "mix_out",
    "o_kept", "pv_used", "run_done", "run_split", "side_prod", "side_sum", "siga_done",
    "siga_saved", "sigb_done", "sigb_saved", "so_kept", "so_mask", "so_turned", "tail_kept",
    "tail_turned", "tap_done", "v_lo", "v_saved",
]


def seen(count):
    return count + 1


def tri(ap):
    return ap.rearrange("p (c n) -> p c n", c=3)


def chain(step):
    c, kb, _ = step
    off = P * max(kb - 4 * c, 0)
    return off, (None if kb == 4 * c + 3 else P * max(kb + 1 - 4 * c, 0))


def run_ops(step):
    off, before = chain(step)
    if step[1] == 0:
        return []
    if before is None:
        return [(off, 512, False)]
    return ([(off, before, False)] if before > off else []) + [(before, 512, True)]


RUN_OPS = [len(run_ops(s)) for s in STEPS]
RUN_TOTAL = sum(RUN_OPS)
RUN_SPLITS = sum(n > 0 for n in RUN_OPS)


def splits_before(j):
    return sum(n > 0 for n in RUN_OPS[:max(j, 0)])


SIDE = 9
MAIN = CW - SIDE
SUMS = (7, 15, 22, 29)
TAPS = 4 + 3 * MAIN + SIDE + 1
HI_FF1, HI_CONV, HI_A, HI_B, HI_OUT, HI_FF2 = 9, 17, 25, 33, 41, 49
LO_FF1, LO_CONV, LO_A, LO_B, LO_OUT, LO_FF2 = 9, 13, 21, 29, 37, 41
HB = KB // 2


def build(nc, A, O):
    with ExitStack() as top:
        def sb(name, shape, dt=F32, ctx=top):
            return ctx.enter_context(nc.sbuf_tensor(name, shape, dt))

        def dram(name, shape):
            return nc.dram_tensor(name, shape, F32, kind="Internal").ap()

        sig_a_d = dram("sig_a_scratch", [KB, P, T])
        sig_b_d = dram("sig_b_scratch", [KB, P, T])
        x1_d = dram("x1_scratch", [KB, P, T])
        conv_d = dram("conv_scratch", [KB, P, T])

        ps = top.enter_context(nc.psum_tensor("ps", [P, 8, 512], F32))

        def pset(s):
            return ps[:, 3 * s:3 * s + 3, 0:CH]

        xh = sb("xh", [P, KB, T], F32R)
        xl = sb("xl", [P, KB, T], F32R)
        acc = sb("acc", [P, KB, T])
        wraw = sb("wraw", [P, 2, D])
        tmp = sb("tmp", [P, 4, T])
        ident = sb("ident", [P, P])
        identb = sb("identb", [P, P], BF16)
        negtri = sb("negtri", [P, P])
        negones = sb("negones", [P, P], F32R)
        avg = sb("avg", [P, P])
        dmask = sb("dmask", [P, P], BF16)
        lnp = sb("lnp", [P, 8, KB])
        bgate = sb("bgate", [P, 2 * KB])
        bdw = sb("bdw", [P, KB])
        wdw = sb("wdw", [P, KB, CW])
        bias_p = sb("bias_p", [P, H])
        bias_s = sb("bias_s", [P, 1])
        epsc = sb("epsc", [P, 1])
        one = sb("one", [P, 1])
        pt_sb = sb("pt_sb", [1, DB * PAGES], I32)

        with ExitStack() as ff1:
            wh1, wl1 = (sb(f"{n}1", [P, 4, D], F32R, ff1) for n in ("wh", "wl"))
            gh1, gl1 = (sb(f"{n}1", [P, 4, T], F32R, ff1) for n in ("gh", "gl"))
        with ExitStack() as start:
            sb("hole_w1", [P, 8 * D], F32, start)
            tok = sb("tok", [P, 8, D], F32, start)
        with ExitStack() as cv:
            whc, wlc = (sb(f"{n}c", [P, 4, D], F32R, cv) for n in ("wh", "wl"))
            glu = sb("glu", [P, SEQ + P], F32, cv)
            ext = sb("ext", [P, DB, HIST + DQ], F32, cv)
            cbuf = sb("cbuf", [P, T], F32, cv)
            csum = sb("csum", [P, T], F32, cv)
            side = sb("side", [P, SEQ], F32, cv)
            prod1 = sb("prod1", [P, SEQ], F32, cv)
            wm = sb("wm", [P, CW + 1], F32, cv)
            tail = sb("tail", [HIST + NS, D], F32, cv)
        with ExitStack() as keep:
            sb("hole_ff1", [P, 8 * (D + T)], F32, keep)
            hist = sb("hist", [P, KB, DB * HIST], F32, keep)
        with ExitStack() as at:
            wha, wla = (sb(f"{n}a", [P, 2, D], F32R, at) for n in ("wh", "wl"))
            runh, runl = (sb(n, [P, 2, 512], F32R, at) for n in ("runh", "runl"))
            qs = sb("qs", [P, KB, NS], F32, at)
            ks = sb("ks", [P, KB, NS], F32, at)
            qh, ql, kh, kl = (sb(n, [P, T], F32R, at) for n in ("qh", "ql", "kh", "kl"))
            nat = sb("nat", [P, 2, KB, P], F32, at)
            nat_s = sb("nat_s", [NS, 2, P], F32, at)
            vh, vl = (sb(n, [P, KB, P], F32R, at) for n in ("vh", "vl"))
            ah, al = (sb(n, [P, 3, 512], F32R, at) for n in ("ah", "al"))
            run = sb("run", [P, 2, 512], F32, at)
            bias_m = sb("bias_m", [P, 2], F32, at)
        with ExitStack() as sa:
            pages = sb("pages", [P, 6, D], F32, sa)
            sb("hole_qs", [P, KB, NS], F32, sa)
            sb("hole_ks", [P, KB, NS], F32, sa)
            qbh, qbl = (sb(n, [P, KB, P], F32R, sa) for n in ("qbh", "qbl"))
            ksh, ksl = (sb(n, [P, KB, NS], F32R, sa) for n in ("ksh", "ksl"))
            ath, atl = (sb(n, [P, KB + 1, P], F32R, sa) for n in ("ath", "atl"))
            vnh, vnl = (sb(n, [NS, D], F32R, sa) for n in ("vnh", "vnl"))
            vn_raw = sb("vn_raw", [NS, D], F32, sa)
            om = sb("om", [P, D], F32, sa)
            mbd = sb("mbd", [P, D], F32, sa)
            sel = sb("sel", [P, 2 * DQ], F32, sa)
            smask = sb("smask", [P, DB // 2, NS], F32, sa)
        with ExitStack() as ou:
            who, wlo = (sb(f"{n}o", [P, 4, D], F32R, ou) for n in ("wh", "wl"))
            gh2, gl2 = (sb(f"{n}2", [P, 4, T], F32R, ou) for n in ("gh", "gl"))
        WH = {W_OUT_B: (who, wlo), W_FF1: (wh1, wl1), W_CONV: (whc, wlc), W_ATT: (wha, wla), W_OUT: (who, wlo), W_FF2: (who, wlo)}
        GH = ((gh1, gl1), (gh2, gl2))

        up_w = [A[f"w_ff{f}_up"].rearrange("a (kb p) c -> p (a kb) c", p=P) for f in (1, 2)]
        down_w = [A[f"w_ff{f}_down"].rearrange("a f c -> (a f) c") for f in (1, 2)]
        in_w = A["w_in"].rearrange("a (kb p) c -> p (a kb) c", p=P)
        out_w = [A[n].rearrange("a (kb p) c -> p (a kb) c", p=P) for n in ("w_proj_a", "w_proj_b", "w_out")]
        page_rows = [A[n].rearrange("a n p h d -> (a n) p (h d)") for n in ("cache_k", "cache_v")]
        new_p = [O[n].rearrange("a b (kb p) h d -> p (a b kb) (h d)", p=P) for n in ("new_k_p", "new_v_p")]
        new_s = [O[n].rearrange("a b q h d -> (a b q) (h d)") for n in ("new_k_s", "new_v_s")]
        state_rows = A["state_conv"].rearrange("a b i c -> (a b i) c")

        CONSTS = [(negtri[:, :], "c_negtri"),
                  (tmp[:, 1, 0:P], "c_negones"), (avg[:, :], "c_avg"), (tmp[:, 0, 0:P], "c_dmask"),
                  (lnp[:, :, :], "norms"), (bgate[:, :], "gate_bias"), (bdw[:, :], "conv_bias"),
                  (wdw[:, :, :], "taps"), (bias_p[:, :], "b_heads"), (bias_s[:, :], "b_rows"),
                  (pt_sb[:, :], "page_table")]

        S = {n: top.enter_context(nc.semaphore(n)) for n in SEMS}

        def load_tile(sp, i, n, src):
            if n >= 2:
                sp.wait_ge(S["w_split"], i + (n - 1))
            dst = wraw[:, n % 2, :]
            if len(src.shape) == 3:
                dst = dst.rearrange("p (kb c) -> p kb c", kb=KB)
            sp.dma_start(dst, src).then_inc(S[f"w_landed{n % 2}"], 16)

        def split_tile(pool, wh, wl, i, n, pos, used):
            pool.wait_ge(S[f"w_landed{n % 2}"], i * 8 + (n // 2 + 1) * 16)
            if used is not None:
                pool.wait_ge(S["w_used"], used)
            raw = wraw[:, n % 2, :]
            pool.tensor_tensor(wh[:, pos, :], raw, one[:, 0:1].to_broadcast([P, D]), ALU.mult).then_inc(S["w_high"], 1)
            pool.wait_ge(S["w_high"], i + (n + 1))
            pool.tensor_tensor(wl[:, pos, :], raw, wh[:, pos, :].bitcast(F32),
                               ALU.subtract).then_inc(S["w_split"], 1)

        def split_phase(pool, base, count, ring, norm_ops=None):
            wh, wl = WH[base]
            body = ring if ring % 2 == 0 else 2 * ring
            if base:
                pool.wait_ge(S["w_used"], base)
            for k in range(body):
                if norm_ops is not None and k == 2:
                    split_lo(pool, norm_ops, range(1, KB, 2), "op_lo_odd")
                split_tile(pool, wh, wl, 0, base + k, k % ring, base + k - ring + 1 if k >= ring else None)
            whole = (count - body) // body * body
            with pool.Fori(0, whole - body + 1, body) as i:
                for k in range(body):
                    split_tile(pool, wh, wl, i, base + body + k, k % ring, i + (base + body + k - ring + 1))
            for k in range(body + whole, count):
                split_tile(pool, wh, wl, 0, base + k, k % ring, base + k - ring + 1)

        def linear(pe, base, pos, s, sem, operand=None):
            wh, wl = WH[base]
            for kb in range(KB):
                if operand in ("conv", "ff2"):
                    if kb % 2:
                        pe.wait_ge(S["op_lo_odd"], (HB if operand == "ff2" else 0) + kb // 2 + 1)
                    else:
                        pe.wait_ge(S["op_lo"], (LO_FF2 if operand == "ff2" else LO_CONV) - HB + kb // 2 + 1)
                elif operand:
                    pe.wait_ge(S["op_lo"], {"a": LO_A, "b": LO_B, "out": LO_OUT}[operand] - KB + kb + 1)
                xh_, xl_ = (gh2, gl2) if base == W_OUT_B and kb < HB else (xh, xl)
                for n, (w, x) in enumerate(((wh, xh_), (wh, xl_), (wl, xh_))):
                    for c in range(3):
                        mm = pe.matmul(ps[:, 3 * s + c, 0:CH], w[:, pos, kb * P:(kb + 1) * P],
                                       x[:, kb, c * CH:(c + 1) * CH],
                                       start=(kb == 0 and n == 0), stop=(kb == KB - 1 and n == 2))
            mm.then_inc(sem, 1)

        def block_sum(L):
            return csum[:, :] if L == 1 else tmp[:, 2, :]

        def ln_sum_pool(pool, L, sem, before):
            buf = block_sum(L)
            for kb in range(1, KB):
                pool.wait_ge(S[sem], seen(before + kb + 1))
                if kb > 1:
                    pool.wait_ge(S["ln_sum"], SUMS[L] - KB + kb)
                pool.tensor_tensor(buf, acc[:, 0, :] if kb == 1 else buf, acc[:, kb, :], ALU.add) \
                    .then_inc(S["ln_sum"], 1)

        def ln_pe(pe, L):
            pe.wait_ge(S["ln_sum"], SUMS[L])
            for c in range(3):
                mm = pe.matmul(ps[:, c, 0:CH], avg[:, :], block_sum(L)[:, c * CH:(c + 1) * CH],
                               start=True, stop=True)
            mm.then_inc(S["ln_mean"], 1)
            for kb in range(KB):
                pe.wait_ge(S["ln_sq"], KB * L + kb + 1)
                for c in range(3):
                    mm = pe.matmul(ps[:, 3 + c, 0:CH], avg[:, :], tmp[:, kb % 2, c * CH:(c + 1) * CH],
                                   start=(kb == 0), stop=(kb == KB - 1))
                mm.then_inc(S["ln_sqread"], 1)

        def ln_dve(dve, L, ops):
            dve.wait_ge(S["ln_mean"], L + 1)
            for kb in range(KB):
                dve.tensor_tensor(tri(acc[:, kb, :]), tri(acc[:, kb, :]), pset(0), ALU.subtract) \
                    .then_inc(S["ln_cent"], 1)
            dve.wait_ge(S["ln_rstd"], L + 1)
            dve.wait_ge(S["ln_cent"], KB * (L + 1))
            for kb in range(KB + 1):
                if kb < KB:
                    dve.scalar_tensor_tensor(out=acc[:, kb, :], in0=acc[:, kb, :], scalar=lnp[:, 2 * L, kb:kb + 1],
                                             in1=tmp[:, 3, :], op0=ALU.mult, op1=ALU.mult) \
                        .then_inc(S["ln_scaled"], 1)
                j = kb - 2
                if ops is not None and j >= 0 and j % 2 == 0:
                    dve.wait_ge(S["op_hi"], ops + j + 1)
                    dve.wait_ge(S["ln_scaled"], KB * L + j + 1)
                    dve.scalar_tensor_tensor(out=xl[:, j, :], in0=acc[:, j, :], scalar=lnp[:, 2 * L + 1, j:j + 1],
                                             in1=xh[:, j, :].bitcast(F32), op0=ALU.add, op1=ALU.subtract) \
                        .then_inc(S["op_lo"], 1)

        def ln_act(act, L, func, ops):
            nc.scalar.preload_act_table_set("natural_log_exp_and_others")
            for kb in range(KB):
                act.wait_ge(S["ln_cent"], KB * L + kb + 1)
                if kb >= 2:
                    act.wait_ge(S["ln_sqread"], KB * L + kb - 1)
                act.activation(tmp[:, kb % 2, :], acc[:, kb, :], ACT.Square).then_inc(S["ln_sq"], 1)
            act.wait_ge(S["ln_sqread"], KB * (L + 1))
            act.activation(tri(tmp[:, 2, :]), pset(1), ACT.Ln, bias=epsc[:, 0:1]).then_inc(S["ln_log"], 1)
            act.wait_ge(S["ln_log"], L + 1)
            act.activation(tmp[:, 3, :], tmp[:, 2, :], ACT.Exp, scale=-0.5).then_inc(S["ln_rstd"], 1)

            def biased(kb, out, sem):
                act.wait_ge(S["ln_scaled"], KB * L + kb + 1)
                act.activation(out[:, kb, :], acc[:, kb, :], func, bias=lnp[:, 2 * L + 1, kb:kb + 1]) \
                    .then_inc(S[sem], 1)

            if ops is None:
                for kb in range(KB):
                    biased(kb, acc, "ln_aff")
                return
            for kb in range(0, KB, 2):
                biased(kb, xh, "op_hi")
                biased(kb + 1, acc, "ln_aff")
                act.wait_ge(S["ln_aff"], KB * L + kb // 2 + 1)
                act.copy(xh[:, kb + 1, :], acc[:, kb + 1, :]).then_inc(S["op_hi"], 1)
            for kb in range(0, KB, 2):
                act.wait_ge(S["op_lo"], (LO_CONV if L == 0 else LO_FF2) - HB + kb // 2 + 1)
                biased(kb, acc, "ln_aff")

        def split_lo(eng, ops, blocks, sem):
            for kb in blocks:
                eng.wait_ge(S["op_hi"], ops + kb + 1)
                eng.tensor_tensor(xl[:, kb, :], acc[:, kb, :], xh[:, kb, :].bitcast(F32),
                                  ALU.subtract).then_inc(S[sem], 1)

        def ff_sp(sp, f):
            base = (W_FF1, W_FF2)[f]
            for k in range(4):
                col = (k // 2) * P + (k % 2) * F
                load_tile(sp, 0, base + k, up_w[f][:, :, col:col + P])
            with sp.Fori(0, FG - 1) as g:
                for k in range(4):
                    load_tile(sp, g * 6, base + 4 + k,
                              up_w[f][:, :, bass.ds(g * (2 * P) + (2 * P + (k // 2) * P + (k % 2) * F), P)])
                for k in range(2):
                    load_tile(sp, g * 6, base + 8 + k, down_w[f][bass.ds(g * (2 * P) + k * P, P), :])
            for k in range(2):
                load_tile(sp, 0, base + 64 + k, down_w[f][(FT - 2 + k) * P:(FT - 1 + k) * P, :])

        def ff_pe(pe, f):
            base = (W_FF1, W_FF2)[f]
            wh, wl = WH[base]
            gh, gl = GH[f]
            t0, y0 = FT * f, KB + (KB * FG + KB) * f
            if f == 0:
                pe.wait_ge(S["op_lo"], LO_FF1)

            def up(g, gc, n, nc_, r):
                for t in range(2):
                    pe.wait_ge(S["w_split"], n + (nc_ + 2 * t + 1))
                    pe.wait_ge(S["silu_done"], g * 2 + (2 * gc + t0 + t))
                    if t == 0 and gc > 0:
                        pe.wait_ge(S["acc_done"], g * 8 + seen(8 * gc + y0 - 9))
                    first = f == 1 and gc == 0 and t == 0
                    linear(pe, base, (r + 2 * t) % 4, 0, S["w_used"], "ff2" if first else None)
                    pe.wait_ge(S["w_split"], n + (nc_ + 2 * t + 2))
                    pe.wait_ge(S["prod_done"], g * 2 + (2 * gc + t0 + t))
                    if t == 0 and gc > 0:
                        pe.wait_ge(S["acc_done"], g * 8 + seen(8 * gc + y0 - 8))
                    linear(pe, base, (r + 2 * t + 1) % 4, 1, S["w_used"])

            def down(g, gc, n, nc_, r, par, last=False):
                pe.wait_ge(S["w_split"], n + (nc_ + 2))
                pe.wait_ge(S["prod_lo"], g * 2 + (2 * gc + t0 + 2))
                for d in range(KB):
                    if d < 2:
                        pe.wait_ge(S[("silu_done", "prod_done")[d]],
                                   g * 2 + (2 * gc + t0 + (2 if last else 4)))
                        if last:
                            pe.wait_ge(S["acc_done"], g * 8 + seen(8 * gc + y0 + d - 1))
                    else:
                        pe.wait_ge(S["acc_done"], g * 8 + seen(8 * gc + y0 + d - 1))
                    for c in range(3):
                        for k in range(2):
                            for i, (w, x) in enumerate(((wh, gh), (wh, gl), (wl, gh))):
                                mm = pe.matmul(ps[:, 3 * (d % 2) + c, 0:CH], w[:, (r + k) % 4, d * P:(d + 1) * P],
                                               x[:, 2 * par + k, c * CH:(c + 1) * CH],
                                               start=(k == 0 and i == 0), stop=(k == 1 and i == 2))
                    mm.then_inc(S["down_out"], 1) if d < KB - 1 else mm.then_inc(S["w_used"], 2)

            up(0, 0, 0, base, 0)
            with pe.Fori(0, FG - 2, 2) as g:
                for u in range(2):
                    up(g, u + 1, g * 6, base + 4 + 6 * u, 2 * u)
                    down(g, u, g * 6, base + 8 + 6 * u, 2 * u, u)
            down(0, FG - 1, 0, base + 64, 0, 0, last=True)

        def ff_act(act, f):
            base = (W_FF1, W_FF2)[f]
            gh = GH[f][0]
            t0 = FT * f

            def hidden(g, gc, n, nc_, par):
                for t in range(2):
                    act.wait_ge(S["w_used"], n + (nc_ + 2 * t + 1))
                    if gc > 0:
                        act.wait_ge(S["prod_done"], g * 2 + (2 * gc + t0 + t - 1))
                    act.activation(tri(tmp[:, t, :]), pset(0), ACT.Silu).then_inc(S["silu_done"], 1)
                    act.wait_ge(S["prod_done"], g * 2 + (2 * gc + t0 + t + 1))
                    if gc > 0:
                        act.wait_ge(S["w_used"], n + nc_)
                    act.copy(gh[:, 2 * par + t, :], tmp[:, 2 + t, :]).then_inc(S["prod_hi"], 1)

            hidden(0, 0, 0, base, 0)
            with act.Fori(0, FG - 2, 2) as g:
                for u in range(2):
                    hidden(g, u + 1, g * 6, base + 4 + 6 * u, 1 - u)

        def ff_dve(dve, f):
            base = (W_FF1, W_FF2)[f]
            gh, gl = GH[f]
            t0, y0, d0 = FT * f, KB + (KB * FG + KB) * f, (KB - 1) * FG * f

            def hidden(g, gc, n, nc_, par):
                for t in range(2):
                    dve.wait_ge(S["w_used"], n + (nc_ + 2 * t + 2))
                    dve.wait_ge(S["silu_done"], g * 2 + (2 * gc + t0 + t + 1))
                    if gc > 0:
                        dve.wait_ge(S["prod_hi"], g * 2 + (2 * gc + t0 + t - 1))
                    dve.scalar_tensor_tensor(out=tri(tmp[:, 2 + t, :]), in0=tri(tmp[:, t, :]), scalar=0.5,
                                             in1=pset(1), op0=ALU.mult, op1=ALU.mult) \
                        .then_inc(S["prod_done"], 1)
                    dve.wait_ge(S["prod_hi"], g * 2 + (2 * gc + t0 + t + 1))
                    dve.tensor_tensor(gl[:, 2 * par + t, :], tmp[:, 2 + t, :],
                                      gh[:, 2 * par + t, :].bitcast(F32), ALU.subtract) \
                        .then_inc(S["prod_lo"], 1)

            def add(g, gc, n):
                for d in range(KB):
                    if d < KB - 1:
                        dve.wait_ge(S["down_out"], g * 7 + (7 * gc + d0 + d + 1))
                    else:
                        dve.wait_ge(S["w_used"], n)
                    dve.wait_ge(S["acc_done"], g * 8 + seen(8 * gc + y0 + d - 7))
                    dve.tensor_tensor(tri(acc[:, d, :]), tri(acc[:, d, :]), pset(d % 2), ALU.add) \
                        .then_inc(S["acc_done"], 1)

            hidden(0, 0, 0, base, 0)
            with dve.Fori(0, FG - 2, 2) as g:
                for u in range(2):
                    hidden(g, u + 1, g * 6, base + 4 + 6 * u, 1 - u)
                    add(g, u, g * 6 + (base + 10 + 6 * u))
            add(0, FG - 1, base + 66)

        def cv_sp(sp):
            with sp.Fori(0, KB) as m:
                for k, col in enumerate((4 * D, 3 * D, 5 * D, 6 * D)):
                    load_tile(sp, m * 4, W_CONV + k, in_w[:, :, bass.ds(m * P + col, P)])

        def side_prod(j):
            return (tmp[:, 3, 0:SEQ], prod1[:, :])[j % 2]

        def cv_pool(pool):
            for k in range(4):
                if k == 2:
                    split_lo(pool, HI_FF1, range(1, KB, 2), "op_lo_odd")
                split_tile(pool, whc, wlc, 0, W_CONV + k, k, None)
            with pool.Fori(0, KB - 1) as m:
                for k in range(4):
                    split_tile(pool, whc, wlc, m * 4, W_CONV + 4 + k, k, m * 4 + (W_CONV + k + 1))
                    side_sums(pool, m, 0, ((), (1, 2, 3), (4, 5, 6, 7), (8,))[k])
            side_sums(pool, 0, KB - 1, range(1, SIDE))

        def side_sums(pool, m, dm, taps):
            for j in taps:
                pool.wait_ge(S["side_prod"], m * SIDE + seen(dm * SIDE + j + 1))
                if j == 1:
                    pool.wait_ge(S["tap_done"], m * TAPS + seen(dm * TAPS))
                else:
                    pool.wait_ge(S["side_sum"], m * (SIDE - 1) + seen(dm * (SIDE - 1) + j - 1))
                pool.tensor_tensor(side[:, :], side_prod(0) if j == 1 else side[:, :], side_prod(j), ALU.add) \
                    .then_inc(S["side_sum"], 1)

        def side_products(act, m, taps):
            for j in taps:
                if j >= 2:
                    act.wait_ge(S["side_sum"], m * (SIDE - 1) + seen(max(j - 2, 1)))
                else:
                    act.wait_ge(S["side_sum"], seen(m * (SIDE - 1)))
                act.activation(side_prod(j), glu[:, MAIN + j:MAIN + j + SEQ], ACT.Identity,
                               scale=wm[:, MAIN + j:MAIN + j + 1]).then_inc(S["side_prod"], 1)

        def hist_pe(pe):
            pe.wait_ge(S["hist_in"], 16)
            n = DB * HIST // 2
            for m in range(KB):
                if m >= 2:
                    pe.wait_ge(S["hist_kept"], m - 1)
                for j in range(2):
                    mm = pe.transpose(ps[:, 6 + m % 2, j * n:(j + 1) * n], tmp[0:n, 2 + j, m * P:(m + 1) * P],
                                      ident[0:n, 0:n])
                mm.then_inc(S["hist_turned"], 1)

        def cv_pe(pe):
            pe.wait_ge(S["hist_kept"], KB)
            with pe.Fori(0, KB) as m:
                for k, (sem, add) in enumerate((("siga_done", 0), ("sigb_done", 0), ("csig_done", 1), ("glu_done", 1))):
                    pe.wait_ge(S["w_split"], m * 4 + (W_CONV + k + 1))
                    pe.wait_ge(S[sem], m + seen(add))
                    linear(pe, W_CONV, k, k % 2, S["w_used"], "conv" if k == 0 else None)
                pe.wait_ge(S["glu_done"], m + seen(1))
                pe.wait_ge(S["tail_kept"], seen(m))
                pe.transpose(ps[:, 6, 0:P], glu[:, SEQ:SEQ + P], ident[:, :]).then_inc(S["tail_turned"], 1)

        def cv_act(act):
            with act.Fori(0, KB) as m:
                act.wait_ge(S["w_used"], m * 4 + (W_CONV + 1))
                act.wait_ge(S["glu_done"], seen(m))
                act.activation(tri(tmp[:, 0, :]), pset(0), ACT.Sigmoid).then_inc(S["csig_done"], 1)
                act.wait_ge(S["glu_done"], m + seen(1))
                side_products(act, m, range(0, 4))
                for k, (sem, dst) in enumerate((("siga", sig_a_d), ("sigb", sig_b_d))):
                    act.wait_ge(S["w_used"], m * 4 + (W_CONV + 3 + k))
                    act.wait_ge(S[sem + "_saved"], seen(m * 16))
                    act.activation(tri(tmp[:, 1 + k, :]), pset(k), ACT.Sigmoid,
                                   bias=bgate[:, bass.ds(m + k * KB, 1)]).then_inc(S[sem + "_done"], 1)
                    act.wait_ge(S[sem + "_done"], m + seen(1))
                    act.dma_start(dst[bass.ds(m, 1), :, :].rearrange("a p t -> (a p) t"), tmp[:, 1 + k, :]) \
                        .then_inc(S[sem + "_saved"], 16)
                    if k == 0:
                        side_products(act, m, range(4, SIDE))
                act.wait_ge(S["tail_turned"], m + seen(1))
                act.copy(tail[:, bass.ds(m * P, P)], ps[0:HIST + NS, 6, 0:P]).then_inc(S["tail_kept"], 1)
            act.wait_ge(S["tail_kept"], seen(KB))
            act.dma_start(O["new_conv_p"].rearrange("a b i c -> (a b i) c"), tail[0:HIST, :]) \
                .then_inc(S["tail_saved"], 16)
            for b in range(DB):
                act.dma_start(O["new_conv_s"][0, b, HIST - DQ:HIST, :], tail[HIST + DQ * b:HIST + DQ * (b + 1), :]) \
                    .then_inc(S["tail_saved"], 16)

        def cv_dve(dve):
            dve.wait_ge(S["w_used"], W_CONV)
            dve.memset(glu[:, 0:HIST], 0.0).then_inc(S["pad_set"], 1)
            dve.memset(glu[:, HIST + T:], 0.0).then_inc(S["pad_set"], 1)
            dve.memset(csum[:, :], 0.0).then_inc(S["pad_set"], 1)

        def hist_dve(dve):
            for m in range(KB):
                dve.wait_ge(S["hist_turned"], m + 1)
                dve.tensor_copy(hist[:, m, :], ps[:, 6 + m % 2, 0:DB * HIST]).then_inc(S["hist_kept"], 1)

        def tap_place(j, q):
            return 4 + (3 * j + q + 1 if j < MAIN else 3 * MAIN + j - MAIN + 1)

        def cv_dve_main(dve):
            dve.wait_ge(S["hist_kept"], KB)
            dve.wait_ge(S["pad_set"], 3)
            with dve.Fori(0, KB) as m:
                dve.wait_ge(S["tap_done"], seen(m * TAPS))
                dve.tensor_copy(wm[:, 0:CW], wdw[:, bass.ds(m, 1), :].rearrange("p a w -> p (a w)")) \
                    .then_inc(S["tap_done"], 1)
                dve.tensor_copy(wm[:, CW:CW + 1], bdw[:, bass.ds(m, 1)]).then_inc(S["tap_done"], 1)
                dve.tensor_copy(ext[:, :, 0:HIST], hist[:, bass.ds(m, 1), :].rearrange("p a (b i) -> p (a b) i", b=DB)) \
                    .then_inc(S["tap_done"], 1)
                dve.wait_ge(S["w_used"], m * 4 + (W_CONV + 2))
                dve.wait_ge(S["csig_done"], m + seen(1))
                dve.wait_ge(S["tail_turned"], seen(m))
                dve.wait_ge(S["side_prod"], seen(m * SIDE))
                dve.tensor_tensor(tri(glu[:, HIST:HIST + T]), tri(tmp[:, 0, :]), pset(1), ALU.mult) \
                    .then_inc(S["glu_done"], 1)
                dve.wait_ge(S["glu_done"], m + seen(1))
                dve.tensor_copy(ext[:, :, HIST:HIST + DQ],
                                glu[:, HIST + SEQ:HIST + T].rearrange("p (b q) -> p b q", b=DB)) \
                    .then_inc(S["tap_done"], 1)
                half = SEQ // 2
                for j in range(CW):
                    if j == MAIN:
                        dve.wait_ge(S["x1_saved"], 16 * KB)
                    for q in range(3) if j < MAIN else (2,):
                        dve.wait_ge(S["tap_done"], m * TAPS + seen(tap_place(j - 1, q) if j else 4))
                        if q < 2:
                            src = glu[:, q * half + j:q * half + j + half]
                            old = cbuf[:, q * half:(q + 1) * half]
                        else:
                            src = ext[:, :, j:j + DQ]
                            old = cbuf[:, SEQ:T].rearrange("p (b q) -> p b q", b=DB)
                            new = acc[:, bass.ds(m, 1), SEQ:T].rearrange("p a (b q) -> p (a b) q", b=DB)
                        dst = new if q == 2 and j == CW - 1 else old
                        if j == 0:
                            dve.tensor_scalar(dst, src, wm[:, 0:1], wm[:, CW:CW + 1], ALU.mult, ALU.add) \
                                .then_inc(S["tap_done"], 1)
                        else:
                            dve.scalar_tensor_tensor(out=dst, in0=src, scalar=wm[:, j:j + 1], in1=old,
                                                     op0=ALU.mult, op1=ALU.add).then_inc(S["tap_done"], 1)
                dve.wait_ge(S["tap_done"], m * TAPS + seen(tap_place(MAIN - 1, 1)))
                dve.wait_ge(S["side_sum"], m * (SIDE - 1) + seen(SIDE - 1))
                dve.tensor_tensor(acc[:, bass.ds(m, 1), 0:SEQ].rearrange("p a t -> p (a t)"), cbuf[:, 0:SEQ],
                                  side[:, :], ALU.add).then_inc(S["tap_done"], 1)
                dve.wait_ge(S["tap_done"], m * TAPS + seen(TAPS))
                dve.wait_ge(S["ln_sum"], m + SUMS[0])
                dve.tensor_tensor(csum[:, :], csum[:, :], acc[:, bass.ds(m, 1), :].rearrange("p a t -> p (a t)"),
                                  ALU.add).then_inc(S["ln_sum"], 1)

        def at_sp(sp):
            with sp.Fori(0, KB - 1, 2) as m:
                for u in range(2):
                    for k in range(3):
                        load_tile(sp, m * 3, W_ATT + 3 * u + k, in_w[:, :, bass.ds(m * P + (u * P + k * D), P)])

        k_t, v_t = tmp[:, 0, :], tmp[:, 1, :]

        def zbank(i):
            return i % 6

        def at_pool(pool):
            pool.wait_ge(S["w_used"], W_ATT)
            for k in range(3):
                at_tile(pool, 0, k)
            with pool.Fori(0, KB - 3, 2) as m:
                for dm in range(2):
                    at_pair_pool(pool, m, dm, True)
            at_pair_pool(pool, 0, KB - 2, True)
            at_pair_pool(pool, 0, KB - 1, False)

        def at_tile(pool, m, k):
            split_tile(pool, wha, wla, m * 3, W_ATT + k, k % 2, m * 3 + (W_ATT + k - 1) if k >= 2 else None)

        def at_pair_pool(pool, m, dm, more):
            for j in range(NSTEP):
                if RUN_OPS[j]:
                    off, _ = chain(STEPS[j])
                    h = STEPS[j][2]
                    s = run[:, h, off:512]
                    pool.wait_ge(S["run_done"], m * RUN_TOTAL + seen(dm * RUN_TOTAL + sum(RUN_OPS[:j + 1])))
                    pool.wait_ge(S["s_ready"], m * NSTEP + (dm * NSTEP + j + 1))
                    pool.tensor_tensor(runh[:, h, off:512], s, one[:, 0:1].to_broadcast([P, 512 - off]), ALU.mult) \
                        .then_inc(S["run_high"], 1)
                    pool.wait_ge(S["run_high"], m * RUN_SPLITS + (dm * RUN_SPLITS + splits_before(j + 1)))
                    pool.tensor_tensor(runl[:, h, off:512], s, runh[:, h, off:512].bitcast(F32), ALU.subtract) \
                        .then_inc(S["run_split"], 1)
                elif more and j == 7:
                    at_tile(pool, m, 3 * dm + 3)
            if more:
                at_tile(pool, m, 3 * dm + 4)
                at_tile(pool, m, 3 * dm + 5)

        def at_linear(pe, m, t, s, c):
            for kb in range(KB):
                for n, (w, x) in enumerate(((wha, xh), (wha, xl), (wla, xh))):
                    mm = pe.matmul(ps[:, 3 * s + c, 0:CH], w[:, t % 2, kb * P:(kb + 1) * P],
                                   x[:, kb, c * CH:(c + 1) * CH],
                                   start=(kb == 0 and n == 0), stop=(kb == KB - 1 and n == 2))
            if c == 2:
                mm.then_inc(S["w_used"], 1)

        def at_pe(pe):
            pe.wait_ge(S["ln_cent"], 2 * KB)
            pe.wait_ge(S["ln_log"], 2)
            pe.wait_ge(S["ln_cent"], 2 * KB)
            pe.wait_ge(S["ln_log"], 2)
            pe.wait_ge(S["w_split"], W_ATT + 1)
            for c in range(3):
                at_linear(pe, 0, 0, 0, c)
            with pe.Fori(0, KB - 3, 2) as m:
                for dm in range(2):
                    at_pair_pe(pe, m, dm, True)
            at_pair_pe(pe, 0, KB - 2, True)
            at_pair_pe(pe, 0, KB - 1, False)

        def at_pair_pe(pe, m, dm, more):
            def count(each, plus):
                return m * each + (dm * each + plus)

            pe.wait_ge(S["a_done"], count(NSTEP, seen(0)))
            pe.wait_ge(S["w_split"], count(3, W_ATT + 2))
            for c in range(3):
                at_linear(pe, m, 3 * dm + 1, 1, c)
            pe.wait_ge(S["w_split"], count(3, W_ATT + 3))
            pe.wait_ge(S["q_hi"], count(1, 1))
            pe.wait_ge(S["q_lo"], count(1, 1))
            for c in range(3):
                at_linear(pe, m, 3 * dm + 2, 0, c)
            pe.wait_ge(S["k_raw"], count(1, 1))
            pe.wait_ge(S["k_lo"], count(1, 1))
            for kb in range(KB):
                pe.transpose(ps[:, 3 + kb // 4, (kb % 4) * P:(kb % 4 + 1) * P], k_t[:, kb * P:(kb + 1) * P], ident[:, :])
            pe.transpose(ps[0:NS, 5, 0:P], k_t[:, SEQ:T], ident[:, :]).then_inc(S["k_turned"], 1)
            for i in range(NSTEP + LAG_OUT):
                if i < NSTEP:
                    c, kb, h = STEPS[i]
                    off, _ = chain(STEPS[i])
                    out = ps[:, zbank(i), off:512]
                    if i == 0:
                        pe.wait_ge(S["v_raw"], count(1, 1))
                    if i == 2:
                        pe.wait_ge(S["o_kept"], count(4, seen(0)))
                        pe.wait_ge(S["k_nat"], count(2, 2))
                        for t in range(KB):
                            pe.transpose(ps[:, 6 + t // 4, (t % 4) * P:(t % 4 + 1) * P],
                                         v_t[:, t * P:(t + 1) * P], ident[:, :])
                        pe.transpose(ps[0:NS, 5, 0:P], v_t[:, SEQ:T], ident[:, :]).then_inc(S["v_turned"], 1)
                    if i == 5:
                        pe.wait_ge(S["v_nat"], count(2, 2))
                    if i >= 6:
                        pe.wait_ge(S["a_done"], count(NSTEP, seen(i - 5)))
                    rows = slice(HD * h, HD * (h + 1))
                    for n, (a, b) in enumerate(((kh, qh), (kh, ql), (kl, qh))):
                        mm = pe.matmul(out, a[rows, kb * P:(kb + 1) * P], b[rows, 512 * c + off:512 * (c + 1)],
                                       start=(n == 0), stop=False, skip_group_check=True)
                    if kb >= 4 * c:
                        mm = pe.matmul(ps[:, zbank(i), off:off + P], identb[:, :], dmask[:, :],
                                       start=False, stop=False, skip_group_check=True)
                    mm.then_inc(S["z_ready"], 1)
                j = i - LAG_SUM
                if 0 <= j < NSTEP:
                    off, before = chain(STEPS[j])
                    h = STEPS[j][2]
                    pe.wait_ge(S["sp_ready"], count(NSTEP, j + 1))
                    if before is not None:
                        pe.wait_ge(S["run_split"], count(RUN_SPLITS, seen(splits_before(j - 1))))
                        for part in (runh, runl):
                            pe.matmul(ps[:, zbank(j), before:512], negones[:, :], part[:, h, before:512],
                                      start=False, stop=False, skip_group_check=True)
                    pe.matmul(ps[:, zbank(j), off:512], negtri[:, :], sp_buf(j)[:, off:512],
                              start=False, stop=True, skip_group_check=True).then_inc(S["s_ready"], 1)
                if more and NSTEP <= i < NSTEP + 3:
                    c = i - NSTEP
                    pe.wait_ge(S["a_done"], count(NSTEP, seen(NSTEP - 5 + c)))
                    if c == 0:
                        pe.wait_ge(S["w_split"], count(3, W_ATT + 4))
                    at_linear(pe, m, 3 * dm + 3, 0, c)
                j = i - LAG_OUT
                if 0 <= j < NSTEP:
                    c, kb, h = STEPS[j]
                    off, before = chain(STEPS[j])
                    if j == 0:
                        pe.wait_ge(S["v_lo"], count(1, seen(1)))
                    if before is None:
                        pe.wait_ge(S["o_kept"], count(4, seen(2 * c)))
                    pe.wait_ge(S["a_lo"], count(NSTEP, seen(j + 1)))
                    for n, (a, b) in enumerate(((vh, ah), (vh, al), (vl, ah))):
                        mm = pe.matmul(ps[:, 6 + h, off:512], a[:, kb, :], b[:, j % 3, off:512],
                                       start=(before is None and n == 0), stop=(kb == 0 and n == 2),
                                       skip_group_check=True)
                    mm.then_inc(S["v_used"], 1)

        def e_buf(i):
            return tmp[:, :, :].rearrange("p a t -> p (a t)")[:, (i % 5) * 512:(i % 5 + 1) * 512]

        def sp_buf(i):
            return tmp[:, :, :].rearrange("p a t -> p (a t)")[:, (5 + i % 3) * 512:(6 + i % 3) * 512]

        def token_major(act, m, n):
            turned, kept, saved = (("k_turned", "k_nat", "k_saved"), ("v_turned", "v_nat", "v_saved"))[n]
            bank = 3 + 3 * n
            act.wait_ge(S[turned], m + 1)
            act.wait_ge(S[saved], seen(m * 32))
            if n:
                act.wait_ge(S["v_lo"], seen(m))
            act.copy(nat[:, n, :, :], ps[:, bank:bank + 2, :].rearrange("p a (b c) -> p (a b) c", b=4)) \
                .then_inc(S[kept], 1)
            act.copy(nat_s[:, n, :], ps[0:NS, 5, 0:P]).then_inc(S[kept], 1)
            act.wait_ge(S[kept], m * 2 + 2)
            act.dma_start(new_p[n][:, :, bass.ds(m * P, P)], nat[:, n, :, :]).then_inc(S[saved], 16)
            act.dma_start(new_s[n][:, bass.ds(m * P, P)], nat_s[:, n, :]).then_inc(S[saved], 16)

        def at_act(act):
            act.wait_ge(S["tail_saved"], 16 * (DB + 1))
            act.wait_ge(S["conv_saved"], 16 * KB)
            nc.scalar.preload_act_table_set("natural_log_exp_and_others")
            with act.Fori(0, KB) as m:
                act.wait_ge(S["w_used"], m * 3 + (W_ATT + 1))
                act.activation(tri(qh[:, :]), pset(0), ACT.Copy, scale=SCALE).then_inc(S["q_hi"], 1)
                act.wait_ge(S["w_used"], m * 3 + (W_ATT + 2))
                act.copy(tri(kh[:, :]), pset(1)).then_inc(S["k_hi"], 1)
                act.wait_ge(S["a_lo"], seen(m * NSTEP))
                act.copy(tri(k_t), pset(1)).then_inc(S["k_raw"], 1)
                act.wait_ge(S["w_used"], m * 3 + (W_ATT + 3))
                act.copy(tri(v_t), pset(0)).then_inc(S["v_raw"], 1)
                token_major(act, m, 0)
                for i in range(NSTEP + LAG_OUT):
                    if i == 2:
                        token_major(act, m, 1)
                        act.copy(vh[:, :, :], nat[:, 1, :, :]).then_inc(S["v_hi"], 1)
                    if i < NSTEP:
                        off, _ = chain(STEPS[i])
                        e = e_buf(i)[:, off:512]
                        act.wait_ge(S["z_capped"], m * NSTEP + (i + 1))
                        act.activation(e, e, ACT.Exp).then_inc(S["e_done"], 1)
                        act.wait_ge(S["e_done"], m * NSTEP + (i + 1))
                        act.activation(e, e, ACT.Ln, bias=1.0).then_inc(S["l_done"], 1)
                    if i in (8 + LAG_OUT, NSTEP + LAG_OUT - 1):
                        c = 0 if i < NSTEP else 1
                        act.wait_ge(S["v_used"], m * NSTEP + (8 if c == 0 else NSTEP))
                        for h in range(2):
                            rows = slice(HD * h, HD * (h + 1))
                            act.copy(acc[rows, bass.ds(m, 1), 512 * c:512 * (c + 1)].rearrange("p a t -> p (a t)"),
                                     ps[rows, 6 + h, :]).then_inc(S["o_kept"], 1)
                    j = i - LAG_SUM
                    if 0 <= j < NSTEP:
                        off, _ = chain(STEPS[j])
                        h = STEPS[j][2]
                        act.wait_ge(S["s_ready"], m * NSTEP + (j + 1))
                        act.activation(e_buf(j)[:, off:512], ps[:, zbank(j), off:512], ACT.Exp,
                                       bias=bias_m[:, h:h + 1]).then_inc(S["a_done"], 1)
                        act.wait_ge(S["a_done"], m * NSTEP + seen(j + 1))
                        if j >= 3:
                            act.wait_ge(S["v_used"], m * NSTEP + (j - 2))
                        act.copy(ah[:, j % 3, off:512], e_buf(j)[:, off:512]).then_inc(S["a_hi"], 1)

        def at_dve(dve):
            with dve.Fori(0, KB) as m:
                dve.wait_ge(S["a_done"], seen(m * NSTEP))
                dve.wait_ge(S["tail_saved"], 16 * (DB + 1))
                dve.tensor_copy(bias_m[:, :], bias_p[:, bass.ds(m * 2, 2)]).then_inc(S["bias_set"], 1)
                dve.wait_ge(S["q_hi"], m + 1)
                dve.tensor_scalar(qs[:, bass.ds(m, 1), :].rearrange("p a t -> p (a t)"), ps[:, 2, CH - NS:CH],
                                  SCALE, None, ALU.mult).then_inc(S["s_row"], 1)
                dve.scalar_tensor_tensor(out=tri(ql[:, :]), in0=pset(0), scalar=SCALE,
                                         in1=tri(qh[:, :].bitcast(F32)), op0=ALU.mult, op1=ALU.subtract) \
                    .then_inc(S["q_lo"], 1)
                dve.wait_ge(S["k_raw"], m + 1)
                dve.tensor_copy(ks[:, bass.ds(m, 1), :].rearrange("p a t -> p (a t)"), ps[:, 5, CH - NS:CH]) \
                    .then_inc(S["s_row"], 1)
                dve.tensor_tensor(tri(kl[:, :]), pset(1), tri(kh[:, :].bitcast(F32)), ALU.subtract) \
                    .then_inc(S["k_lo"], 1)
                dve.wait_ge(S["bias_set"], m + 1)
                for i in range(NSTEP + LAG_OUT):
                    if i == 4:
                        dve.wait_ge(S["v_hi"], m + 1)
                        dve.tensor_tensor(vl[:, :, :], nat[:, 1, :, :], vh[:, :, :].bitcast(F32), ALU.subtract) \
                            .then_inc(S["v_lo"], 1)
                    if i < NSTEP:
                        off, _ = chain(STEPS[i])
                        h = STEPS[i][2]
                        dve.wait_ge(S["z_ready"], m * NSTEP + (i + 1))
                        if i >= 5:
                            dve.wait_ge(S["a_hi"], m * NSTEP + (i - 4))
                            dve.wait_ge(S["a_lo"], m * NSTEP + seen(i - 4))
                        dve.tensor_scalar(e_buf(i)[:, off:512], ps[:, zbank(i), off:512], bias_m[:, h:h + 1],
                                          ZCAP, ALU.add, ALU.min).then_inc(S["z_capped"], 1)
                    j = i - LAG_SUM
                    if 0 <= j < NSTEP and run_ops(STEPS[j]):
                        h = STEPS[j][2]
                        dve.wait_ge(S["sp_ready"], m * NSTEP + (j + 1))
                        dve.wait_ge(S["run_split"], m * RUN_SPLITS + seen(splits_before(j - 1)))
                        dve.wait_ge(S["run_done"], m * RUN_TOTAL + seen(sum(RUN_OPS[:j])))
                        for lo, hi, adds in run_ops(STEPS[j]):
                            s = sp_buf(j)[:, lo:hi]
                            r = run[:, h, lo:hi]
                            ins = dve.tensor_tensor(r, r, s, ALU.add) if adds else dve.tensor_copy(r, s)
                            ins.then_inc(S["run_done"], 1)
                    j = i - 1
                    if 0 <= j < NSTEP:
                        off, _ = chain(STEPS[j])
                        h = STEPS[j][2]
                        dve.wait_ge(S["l_done"], m * NSTEP + (j + 1))
                        if j >= 3:
                            dve.wait_ge(S["s_ready"], m * NSTEP + (j - 2))
                            dve.wait_ge(S["run_done"], m * RUN_TOTAL + seen(sum(RUN_OPS[:j - 2])))
                        dve.scalar_tensor_tensor(out=sp_buf(j)[:, off:512], in0=ps[:, zbank(j), off:512],
                                                 scalar=bias_m[:, h:h + 1], in1=e_buf(j)[:, off:512],
                                                 op0=ALU.add, op1=ALU.max).then_inc(S["sp_ready"], 1)
                    j = i - LAG_SUM - 1
                    if 0 <= j < NSTEP:
                        off, _ = chain(STEPS[j])
                        dve.wait_ge(S["a_hi"], m * NSTEP + (j + 1))
                        if j >= 3:
                            dve.wait_ge(S["v_used"], m * NSTEP + (j - 2))
                        dve.tensor_tensor(al[:, j % 3, off:512], e_buf(j)[:, off:512],
                                          ah[:, j % 3, off:512].bitcast(F32), ALU.subtract) \
                            .then_inc(S["a_lo"], 1)

        NP = 2 * PAGES
        GCOLS = KB * 2 * P

        def page_slot(k):
            return wraw[:, k % 8, :] if k % 8 < 2 else pages[:, k % 8 - 2, :]

        def flat(t):
            return t[:, :, :].rearrange("p a t -> p (a t)")

        def kt_group(t, g):
            return flat(t)[:, (g % 2) * GCOLS:(g % 2 + 1) * GCOLS]

        def kt_block(t, k):
            return kt_group(t, k // 2).rearrange("p (e n) -> p e n", e=KB)[:, :, (k % 2) * P:(k % 2 + 1) * P]

        def kt_psum(k):
            return ps[:, 2 * (k % 2):2 * (k % 2) + 2, :].rearrange("p a (b c) -> p (a b) c", b=4)

        def v_slot(t, k):
            return flat(t)[:, 2 * GCOLS + (k % 4) * D:2 * GCOLS + (k % 4 + 1) * D]

        def out_banks(b):
            return 6 - 2 * b

        def page_count(k):
            return (k // 8 + 1) * 16

        def load_page(sp, i, d, kv, k):
            page = sp.value_load(pt_sb[0:1, bass.ds(i * NP + (d * NP + k), 1)], min_val=0, max_val=POOL - 1)
            return page_rows[kv][bass.ds(page, 1), :, :].rearrange("a p c -> (a p) c")

        def k_pages_sp(sp, i, d, lo, hi):
            for k in range(lo, hi):
                src = load_page(sp, i, d, 0, k)
                if k >= 8:
                    sp.wait_ge(S["pk_turned"], i * NP + (d * NP + k - 7))
                elif d:
                    sp.wait_ge(S["pv_lo"], i * NP + (k + 9))
                sp.dma_start(page_slot(k), src).then_inc(S[f"page_in{k % 8}"], 16)

        def v_pages_sp(sp, i, d):
            for k in range(NP):
                src = load_page(sp, i, d, 1, k)
                if k >= 8:
                    sp.wait_ge(S["pv_lo"], i * NP + (d * NP + NP + k - 7))
                elif d:
                    sp.wait_ge(S["pv_lo"], i * NP + (d * NP + k + 9))
                else:
                    sp.wait_ge(S["pk_turned"], i * NP + (NP + k + 9))
                sp.dma_start(page_slot(k), src).then_inc(S[f"page_in{k % 8}"], 16)

        def sa_sp(sp):
            sp.wait_ge(S["w_used"], W_OUT)
            k_pages_sp(sp, 0, 0, 0, 6)
            sp.wait_ge(S["s_ready"], NSTEP * KB)
            sp.wait_ge(S["v_used"], NSTEP * KB)
            sp.wait_ge(S["a_lo"], seen(NSTEP * KB))
            sp.wait_ge(S["o_kept"], seen(4 * KB))
            sp.wait_ge(S["v_saved"], seen(32 * KB))
            sp.wait_ge(S["k_saved"], seen(32 * KB))
            sp.dma_start(vn_raw[:, :], new_s[1]).then_inc(S["sconst_in"], 16)
            sp.dma_start(mbd[:, :], A["c_mbd"]).then_inc(S["sconst_in"], 16)
            sp.dma_start(sel[:, :], A["c_sel"]).then_inc(S["sconst_in"], 16)
            sp.dma_start(smask[:, :, :], A["c_smask"]).then_inc(S["sconst_in"], 16)
            k_pages_sp(sp, 0, 0, 6, NP)
            sp.wait_ge(S["pk_turned"], NP)
            with sp.Fori(0, DB // 2 - 1) as i:
                k_pages_sp(sp, i, 1, 0, NP)
                v_pages_sp(sp, i, 0)
            v_pages_sp(sp, 0, DB // 2 - 1)

        def k_phase_pe(pe, i, d):
            for g in range(PAGES + 1):
                if g < PAGES:
                    for u in range(2):
                        k = 2 * g + u
                        pe.wait_ge(S[f"page_in{k % 8}"], i * 64 + (d * 32 + page_count(k)))
                        pe.wait_ge(S["pk_lo"], i * NP + (d * NP + max(k - 1, 0)))
                        if g == 0 and d:
                            pe.wait_ge(S["sa_lo"], i * 2 + 2)
                            pe.wait_ge(S["so_kept"], seen(i))
                        for e in range(KB):
                            mm = pe.transpose(ps[:, 2 * u + e // 4, (e % 4) * P:(e % 4 + 1) * P],
                                              page_slot(k)[:, e * P:(e + 1) * P], ident[:, :])
                        mm.then_inc(S["pk_turned"], 1)
                if g:
                    q = g - 1
                    pe.wait_ge(S["pk_lo"], i * NP + (d * NP + 2 * g))
                    pe.wait_ge(S["sz_kept"], i * 9 + (d * 9 + max(q - 1, 0)))
                    if q == 0:
                        pe.wait_ge(S["qb_lo"], i * NP + (d * NP + NP))
                    for e in range(KB):
                        for n, (a, b) in enumerate(((qbh, xh), (qbh, xl), (qbl, xh))):
                            mm = pe.matmul(ps[:, 4 + q % 2, 0:2 * P], a[:, e, :],
                                           kt_group(b, q)[:, e * 2 * P:(e + 1) * 2 * P],
                                           start=(e == 0 and n == 0), stop=(e == KB - 1 and n == 2))
                    mm.then_inc(S["sz_out"], 1)
            if d == 0:
                pe.wait_ge(S["sconst_in"], 64)
                pe.wait_ge(S["new_lo"], 1)
                pe.wait_ge(S["pv_lo"], NP)
            pe.wait_ge(S["sz_kept"], i * 9 + (d * 9 + 7))
            for e in range(KB):
                for n, (a, b) in enumerate(((qbh, ksh), (qbh, ksl), (qbl, ksh))):
                    pe.matmul(ps[:, 4, 0:NS], a[:, e, :], b[:, e, :], start=(e == 0 and n == 0), stop=False)
            mask = smask[:, bass.ds(i + d, 1), :].rearrange("p a n -> p (a n)") if d else smask[:, 0, :]
            pe.matmul(ps[:, 4, 0:NS], ident[:, :], mask, start=False, stop=True).then_inc(S["sz_out"], 1)

        def turn_weights_pe(pe, i, d):
            pe.wait_ge(S["s_a"], i + (d + 1))
            for kb in range(PAGES):
                pe.transpose(ps[:, kb // 4, (kb % 4) * P:(kb % 4 + 1) * P], tmp[:, 1, kb * P:(kb + 1) * P], ident[:, :])
            pe.transpose(ps[0:NS, 2, 0:P], tmp[:, 1, PAST:KEYS], ident[:, :]).then_inc(S["sa_turned"], 1)

        def v_phase_pe(pe, i, d):
            pe.wait_ge(S["sa_lo"], i * 2 + (d * 2 + 2))
            for b in range(2):
                bank = out_banks(b)
                if b == 0:
                    pe.wait_ge(S["so_mask"], i * 2 + seen(d * 2))
                else:
                    pe.wait_ge(S["sz_kept"], i * 9 + (9 * min(d + 2, DB // 2)))
                for pg in range(PAGES + 1):
                    new = pg == PAGES
                    k = PAGES * b + pg
                    if not new:
                        pe.wait_ge(S["pv_lo"], i * NP + (d * NP + NP + k + 1))
                    r = slice(0, NS) if new else slice(0, P)
                    for n2 in range(2):
                        c = slice(n2 * 512, (n2 + 1) * 512)
                        vv = (vnh[:, c], vnl[:, c]) if new else (v_slot(xh, k)[:, c], v_slot(xl, k)[:, c])
                        for n, (a, x) in enumerate(((ath, vv[0]), (ath, vv[1]), (atl, vv[0]))):
                            mm = pe.matmul(ps[:, bank + n2, :], a[r, pg, :], x,
                                           start=(pg == 0 and n == 0), stop=(new and n == 2))
                    mm.then_inc(S["so_out" if new else "pv_used"], 1)

        def turn_out_pe(pe, i, d):
            pe.wait_ge(S["so_mask"], i * 2 + seen(d * 2 + 2))
            pe.wait_ge(S["so_kept"], i + seen(d))
            for e in range(KB):
                mm = pe.matmul(ps[:, 3, e * 2 * DQ:(e + 1) * 2 * DQ], om[:, e * P:(e + 1) * P], sel[:, :],
                               start=True, stop=True)
            mm.then_inc(S["so_turned"], 1)

        def sa_pe(pe):
            pe.wait_ge(S["a_done"], seen(NSTEP * KB))
            pe.wait_ge(S["o_kept"], seen(4 * KB))
            k_phase_pe(pe, 0, 0)
            turn_weights_pe(pe, 0, 0)
            with pe.Fori(0, DB // 2 - 1) as i:
                k_phase_pe(pe, i, 1)
                v_phase_pe(pe, i, 0)
                turn_weights_pe(pe, i, 1)
                turn_out_pe(pe, i, 0)
            v_phase_pe(pe, 0, DB // 2 - 1)
            turn_out_pe(pe, 0, DB // 2 - 1)

        def k_phase_act(act, i, d):
            for k in range(NP):
                if d == 0 and k == 8:
                    act.wait_ge(S["sconst_in"], 64)
                    act.wait_ge(S["s_zero"], 2)
                    for dst, src in ((ksh, ks), (vnh, vn_raw)):
                        act.copy(dst[:], src[:]).then_inc(S["new_hi"], 1)
                act.wait_ge(S["pk_turned"], i * NP + (d * NP + k + 1))
                act.wait_ge(S["sz_out"], i * 9 + (d * 9 + max(k // 2 - 1, 0)))
                act.copy(kt_block(xh, k), kt_psum(k)).then_inc(S["pk_hi"], 1)

        def exp_act(act, i, d):
            act.wait_ge(S["s_capped"], i + (d + 1))
            act.activation(tmp[:, 1, :], tmp[:, 1, :], ACT.Exp).then_inc(S["s_exp"], 1)
            act.wait_ge(S["s_exp"], i + (d + 1))
            act.activation(tmp[:, 1, :], tmp[:, 1, :], ACT.Ln, bias=1.0).then_inc(S["s_ln"], 1)

        def weights_act(act, i, d):
            act.wait_ge(S["s_log"], i + (d + 1))
            act.activation(tmp[:, 1, :], tmp[:, 0, :], ACT.Exp).then_inc(S["s_a"], 1)

        def turned_act(act, i, d):
            act.wait_ge(S["sa_turned"], i + (d + 1))
            act.wait_ge(S["so_out"], i * 2 + d * 2)
            act.copy(ath[:, 0:PAGES, :], ps[:, 0:2, :].rearrange("p a (b c) -> p (a b) c", b=4)).then_inc(S["sa_hi"], 1)
            act.copy(ath[0:NS, PAGES, :], ps[0:NS, 2, 0:P]).then_inc(S["sa_hi"], 1)

        def v_phase_act(act, i, d, first_page):
            for k in range(NP):
                if d == 0 and k == 2:
                    exp_act(act, i, 1)
                if d == 0 and k == 8:
                    weights_act(act, i, 1)
                act.wait_ge(S["pv_used"], i * NP + seen(d * NP + max(k - 3, 0)))
                act.wait_ge(S[f"page_in{k % 8}"], i * 64 + (first_page + page_count(k)))
                act.copy(v_slot(xh, k), page_slot(k)).then_inc(S["pv_hi"], 1)

        def keep_out_act(act, i, d):
            act.wait_ge(S["so_turned"], i + seen(d + 1))
            src = ps[:, 3, 0:NS * 2].rearrange("p (e n) -> p e n", e=KB)
            act.copy(acc[:, :, bass.ds(i * (2 * DQ) + (d * 2 * DQ + SEQ), 2 * DQ)], src).then_inc(S["so_kept"], 1)

        def sa_act(act):
            k_phase_act(act, 0, 0)
            exp_act(act, 0, 0)
            weights_act(act, 0, 0)
            turned_act(act, 0, 0)
            with act.Fori(0, DB // 2 - 1) as i:
                k_phase_act(act, i, 1)
                v_phase_act(act, i, 0, 64)
                turned_act(act, i, 1)
                keep_out_act(act, i, 0)
            v_phase_act(act, 0, DB // 2 - 1, 7 * 32)
            keep_out_act(act, 0, DB // 2 - 1)

        def qb_block(t, e, h):
            rows = slice(HD * h, HD * (h + 1))
            return t[rows, e, :].rearrange("p (b c) -> p b c", b=2)[:, :, DQ * (2 * e + h):DQ * (2 * e + h + 1)]

        def qs_block(i, e, rows):
            return qs[rows, e, i * (2 * DQ):(i + 1) * (2 * DQ)].rearrange("p (b q) -> p b q", b=2)

        def sa_pool(pool):
            pool.wait_ge(S["s_zero"], 2)
            pool.wait_ge(S["s_row"], 2 * KB)
            for i in range(DB // 2):
                pool.wait_ge(S["sz_out"], i * 9)
                for e in range(KB):
                    for h in range(2):
                        rows = slice(HD * h, HD * (h + 1))
                        ones = one[rows, 0:1].to_broadcast([HD, 2 * DQ]).rearrange("p (b q) -> p b q", b=2)
                        pool.tensor_tensor(qb_block(qbh, e, h), qs_block(i, e, rows), ones, ALU.mult) \
                            .then_inc(S["qb_hi"], 1)
                for e in range(KB):
                    for h in range(2):
                        rows = slice(HD * h, HD * (h + 1))
                        pool.wait_ge(S["qb_hi"], i * NP + (2 * e + h + 1))
                        pool.tensor_tensor(qb_block(qbl, e, h), qs_block(i, e, rows), qb_block(qbh, e, h).bitcast(F32),
                                           ALU.subtract).then_inc(S["qb_lo"], 1)

        def k_phase_dve(dve, i, d):
            for g in range(PAGES + 1):
                if d == 0 and g == 5:
                    dve.wait_ge(S["sconst_in"], 64)
                    dve.wait_ge(S["new_hi"], 2)
                    dve.tensor_tensor(ksl[:], ks[:], ksh[:].bitcast(F32), ALU.subtract).then_inc(S["new_lo"], 1)
                    dve.tensor_tensor(vnl[:], vn_raw[:], vnh[:].bitcast(F32), ALU.subtract).then_inc(S["pv_lo"], NP)
                if g < PAGES:
                    for k in (2 * g, 2 * g + 1):
                        dve.wait_ge(S["pk_hi"], i * NP + (d * NP + k + 1))
                        dve.tensor_tensor(kt_block(xl, k), kt_psum(k), kt_block(xh, k).bitcast(F32),
                                          ALU.subtract).then_inc(S["pk_lo"], 1)
                if g:
                    q = g - 1
                    rows = slice(64 * (q // 4), 64 * (q // 4) + 64)
                    dve.wait_ge(S["sz_out"], i * 9 + (d * 9 + g))
                    if q == 0:
                        dve.wait_ge(S["s_a"], i + d)
                    dve.tensor_scalar(tmp[rows, 0, (q % 4) * 2 * P:(q % 4 + 1) * 2 * P], ps[rows, 4 + q % 2, 0:2 * P],
                                      bias_s[rows, 0:1], None, ALU.add).then_inc(S["sz_kept"], 1)
            dve.wait_ge(S["sz_out"], i * 9 + (d * 9 + 9))
            dve.tensor_scalar(tmp[:, 0, PAST:KEYS], ps[:, 4, 0:NS], bias_s[:, 0:1], None, ALU.add) \
                .then_inc(S["sz_kept"], 1)

        def softmax_dve(dve, i, d, step):
            if step == 0:
                dve.wait_ge(S["sz_kept"], i * 9 + (d * 9 + 9))
                dve.wait_ge(S["sa_turned"], i + d)
                dve.tensor_scalar(tmp[:, 1, :], tmp[:, 0, :], ZCAP, None, ALU.min).then_inc(S["s_capped"], 1)
            elif step == 1:
                dve.wait_ge(S["s_ln"], i + (d + 1))
                dve.tensor_tensor(tmp[:, 1, :], tmp[:, 0, :], tmp[:, 1, :], ALU.max).then_inc(S["s_chain"], 1)
            elif step == 2:
                dve.wait_ge(S["s_chain"], i * 2 + (d * 2 + 1))
                dve.tensor_tensor_scan(out=tmp[:, 2, ::-1], data0=tmp[:, 1, ::-1], data1=tmp[:, 1, ::-1],
                                       initial=0.0, op0=ALU.add, op1=ALU.bypass).then_inc(S["s_chain"], 1)
            else:
                dve.wait_ge(S["s_chain"], i * 2 + (d * 2 + 2))
                dve.tensor_tensor(tmp[:, 0, :], tmp[:, 0, :], tmp[:, 2, :], ALU.subtract).then_inc(S["s_log"], 1)

        def turned_dve(dve, i, d):
            dve.wait_ge(S["sa_hi"], i * 2 + (d * 2 + 2))
            dve.tensor_tensor(atl[:, 0:PAGES, :], ps[:, 0:2, :].rearrange("p a (b c) -> p (a b) c", b=4),
                              ath[:, 0:PAGES, :].bitcast(F32), ALU.subtract).then_inc(S["sa_lo"], 1)
            dve.tensor_tensor(atl[0:NS, PAGES, :], ps[0:NS, 2, 0:P], ath[0:NS, PAGES, :].bitcast(F32),
                              ALU.subtract).then_inc(S["sa_lo"], 1)

        def mask_out_dve(dve, i, d, b):
            rows = slice(64 * b, 64 * b + 64)
            dve.wait_ge(S["so_out"], i * 2 + (d * 2 + b + 1))
            dve.wait_ge(S["so_turned"], i + seen(d))
            dve.tensor_tensor(om[rows, :], ps[rows, out_banks(b):out_banks(b) + 2, :].rearrange("p a c -> p (a c)"),
                              mbd[rows, :], ALU.mult).then_inc(S["so_mask"], 1)

        def v_phase_dve(dve, i, d):
            for k in range(NP):
                if d == 0 and k in (0, 4, 5, 6):
                    softmax_dve(dve, i, 1, (0, 4, 5, 6).index(k))
                if k == 12:
                    mask_out_dve(dve, i, d, 0)
                dve.wait_ge(S["pv_hi"], i * NP + (d * NP + k + 1))
                dve.tensor_tensor(v_slot(xl, k), page_slot(k), v_slot(xh, k).bitcast(F32), ALU.subtract) \
                    .then_inc(S["pv_lo"], 1)
            mask_out_dve(dve, i, d, 1)

        def sa_dve(dve):
            dve.wait_ge(S["v_used"], NSTEP * KB)
            dve.wait_ge(S["w_used"], W_OUT)
            dve.wait_ge(S["a_hi"], NSTEP * KB)
            dve.wait_ge(S["v_saved"], seen(32 * KB))
            dve.memset(qbh[:, :, :].bitcast(F32), 0.0).then_inc(S["s_zero"], 1)
            dve.memset(qbl[:, :, :].bitcast(F32), 0.0).then_inc(S["s_zero"], 1)
            k_phase_dve(dve, 0, 0)
            for step in range(4):
                softmax_dve(dve, 0, 0, step)
            turned_dve(dve, 0, 0)
            with dve.Fori(0, DB // 2 - 1) as i:
                k_phase_dve(dve, i, 1)
                v_phase_dve(dve, i, 0)
                turned_dve(dve, i, 1)
            v_phase_dve(dve, 0, DB // 2 - 1)

        def ou_sp(sp):
            sp.wait_ge(S["pv_lo"], NP * (DB // 2 + 1))
            for n in range(3):
                with sp.Fori(0, KB - 1, 2) as m:
                    for u in range(2):
                        load_tile(sp, m, W_OUT + n * KB + u, out_w[n][:, :, bass.ds(m * P + u * P, P)])

        def ou_pe(pe):
            for n in range(3):
                with pe.Fori(0, KB - 3, 4) as m:
                    for u in range(4):
                        pe.wait_ge(S["w_split"], m + (W_OUT + n * KB + u + 1))
                        if n or u >= 2:
                            pe.wait_ge(S["mix_out"], m + seen(n * KB + u - 1))
                        else:
                            pe.wait_ge(S["mix_out"], seen(m))
                        linear(pe, W_OUT_B if n == 1 else W_OUT, u, u % 2, S["w_used"],
                               ("a", "b", "out")[n] if u == 0 else None)

        def aux_load(act, src, m, n, u):
            act.wait_ge(S["mix_out"], m + seen(n + u - 1))
            act.dma_start(tmp[:, u % 2, :], src[bass.ds(m + u, 1), :, :].rearrange("a p t -> (a p) t")) \
                .then_inc(S[f"aux_in{u % 2}"], 16)

        def conv_load(act, kb):
            if kb >= 2:
                act.wait_ge(S["op_lo"], LO_A + kb - 1)
            act.dma_start(tmp[:, 2 + kb % 2, :], conv_d[kb, :, :]).then_inc(S[f"conv_in{kb % 2}"], 16)

        def conv_high(act, kb):
            act.wait_ge(S[f"conv_in{kb % 2}"], 16 * (kb // 2 + 1))
            dst = gh2 if kb < HB else xh
            act.copy(dst[:, kb, :], tmp[:, 2 + kb % 2, :]).then_inc(S["op_hi"], 1)

        def conv_low(dve, kb):
            hi, lo = (gh2, gl2) if kb < HB else (xh, xl)
            dve.wait_ge(S["op_hi"], HI_A + kb + 1)
            dve.tensor_tensor(lo[:, kb, :], tmp[:, 2 + kb % 2, :], hi[:, kb, :].bitcast(F32),
                              ALU.subtract).then_inc(S["op_lo"], 1)

        def ou_act(act):
            act.wait_ge(S["siga_saved"], seen(16 * KB))
            act.wait_ge(S["sigb_saved"], seen(16 * KB))
            act.wait_ge(S["conv_saved"], 16 * KB)
            act.wait_ge(S["sa_turned"], DB // 2)
            act.dma_start(tmp[:, 0, :], sig_a_d[0, :, :]).then_inc(S["aux_in0"], 16)
            act.dma_start(tmp[:, 1, :], sig_a_d[1, :, :]).then_inc(S["aux_in1"], 16)
            conv_load(act, 0)
            conv_load(act, 1)
            act.wait_ge(S["so_kept"], seen(DB // 2))
            for kb in range(KB):
                act.copy(xh[:, kb, :], acc[:, kb, :]).then_inc(S["op_hi"], 1)
            for kb in range(HB):
                conv_high(act, kb)
                conv_load(act, kb + 2)
            with act.Fori(0, KB - 3, 2) as m:
                for u in range(2):
                    aux_load(act, sig_a_d, m, 0, u + 2)
            act.wait_ge(S["w_used"], W_OUT + KB)
            for kb in range(HB, KB):
                conv_high(act, kb)
                if kb + 2 < KB:
                    conv_load(act, kb + 2)
            for kb in range(KB):
                aux_load(act, sig_b_d, 0, KB, kb)
                if 2 <= kb < HB + 2:
                    act.wait_ge(S["mix_out"], seen(KB + kb - 1))
                    act.copy(xh[:, kb - 2, :], acc[:, kb - 2, :]).then_inc(S["op_hi"], 1)
            act.wait_ge(S["x1_saved"], 16 * KB)
            for u in range(2):
                aux_load(act, x1_d, 0, 2 * KB, u)
            act.wait_ge(S["w_used"], W_OUT + 2 * KB)
            for kb in range(HB, KB):
                act.wait_ge(S["mix_out"], seen(KB + kb + 1))
                act.copy(xh[:, kb, :], acc[:, kb, :]).then_inc(S["op_hi"], 1)
            with act.Fori(0, KB - 3, 2) as m:
                for u in range(2):
                    aux_load(act, x1_d, m, 2 * KB, u + 2)

        def mix(dve, m, n, u):
            out = acc[:, bass.ds(m + u, 1), :].rearrange("p a (c n) -> p (a c) n", c=3)
            aux = tri(tmp[:, u % 2, :])
            dve.wait_ge(S["w_used"], m + (W_OUT + n * KB + u + 1))
            dve.wait_ge(S[f"aux_in{u % 2}"], m * 8 + (n * KB // 2 + u // 2 + 1) * 16)
            if n == 0:
                dve.tensor_tensor(out, aux, pset(u % 2), ALU.mult).then_inc(S["mix_out"], 1)
            elif n == 1:
                dve.tensor_tensor(aux, aux, pset(u % 2), ALU.mult).then_inc(S["mix_tmp"], 1)
                dve.wait_ge(S["mix_tmp"], m + (u + 1))
                dve.wait_ge(S["mix_out"], m + seen(KB + u))
                dve.tensor_tensor(out, out, aux, ALU.add).then_inc(S["mix_out"], 1)
            else:
                dve.scalar_tensor_tensor(out=out, in0=aux, scalar=ALPHA, in1=pset(u % 2), op0=ALU.mult,
                                         op1=ALU.add).then_inc(S["mix_out"], 1)

        def ou_dve(dve):
            dve.wait_ge(S["so_kept"], seen(DB // 2))
            split_lo(dve, HI_A - KB, range(KB), "op_lo")
            for kb in range(HB):
                conv_low(dve, kb)
            with dve.Fori(0, KB - 1, 2) as m:
                for u in range(2):
                    mix(dve, m, 0, u)
            for kb in range(HB, KB):
                conv_low(dve, kb)
            for kb in range(KB):
                mix(dve, 0, 1, kb)
                if kb < HB:
                    split_lo(dve, HI_OUT - KB, (kb,), "op_lo")
            split_lo(dve, HI_OUT - KB, range(HB, KB), "op_lo")
            with dve.Fori(0, KB - 1, 2) as m:
                for u in range(2):
                    mix(dve, m, 2, u)

        NTOK = SEQ // P + 1

        def tok_rows(k):
            return P if k < NTOK - 1 else NS

        def tok_psum(k, n):
            return ps[:, 2 * (k % 3):2 * (k % 3) + 2, :].rearrange("p a (b c) -> p (a b) c", b=4)[:, :, 0:n]

        def start_at_one(eng, n):
            for name in FROM_ONE[n::5]:
                eng.sem_inc(S[name], 1)

        block = top.enter_context(nc.Block())

        @block.sync
        def _(sp):
            start_at_one(sp, 0)
            sp.dma_start(ident[:, :], A["c_ident"]).then_inc(S["ident_in"], 16)
            for k in range(NTOK):
                if k == 4:
                    sp.dma_start(tmp[0:DB * HIST // 2, 2:4, 0:D], state_rows.rearrange("(j p) c -> p j c", j=2)) \
                        .then_inc(S["hist_in"], 16)
                if k >= 8:
                    sp.wait_ge(S["tok_turned"], k - 7)
                src = A["x_prompt"][0, k * P:(k + 1) * P, :] if k < NTOK - 1 else \
                    A["x_sample"].rearrange("b q d -> (b q) d")
                sp.dma_start(tok[0:tok_rows(k), k % 8, :], src).then_inc(S[f"tok_in{k % 8}"], 16)
            sp.dma_start(O["new_conv_s"][0, :, 0:HIST - DQ, :], A["state_conv"][0, :, DQ:HIST, :]) \
                .then_inc(S["state_saved"], 16)
            ff_sp(sp, 0)
            cv_sp(sp)
            at_sp(sp)
            sa_sp(sp)
            ou_sp(sp)
            ff_sp(sp, 1)
            for k in range(NTOK):
                sp.wait_ge(S["y_kept"], k + 1)
                dst = O["y_p"][0, k * P:(k + 1) * P, :] if k < NTOK - 1 else O["y_s"].rearrange("b q d -> (b q) d")
                sp.dma_start(dst, tmp[0:tok_rows(k), k % 4, 0:D]).then_inc(S[f"y_saved{k % 4}"], 16)
            for k in range(4):
                sp.wait_ge(S[f"y_saved{k}"], 16 * ((NTOK - k + 3) // 4))
            sp.wait_ge(S["k_saved"], seen(32 * KB))
            sp.wait_ge(S["v_saved"], seen(32 * KB))
            sp.wait_ge(S["tail_saved"], 16 * (DB + 1))
            sp.wait_ge(S["state_saved"], 16)

        @block.gpsimd
        def _(pool):
            start_at_one(pool, 1)
            pool.memset(one[:, :], 1.0).then_inc(S["one_set"], 1)
            pool.wait_ge(S["one_set"], 1)
            split_phase(pool, W_FF1, W_CONV - W_FF1, 4)
            ln_sum_pool(pool, 0, "acc_done", KB * FG)
            pool.wait_ge(S["w_used"], W_CONV)
            cv_pool(pool)
            at_pool(pool)
            sa_pool(pool)
            pool.wait_ge(S["pv_lo"], NP * (DB // 2 + 1))
            split_phase(pool, W_OUT, W_FF2 - W_OUT, 4)
            ln_sum_pool(pool, 2, "mix_out", 2 * KB)
            split_phase(pool, W_FF2, W_END - W_FF2, 4, HI_OUT)
            ln_sum_pool(pool, 3, "acc_done", KB + 2 * KB * FG)

        @block.tensor
        def _(pe):
            start_at_one(pe, 2)
            pe.wait_ge(S["ident_in"], 16)
            for k in range(NTOK):
                n = tok_rows(k)
                pe.wait_ge(S[f"tok_in{k % 8}"], 16 * (k // 8 + 1))
                if k >= 3:
                    pe.wait_ge(S["op_lo"], k - 2)
                    pe.wait_ge(S["acc_done"], seen(k - 2))
                for e in range(KB):
                    mm = pe.transpose(ps[:, 2 * (k % 3) + e // 4, (e % 4) * P:(e % 4) * P + n],
                                      tok[0:n, k % 8, e * P:(e + 1) * P], ident[0:n, 0:n])
                mm.then_inc(S["tok_turned"], 1)
            pe.wait_ge(S["acc_init"], seen(1))
            hist_pe(pe)
            pe.wait_ge(S["const_in"], 16 * len(CONSTS))
            pe.wait_ge(S["mask_set"], 3)
            ff_pe(pe, 0)
            pe.wait_ge(S["acc_done"], seen(KB + KB * FG))
            ln_pe(pe, 0)
            cv_pe(pe)
            pe.wait_ge(S["tap_done"], seen(TAPS * KB))
            pe.wait_ge(S["siga_done"], seen(KB))
            pe.wait_ge(S["sigb_done"], seen(KB))
            ln_pe(pe, 1)
            at_pe(pe)
            sa_pe(pe)
            ou_pe(pe)
            pe.wait_ge(S["mix_out"], seen(3 * KB))
            ln_pe(pe, 2)
            ff_pe(pe, 1)
            pe.wait_ge(S["acc_done"], seen(2 * (KB + KB * FG)))
            ln_pe(pe, 3)
            for k in range(NTOK):
                n = tok_rows(k)
                pe.wait_ge(S["ln_aff"], 4 * KB)
                if k >= 3:
                    pe.wait_ge(S["y_kept"], k - 2)
                for e in range(KB):
                    mm = pe.transpose(ps[0:n, 2 * (k % 3) + e // 4, (e % 4) * P:(e % 4 + 1) * P],
                                      acc[:, e, k * P:k * P + n], ident[:, :])
                mm.then_inc(S["y_turned"], 1)

        @block.scalar
        def _(act):
            start_at_one(act, 3)
            for dst, name in CONSTS:
                act.dma_start(dst, A[name]).then_inc(S["const_in"], 16)
            for k in range(NTOK):
                n = tok_rows(k)
                act.wait_ge(S["tok_turned"], k + 1)
                act.copy(xh[:, :, k * P:k * P + n], tok_psum(k, n)).then_inc(S["op_hi"], 1)
                act.mul(acc[:, :, k * P:k * P + n], tok_psum(k, n), ALPHA) \
                    .then_inc(S["acc_done" if k < KB else "acc_init"], 1)
            act.wait_ge(S["const_in"], 16 * len(CONSTS))
            act.wait_ge(S["mask_set"], 3)
            ff_act(act, 0)
            act.wait_ge(S["eps_set"], 1)
            ln_act(act, 0, ACT.Identity, HI_FF1)
            for kb in range(KB):
                act.wait_ge(S["ln_aff"], KB)
                act.dma_start(x1_d[kb, :, :], acc[:, kb, :]).then_inc(S["x1_saved"], 16)
            cv_act(act)
            act.wait_ge(S["siga_saved"], seen(16 * KB))
            act.wait_ge(S["sigb_saved"], seen(16 * KB))
            ln_act(act, 1, ACT.Silu, None)
            for kb in range(KB):
                act.wait_ge(S["ln_aff"], KB + kb + 1)
                act.dma_start(conv_d[kb, :, :], acc[:, kb, :]).then_inc(S["conv_saved"], 16)
            at_act(act)
            sa_act(act)
            ou_act(act)
            ln_act(act, 2, ACT.Identity, HI_OUT)
            act.wait_ge(S["ln_aff"], 3 * KB)
            for kb in range(KB):
                act.wait_ge(S["op_lo_odd"] if kb % 2 else S["op_lo"], (HB if kb % 2 else LO_OUT) + kb // 2 + 1)
                act.mul(acc[:, kb, :], acc[:, kb, :], ALPHA).then_inc(S["acc_done"], 1)
            ff_act(act, 1)
            ln_act(act, 3, ACT.Identity, None)

        @block.vector
        def _(dve):
            start_at_one(dve, 4)
            dve.memset(epsc[:, :], EPS).then_inc(S["eps_set"], 1)
            for k in range(NTOK):
                n = tok_rows(k)
                dve.wait_ge(S["op_hi"], k + 1)
                dve.wait_ge(S["acc_done" if k < KB else "acc_init"], seen(k + 1 if k < KB else 1))
                dve.tensor_tensor(xl[:, :, k * P:k * P + n], tok_psum(k, n), xh[:, :, k * P:k * P + n].bitcast(F32),
                                  ALU.subtract).then_inc(S["op_lo"], 1)
            hist_dve(dve)
            dve.wait_ge(S["const_in"], 16 * len(CONSTS))
            dve.wait_ge(S["ident_in"], 16)
            dve.tensor_copy(identb[:, :], ident[:, :]).then_inc(S["mask_set"], 1)
            dve.tensor_copy(dmask[:, :], tmp[:, 0, 0:P]).then_inc(S["mask_set"], 1)
            dve.tensor_copy(negones[:, :], tmp[:, 1, 0:P]).then_inc(S["mask_set"], 1)
            dve.wait_ge(S["acc_init"], seen(1))
            ff_dve(dve, 0)
            dve.wait_ge(S["acc_done"], seen(KB + KB * FG))
            ln_dve(dve, 0, HI_FF1)
            cv_dve(dve)
            cv_dve_main(dve)
            dve.wait_ge(S["tap_done"], seen(TAPS * KB))
            ln_dve(dve, 1, None)
            at_dve(dve)
            sa_dve(dve)
            ou_dve(dve)
            dve.wait_ge(S["mix_out"], seen(3 * KB))
            ln_dve(dve, 2, HI_OUT)
            ff_dve(dve, 1)
            dve.wait_ge(S["acc_done"], seen(2 * (KB + KB * FG)))
            ln_dve(dve, 3, None)
            for k in range(NTOK):
                n = tok_rows(k)
                dve.wait_ge(S["y_turned"], k + 1)
                if k >= 4:
                    dve.wait_ge(S[f"y_saved{k % 4}"], 16 * (k // 4))
                dve.tensor_copy(tmp[0:n, k % 4, 0:D].rearrange("p (a c) -> p a c", a=2),
                                ps[0:n, 2 * (k % 3):2 * (k % 3) + 2, :]).then_inc(S["y_kept"], 1)


def shape_constants():
    i = np.arange(P)
    col = np.arange(D)
    head = (i // DQ) % H
    new = np.arange(NS)
    low = -(2.0 ** 60)
    smask = np.full((P, DB // 2, NS), low, np.float32)
    for pair in range(DB // 2):
        own = (new[None, :] // DQ == 2 * pair + i[:, None] // 64) & (new[None, :] % DQ < i[:, None] % DQ)
        smask[:, pair, :][own] = 0.0
    return {
        "c_ident": np.eye(P, dtype=np.float32),
        "c_negtri": -(i[:, None] >= i[None, :]).astype(np.float32),
        "c_negones": -np.ones((P, P), np.float32),
        "c_avg": np.full((P, P), 1.0 / D, np.float32),
        "c_dmask": np.where(i[:, None] < i[None, :], 0.0, low).astype(np.float32),
        "c_mbd": (col[None, :] // HD == head[:, None]).astype(np.float32),
        "c_sel": ((i[:, None] // 64) * DQ + i[:, None] % DQ == np.arange(2 * DQ)[None, :]).astype(np.float32),
        "c_smask": smask,
    }


def by_feature(a):
    return np.ascontiguousarray(np.reshape(a, (-1, P)).T)


OUTS = {
    "y_p": (1, SEQ, D), "y_s": (DB, DQ, D), "new_k_p": (1, 1, SEQ, H, HD), "new_v_p": (1, 1, SEQ, H, HD),
    "new_conv_p": (1, 1, HIST, D), "new_k_s": (1, DB, DQ, H, HD), "new_v_s": (1, DB, DQ, H, HD),
    "new_conv_s": (1, DB, HIST, D),
}


def kernel(**inputs):
    import concourse.bacc as bacc
    from concourse.bass_utils import run_bass_kernel_spmd

    x = {k: np.asarray(v) for k, v in inputs.items()}
    arrays = {k: np.ascontiguousarray(x[k]) for k in (
        "x_prompt", "x_sample", "cache_k", "cache_v", "state_conv", "w_ff1_up", "w_ff1_down", "w_in",
        "w_proj_a", "w_proj_b", "w_out", "w_ff2_up", "w_ff2_down")}
    arrays["page_table"] = np.ascontiguousarray(x["page_table"].reshape(1, -1))
    arrays["norms"] = np.stack([by_feature(x[n]) for n in (
        "ln1_g", "ln1_b", "ln_conv_g", "ln_conv_b", "ln2_g", "ln2_b", "ln3_g", "ln3_b")], axis=1)
    arrays["gate_bias"] = by_feature(x["b_gate"])
    arrays["conv_bias"] = by_feature(x["b_dw"])
    arrays["taps"] = np.ascontiguousarray(x["w_dw"].reshape(CW, KB, P).transpose(2, 1, 0))
    arrays["b_heads"] = np.ascontiguousarray(np.broadcast_to(x["b_sb"].reshape(1, H), (P, H)))
    arrays["b_rows"] = np.ascontiguousarray(np.tile(np.repeat(x["b_sb"].reshape(H), DQ), 2).reshape(P, 1))
    arrays.update(shape_constants())

    nc = bacc.Bacc("TRN2", target_bir_lowering=False, num_devices=1)
    A = {k: nc.dram_tensor("in_" + k, a.shape, mybir.dt.from_np(a.dtype), kind="ExternalInput").ap()
         for k, a in arrays.items()}
    O = {k: nc.dram_tensor("out_" + k, s, F32, kind="ExternalOutput").ap() for k, s in OUTS.items()}
    build(nc, A, O)
    r = run_bass_kernel_spmd(nc, [{"in_" + k: a for k, a in arrays.items()}], core_ids=[0])
    return tuple(r.results[0]["out_" + k] for k in OUTS)
```
